# Optimizing a Trainium2 kernel written in Bass

```python
import jax, jax.numpy as jnp
from jax import lax
import numpy as np

D_MODEL = 2048
BATCH = 1
SEQ = 128
DEPTH = 1
DEC_BATCH = 1
DEC_SEQ = 512
PAST_LEN = 128

GRID_W = 64
NA_HEADS = 8
NA_HEAD_DIM = 128
NA_WIN_ROWS = 8
NA_WIN_COLS = 16
MLA_HEADS = 8
MLA_NOPE_DIM = 128
MLA_ROPE_DIM = 64
MLA_V_DIM = 128
Q_LORA = 512
KV_LORA = 512
NA_WIDTH = NA_HEADS * NA_HEAD_DIM
MLA_WIDTH = MLA_HEADS * MLA_V_DIM
MIX_WIDTH = NA_WIDTH + MLA_WIDTH
IN_COLS = 3 * NA_WIDTH + Q_LORA + KV_LORA + MLA_ROPE_DIM
D_FF = -(-8 * D_MODEL // (3 * 256)) * 256
ROPE_THETA = 10000.0
LN_EPS = 1e-5
RMS_EPS = 1e-6
ALPHA = (2.0 * DEPTH) ** 0.25
BETA = (8.0 * DEPTH) ** -0.25
Q_BLOCK = 128
NA_SCALE = NA_HEAD_DIM ** -0.5
MLA_SCALE = (MLA_NOPE_DIM + MLA_ROPE_DIM) ** -0.5

kernel_name = "hybrid_natten_mla_dit_step"

def _layernorm(x, g, b):
    xf = x.astype(jnp.float32)
    mu = xf.mean(-1, keepdims=True)
    var = jnp.square(xf - mu).mean(-1, keepdims=True)
    return ((xf - mu) * lax.rsqrt(var + LN_EPS) * g.astype(jnp.float32) + b.astype(jnp.float32)).astype(x.dtype)

def _rmsnorm(x, g):
    xf = x.astype(jnp.float32)
    return (xf * lax.rsqrt(jnp.mean(xf * xf, -1, keepdims=True) + RMS_EPS) * g.astype(jnp.float32)).astype(x.dtype)

def _modulation(cond, w_mod, b_mod):
    m = jax.nn.silu(cond) @ w_mod + b_mod
    return jnp.split(m[..., None, :], 6, axis=-1)

def _rope_2d(x):
    n = x.shape[1]
    t = jnp.arange(n, dtype=jnp.int32)
    half = MLA_ROPE_DIM // 2
    inv_freq = ROPE_THETA ** (-jnp.arange(0, half, 2, dtype=jnp.float32) / half)

    def rot(xa, pos):
        ang = pos.astype(jnp.float32)[:, None] * inv_freq
        cos = jnp.concatenate([jnp.cos(ang)] * 2, -1)[None, :, None, :]
        sin = jnp.concatenate([jnp.sin(ang)] * 2, -1)[None, :, None, :]
        x1, x2 = jnp.split(xa, 2, -1)
        return xa * cos + jnp.concatenate([-x2, x1], -1) * sin

    xf = x.astype(jnp.float32)
    xr = rot(xf[..., :half], t // GRID_W)
    xc = rot(xf[..., half:], t % GRID_W)
    return jnp.concatenate([xr, xc], -1).astype(x.dtype)

def _project(h, w_in, q_a_g, kv_a_g, w_q_b):
    B, N, _ = h.shape
    z = h @ w_in
    s0 = 3 * NA_WIDTH
    na_qkv, q_lat, kv_lat, k_rope = jnp.split(z, [s0, s0 + Q_LORA, s0 + Q_LORA + KV_LORA], axis=-1)
    na_q, na_k, na_v = [t.reshape(B, N, NA_HEADS, NA_HEAD_DIM) for t in jnp.split(na_qkv, 3, axis=-1)]
    q = (_rmsnorm(q_lat, q_a_g) @ w_q_b).reshape(B, N, MLA_HEADS, MLA_NOPE_DIM + MLA_ROPE_DIM)
    q_nope, q_rope = q[..., :MLA_NOPE_DIM], q[..., MLA_NOPE_DIM:]
    c_kv = _rmsnorm(kv_lat, kv_a_g)
    return na_q, na_k, na_v, q_nope, q_rope, c_kv, k_rope

def _mla_expand(c_kv, w_kv_b):
    B, N, _ = c_kv.shape
    kv = (c_kv @ w_kv_b).reshape(B, N, MLA_HEADS, MLA_NOPE_DIM + MLA_V_DIM)
    return kv[..., :MLA_NOPE_DIM], kv[..., MLA_NOPE_DIM:]

def _attend(q, k, v, scale):
    B, Nq, H, dk = q.shape
    nb = Nq // Q_BLOCK
    qb = q.reshape(B, nb, Q_BLOCK, H, dk).transpose(1, 0, 2, 3, 4)

    def one(qblk):
        s = jnp.einsum('bqhd,bkhd->bhqk', qblk, k).astype(jnp.float32) * scale
        p = jax.nn.softmax(s, axis=-1).astype(v.dtype)
        return jnp.einsum('bhqk,bkhd->bqhd', p, v)

    o = lax.map(one, qb)
    return o.transpose(1, 0, 2, 3, 4).reshape(B, Nq, H, v.shape[-1])

def _neighbourhood_attention(q, k, v, k_ctx, v_ctx, rpb):
    B, N, H, d = q.shape
    rows = N // GRID_W
    wr = min(NA_WIN_ROWS, rows)
    r = jnp.arange(rows)
    rs = jnp.clip(r - wr // 2, 0, rows - wr)
    key_rows = rs[:, None] + jnp.arange(wr)[None, :]
    col = jnp.arange(GRID_W)
    cs = jnp.clip(col - NA_WIN_COLS // 2, 0, GRID_W - NA_WIN_COLS)
    in_win = (col[None, :] >= cs[:, None]) & (col[None, :] < cs[:, None] + NA_WIN_COLS)
    dr = key_rows - r[:, None] + NA_WIN_ROWS - 1
    dc = jnp.clip(col[None, :] - col[:, None] + NA_WIN_COLS - 1, 0, 2 * NA_WIN_COLS - 2)
    bias = rpb[:, dr[:, None, :, None], dc[None, :, None, :]].astype(jnp.float32)

    qg = q.reshape(B, rows, GRID_W, H, d)
    kg = k.reshape(B, rows, GRID_W, H, d)[:, key_rows]
    vg = v.reshape(B, rows, GRID_W, H, d)[:, key_rows]
    s_loc = jnp.einsum('brqhd,brwkhd->bhrqwk', qg, kg).astype(jnp.float32) * NA_SCALE + bias
    s_loc = jnp.where(in_win[:, None, :], s_loc, -jnp.inf)
    s_ctx = jnp.einsum('brqhd,blhd->bhrql', qg, k_ctx).astype(jnp.float32) * NA_SCALE
    nloc = wr * GRID_W
    s = jnp.concatenate([s_loc.reshape(B, H, rows, GRID_W, nloc), s_ctx], axis=-1)
    p = jax.nn.softmax(s, axis=-1).astype(v.dtype)
    p_loc = p[..., :nloc].reshape(B, H, rows, GRID_W, wr, GRID_W)
    p_ctx = p[..., nloc:]
    o = jnp.einsum('bhrqwk,brwkhd->brqhd', p_loc, vg) + jnp.einsum('bhrql,blhd->brqhd', p_ctx, v_ctx)
    return o.reshape(B, N, H, d)

def _merge_and_ffn(x, o_na, o_mla, mod, w_o, ln1_g, ln1_b, w_gu, w_down, ln2_g, ln2_b):
    sh1, sc1, g1, sh2, sc2, g2 = mod
    B, N = x.shape[:2]
    o = jnp.concatenate([o_na.reshape(B, N, NA_WIDTH), o_mla.reshape(B, N, MLA_WIDTH)], axis=-1) @ w_o
    x = _layernorm(ALPHA * x + g1 * o, ln1_g, ln1_b)
    h = x * (1 + sc2) + sh2
    gate, up = jnp.split(h @ w_gu, 2, axis=-1)
    f = (jax.nn.silu(gate) * up) @ w_down
    return _layernorm(ALPHA * x + g2 * f, ln2_g, ln2_b)

def _context_layer(x, mod, w_in, q_a_g, kv_a_g, w_q_b, w_kv_b, w_o, ln1_g, ln1_b, w_gu, w_down, ln2_g, ln2_b):
    sh1, sc1 = mod[0], mod[1]
    h = x * (1 + sc1) + sh1
    na_q, na_k, na_v, q_nope, q_rope, c_kv, k_rope = _project(h, w_in, q_a_g, kv_a_g, w_q_b)
    o_na = _attend(na_q, na_k, na_v, NA_SCALE)
    k_nope, v_m = _mla_expand(c_kv, w_kv_b)
    B, L = x.shape[:2]
    q_m = jnp.concatenate([q_nope, q_rope], axis=-1)
    k_m = jnp.concatenate([k_nope, jnp.broadcast_to(k_rope[:, :, None, :], (B, L, MLA_HEADS, MLA_ROPE_DIM))], axis=-1)
    o_mla = _attend(q_m, k_m, v_m, MLA_SCALE)
    y = _merge_and_ffn(x, o_na, o_mla, mod, w_o, ln1_g, ln1_b, w_gu, w_down, ln2_g, ln2_b)
    return y, na_k, na_v, c_kv, k_rope

def _latent_layer(x, mod, ck, cv, cckv, ckrope, w_in, q_a_g, kv_a_g, w_q_b, w_kv_b, rpb, w_o,
                  ln1_g, ln1_b, w_gu, w_down, ln2_g, ln2_b):
    sh1, sc1 = mod[0], mod[1]
    h = x * (1 + sc1) + sh1
    na_q, na_k, na_v, q_nope, q_rope, c_kv, k_rope = _project(h, w_in, q_a_g, kv_a_g, w_q_b)
    o_na = _neighbourhood_attention(na_q, na_k, na_v, ck, cv, rpb)
    B, N = x.shape[:2]
    L = cckv.shape[1]
    k_nope, v_lat = _mla_expand(c_kv, w_kv_b)
    k_nope_ctx, v_ctx = _mla_expand(cckv, w_kv_b)
    q_m = jnp.concatenate([q_nope, _rope_2d(q_rope)], axis=-1)
    k_rope_lat = jnp.broadcast_to(_rope_2d(k_rope[:, :, None, :]), (B, N, MLA_HEADS, MLA_ROPE_DIM))
    k_rope_ctx = jnp.broadcast_to(ckrope[:, :, None, :], (B, L, MLA_HEADS, MLA_ROPE_DIM))
    k_m = jnp.concatenate([jnp.concatenate([k_nope, k_rope_lat], -1),
                           jnp.concatenate([k_nope_ctx, k_rope_ctx], -1)], axis=1)
    v_m = jnp.concatenate([v_lat, v_ctx], axis=1)
    o_mla = _attend(q_m, k_m, v_m, MLA_SCALE)
    return _merge_and_ffn(x, o_na, o_mla, mod, w_o, ln1_g, ln1_b, w_gu, w_down, ln2_g, ln2_b)

def setup_inputs(seed: int = 0) -> dict:
    key = jax.random.key(seed)
    ks = jax.random.split(key, 32)
    nrm = lambda k, shape, s: jax.random.normal(k, shape, jnp.float32) * s
    return {
        "x_prompt": nrm(ks[0], (BATCH, SEQ, D_MODEL), 1.0),
        "x_sample": nrm(ks[1], (DEC_BATCH, DEC_SEQ, D_MODEL), 1.0),
        "cache_na_k": nrm(ks[2], (DEC_BATCH, DEPTH, PAST_LEN, NA_HEADS, NA_HEAD_DIM), 1.0),
        "cache_na_v": nrm(ks[3], (DEC_BATCH, DEPTH, PAST_LEN, NA_HEADS, NA_HEAD_DIM), 1.0),
        "cache_mla_ckv": nrm(ks[4], (DEC_BATCH, DEPTH, PAST_LEN, KV_LORA), 1.0),
        "cache_mla_krope": nrm(ks[5], (DEC_BATCH, DEPTH, PAST_LEN, MLA_ROPE_DIM), 1.0),
        "c": nrm(ks[6], (DEC_BATCH, D_MODEL), 1.0),
        "c_ctx": nrm(ks[7], (D_MODEL,), 1.0),
        "w_mod": nrm(ks[8], (DEPTH, D_MODEL, 6 * D_MODEL), 0.5 * D_MODEL ** -0.5),
        "b_mod": nrm(ks[9], (DEPTH, 6 * D_MODEL), 0.02),
        "w_in": nrm(ks[10], (DEPTH, D_MODEL, IN_COLS), D_MODEL ** -0.5),
        "q_a_norm": 1.0 + nrm(ks[11], (DEPTH, Q_LORA), 0.02),
        "kv_a_norm": 1.0 + nrm(ks[12], (DEPTH, KV_LORA), 0.02),
        "w_q_b": nrm(ks[13], (DEPTH, Q_LORA, MLA_HEADS * (MLA_NOPE_DIM + MLA_ROPE_DIM)), Q_LORA ** -0.5),
        "w_kv_b": nrm(ks[14], (DEPTH, KV_LORA, MLA_HEADS * (MLA_NOPE_DIM + MLA_V_DIM)), KV_LORA ** -0.5),
        "na_rpb": nrm(ks[15], (DEPTH, NA_HEADS, 2 * NA_WIN_ROWS - 1, 2 * NA_WIN_COLS - 1), 0.1),
        "w_o": nrm(ks[16], (DEPTH, MIX_WIDTH, D_MODEL), BETA * MIX_WIDTH ** -0.5),
        "ln1_g": 1.0 + nrm(ks[17], (DEPTH, D_MODEL), 0.02),
        "ln1_b": nrm(ks[18], (DEPTH, D_MODEL), 0.02),
        "w_gu": nrm(ks[19], (DEPTH, D_MODEL, 2 * D_FF), D_MODEL ** -0.5),
        "w_down": nrm(ks[20], (DEPTH, D_FF, D_MODEL), BETA * D_FF ** -0.5),
        "ln2_g": 1.0 + nrm(ks[21], (DEPTH, D_MODEL), 0.02),
        "ln2_b": nrm(ks[22], (DEPTH, D_MODEL), 0.02),
    }

def reference(x_prompt, x_sample, cache_na_k, cache_na_v, cache_mla_ckv, cache_mla_krope, c, c_ctx,
              w_mod, b_mod, w_in, q_a_norm, kv_a_norm, w_q_b, w_kv_b, na_rpb, w_o,
              ln1_g, ln1_b, w_gu, w_down, ln2_g, ln2_b):
    xp = x_prompt
    nk, nv, nckv, nkr = [], [], [], []
    for l in range(DEPTH):
        mod_ctx = _modulation(c_ctx, w_mod[l], b_mod[l])
        xp, k_l, v_l, ckv_l, kr_l = _context_layer(
            xp, mod_ctx, w_in[l], q_a_norm[l], kv_a_norm[l], w_q_b[l], w_kv_b[l], w_o[l],
            ln1_g[l], ln1_b[l], w_gu[l], w_down[l], ln2_g[l], ln2_b[l])
        nk.append(k_l)
        nv.append(v_l)
        nckv.append(ckv_l)
        nkr.append(kr_l)
    state_na_k = jnp.stack(nk, axis=1)
    state_na_v = jnp.stack(nv, axis=1)
    state_mla_ckv = jnp.stack(nckv, axis=1)
    state_mla_krope = jnp.stack(nkr, axis=1)

    xs = x_sample
    for l in range(DEPTH):
        mod_lat = _modulation(c, w_mod[l], b_mod[l])
        xs = _latent_layer(
            xs, mod_lat, cache_na_k[:, l], cache_na_v[:, l], cache_mla_ckv[:, l], cache_mla_krope[:, l],
            w_in[l], q_a_norm[l], kv_a_norm[l], w_q_b[l], w_kv_b[l], na_rpb[l], w_o[l],
            ln1_g[l], ln1_b[l], w_gu[l], w_down[l], ln2_g[l], ln2_b[l])

    return (xp, xs, state_na_k, state_na_v, state_mla_ckv, state_mla_krope)


_drawn_inputs = setup_inputs


def setup_inputs(seed=0):
    import zlib

    import numpy as np

    out = dict(_drawn_inputs(seed))
    spreads = {}
    factors = {'cache_na_k': 8.0,
     'cache_na_v': 7.28,
     'cache_mla_ckv': 8.0,
     'cache_mla_krope': 8.0,
     'q_a_norm': 8.0,
     'kv_a_norm': 2.909,
     'w_q_b': 4.693,
     'na_rpb': 64.0,
     'ln1_g': 7.555,
     'ln1_b': 7.64,
     'ln2_g': 7.684,
     'ln2_b': 7.808}
    for name, (base, spread) in spreads.items():
        noise = np.random.default_rng([zlib.crc32(name.encode()), seed]).standard_normal(out[name].shape)
        drawn = base * np.exp(spread * noise) if base else spread * noise
        out[name] = __import__('jax').numpy.asarray(drawn.astype(out[name].dtype))
    for name, factor in factors.items():
        out[name] = (out[name] * factor).astype(out[name].dtype)
    return out
```

```python
import concourse.bass as bass
from concourse import mybir
from contextlib import ExitStack

P = 128
D = 2048
KD = D // P
LAT = 512
CTX = 128
T = LAT + CTX
TT = T // P
LT = LAT // P
HT = T // 2
NH = 8
GRID = 64
WR, WC = 8, 16
RPB = (2 * WR - 1) * (2 * WC - 1)
LORA = 512
KL = LORA // P
ROPE = 64
KEYS = LAT + CTX + CTX
FF = 5632
GT = 4
NG = FF // (GT * P)
ALPHA = 2.0 ** 0.25
LN_EPS = 1e-5
RMS_EPS = 1e-6
NA_SCALE = 128 ** -0.5
MLA_SCALE = 192 ** -0.5
BIG = -1.0e30

MOD_CHUNKS = 24
B_MOD = 0
B_V = B_MOD + 8 * 8
B_NA = B_V + 2 * 8
NA_PER = 4 * 5
B_KVL = B_NA + NH * NA_PER
B_QL = B_KVL + 8
B_KR = B_QL + 8
B_QR = B_KR + 1
B_VM = B_QR + 2
B_HEAD = B_VM + 4
B_WO = B_HEAD + NH
B_FF = B_WO + 4 * 8
FF_PER = GT * 4 + 4 * 2
N_BLOCKS = B_FF + NG * FF_PER

TOK_BANKS = [0, 1, 2, 3, 7]
DOWN_BANKS = [4, 5, 6, 7, 0]
UP_BANKS = [1, 2, 3, 0]


class Chain:

    def __init__(self, engine, sem):
        self.engine, self.sem, self.n, self.i, self.per = engine, sem, 0, None, 0

    def link(self, ins):
        ins.then_inc(self.sem, 1)
        self.n += 1
        self.engine.wait_ge(self.sem, self.n if self.i is None else self.i * self.per + self.n)

    def enter(self, i, first, per):
        self.start, self.i, self.per, self.first = self.n, i, per, first
        self.n -= first * per

    def leave(self, trips):
        assert self.n + self.first * self.per == self.start + self.per, self.n + self.first * self.per - self.start
        self.n, self.i = self.start + trips * self.per, None


def at(i, per, c):
    return c if i is None else i * per + c


def build(nc, wstream, xT, xtok, cond, bmod, rpb, kcT, vc, ckvcT, krcT, lncol, lnrow, latg, rope, cap, ident, sel,
          y, s_k, s_v, s_ckv, s_kr):
    f32, f32r = mybir.dt.float32, mybir.dt.float32r
    ALU, ACT, AX = mybir.AluOpType, mybir.ActivationFunctionType, mybir.AxisListType

    modraw = nc.dram_tensor("modraw", (4, 6 * D), f32, kind="Internal").ap()
    PAD = GRID - WC
    rpbpad = nc.dram_tensor("rpbpad", (PAD + NH * RPB + PAD,), f32, kind="Internal").ap()
    tbl = nc.dram_tensor("tbl", (NH, P, 14 * GRID), f32, kind="Internal").ap()
    oscr = nc.dram_tensor("oscr", (2 * NH, P, T), f32, kind="Internal").ap()

    ctx = ExitStack()
    with ctx:
        def sb(name, shape, dt=f32, scope=ctx):
            return scope.enter_context(nc.sbuf_tensor(name, shape, dt))

        def sem(name):
            return ctx.enter_context(nc.semaphore(name))

        raw = sb("raw", [P, 4, 1024])
        whi = sb("whi", [P, 2, 1024], f32r)
        wlo = sb("wlo", [P, 2, 1024], f32r)
        acc = sb("acc", [P, TT * D])
        idt = sb("idt", [P, P])
        selt = sb("selt", [5, 2 + 2 * P])
        lncols = sb("lncols", [P, 2, KD])
        ropet = sb("ropet", [P, 2, LT, ROPE])
        mod1 = sb("mod1", [P, 2 * KD, 2])
        mod2 = sb("mod2", [P, 2 * KD, 2])
        small = sb("small", [P, 64])
        stat = sb("stat", [P, TT, 4, 6])
        mv = sb("mv", [P, TT, 2])
        rstd = sb("rstd", [P, TT])

        att = ExitStack()
        modrow = sb("modrow", [4, 2, 512], f32, att)
        first = ExitStack()
        rows1 = sb("rows1", [5, 2 * D], f32, first)
        first.close()
        qT = sb("qT", [P, T], f32, att)
        kT = sb("kT", [P, KEYS], f32, att)
        vh = sb("vh", [P, 6, P], f32, att)
        pb = sb("pb", [P, 3, T], f32, att)
        PT = sb("PT", [P, 5, LAT], f32, att)
        PTc = sb("PTc", [P, P], f32, att)
        ost = sb("ost", [P, T], f32, att)
        kst = sb("kst", [P, P], f32, att)
        mx = sb("mx", [P, 3, 4], f32, att)
        rs = sb("rs", [P, 3, 4], f32, att)

        s1 = ExitStack()
        hh = sb("hh", [P, KD, T], f32r, s1)
        hl = sb("hl", [P, KD, T], f32r, s1)
        condw = sb("condw", [P, KD, P], f32r, s1)
        condf = sb("condf", [P, KD, 2], f32, s1)
        conds = sb("conds", [P, 2, KD, 2], f32, s1)
        s1.close()

        s2 = ExitStack()
        ckvh = sb("ckvh", [P, KL, KEYS], f32r, s2)
        ckvl = sb("ckvl", [P, KL, KEYS], f32r, s2)
        qlh = sb("qlh", [P, KL, T], f32r, s2)
        qll = sb("qll", [P, KL, T], f32r, s2)
        qrT = sb("qrT", [ROPE, NH, T], f32, s2)
        krT = sb("krT", [ROPE, KEYS], f32, s2)
        ckvs = sb("ckvs", [P, KL, CTX], f32, s2)
        vm = sb("vm", [P, 6, NH * P], f32, s2)
        s2.close()
        att.close()

        s3 = ExitStack()
        oh = sb("oh", [P, KD, T], f32r, s3)
        ol = sb("ol", [P, KD, T], f32r, s3)
        gate = sb("gate", [P, 2, D], f32, s3)
        tmp = sb("tmp", [P, 2, T], f32, s3)
        s3b = ExitStack()
        ostage = sb("ostage", [P, 3, T], f32, s3b)
        rows2 = sb("rows2", [5, D], f32, s3b)
        rows3 = sb("rows3", [5, D], f32, s3b)
        s3b.close()
        s3c = ExitStack()
        fh = sb("fh", [P, GT, T], f32r, s3c)
        fl = sb("fl", [P, GT, T], f32r, s3c)
        ex = sb("ex", [P, T], f32, s3c)
        gb = sb("gb", [P, 2, 512], f32, s3c)
        s3c.close()
        s3.close()
        s4 = ExitStack()
        lnb = sb("lnb", [P, 2, D], f32, s4)
        s4.close()

        xstage = acc[:, :].rearrange("p (k t) -> p k t", k=KD)
        vall = acc[:, 0:6 * NH * P].rearrange("p (k d) -> p k d", k=6)
        A1 = 6 * NH * P
        kct = acc[:, A1:A1 + NH * CTX].rearrange("p (h t) -> p h t", h=NH)
        A2 = A1 + NH * CTX
        TB = acc[:, A2:A2 + 14 * GRID]
        A3 = A2 + 14 * GRID
        capx = acc[:, A3:A3 + 14 * GRID]
        A4 = A3 + 14 * GRID
        latgt = acc[:, A4:A4 + 2 * LORA].rearrange("p (g c) -> p g c", g=2)
        assert A4 + 2 * LORA <= TT * D
        kvl = acc[:, 0:TT * LORA].rearrange("p (t c) -> p t c", t=TT)
        ql = acc[:, TT * LORA:2 * TT * LORA].rearrange("p (t c) -> p t c", t=TT)
        A5 = 2 * TT * LORA
        kr = acc[:, A5:A5 + TT * ROPE].rearrange("p (t c) -> p t c", t=TT)
        krr = acc[:, A5 + TT * ROPE:A5 + 2 * TT * ROPE].rearrange("p (t c) -> p t c", t=TT)
        assert A5 + 2 * TT * ROPE <= A1
        sq = acc[:, A1:A1 + LORA]
        qr = acc[:, A2:A2 + 2 * LORA].rearrange("p (b c) -> p b c", b=2)
        xs = acc[:, :].rearrange("p (t c) -> p t c", t=TT)

        ps = [ctx.enter_context(nc.psum_tensor(f"ps{i}", [P, 512], f32)) for i in range(8)]

        loaded = [sem(f"loaded{i}") for i in range(4)]
        hi_ready = sem("hi_ready")
        lo_ready = sem("lo_ready")
        used = sem("used")
        act_own = sem("act_own")
        dve_own = sem("dve_own")
        consts_in = sem("consts_in")
        x_in = sem("x_in")
        pad_in = sem("pad_in")
        tbl_in = sem("tbl_in")
        cond_exp = sem("cond_exp")
        cond_ready = sem("cond_ready")
        modrow_ready = sem("modrow_ready")
        modrow_out = [sem("modrow_out0"), sem("modrow_out1")]
        rows1_in = sem("rows1_in")
        mod1_psum = sem("mod1_psum")
        mod1_ready = sem("mod1_ready")
        h_scaled = sem("h_scaled")
        h_hi = sem("h_hi")
        h_ready = sem("h_ready")
        na_consts_in = sem("na_consts_in")
        tb_in = sem("tb_in")
        tb_ready = sem("tb_ready")
        v_done = sem("v_done")
        v_evac = sem("v_evac")
        sv_out = sem("sv_out")
        vh_ready = sem("vh_ready")
        q_evac = sem("q_evac")
        k_evac = sem("k_evac")
        scores_ready = sem("scores_ready")
        ctx_scores = sem("ctx_scores")
        max_ready = sem("max_ready")
        exp_ready = sem("exp_ready")
        p_ready = sem("p_ready")
        pt_ready = sem("pt_ready")
        pt_free = sem("pt_free")
        kst_ready = sem("kst_ready")
        kst_out = sem("kst_out")
        pv_ready = sem("pv_ready")
        o_evac = sem("o_evac")
        o_out = sem("o_out")
        lat_done = sem("lat_done")
        lat_evac = sem("lat_evac")
        lat_rt = sem("lat_rt")
        kvl_ready = sem("kvl_ready")
        ql_ready = sem("ql_ready")
        kr_ready = sem("kr_ready")
        skv_out = sem("skv_out")
        mla_in = sem("mla_in")
        tr_done = sem("tr_done")
        tr_hi = sem("tr_hi")
        tr_lo = sem("tr_lo")
        krt_evac = sem("krt_evac")
        qr_done = sem("qr_done")
        qr_roped = sem("qr_roped")
        qrt_done = sem("qrt_done")
        qrt_evac = sem("qrt_evac")
        vm_done = sem("vm_done")
        vm_evac = sem("vm_evac")
        xs_in = sem("xs_in")
        o_in = [sem(f"o_in{i}") for i in range(3)]
        o_hi = sem("o_hi")
        o_lo = sem("o_lo")
        rows2_in = sem("rows2_in")
        rows3_in = sem("rows3_in")
        g_psum = sem("g_psum")
        g_evac = sem("g_evac")
        wo_done = sem("wo_done")
        wo_evac = sem("wo_evac")
        mod2_psum = sem("mod2_psum")
        mod2_ready = sem("mod2_ready")
        var_ready = sem("var_ready")
        sd_ready = sem("sd_ready")
        xn_ready = sem("xn_ready")
        xt_ready = sem("xt_ready")
        h2_scaled = sem("h2_scaled")
        h2_hi = sem("h2_hi")
        h2_ready = sem("h2_ready")
        ln_in = sem("ln_in")
        lng_ready = sem("lng_ready")
        res_ready = sem("res_ready")
        gate_done = sem("gate_done")
        fexp = sem("fexp")
        gate_used = sem("gate_used")
        f_ready = sem("f_ready")
        f_hi = sem("f_hi")
        f_lo = sem("f_lo")
        down_done = sem("down_done")
        down_evac = sem("down_evac")
        lnb_in = sem("lnb_in")
        y_ready = sem("y_ready")
        y_out = sem("y_out")

        def hi_of(n):
            return whi[:, n % 2, :]

        def lo_of(n):
            return wlo[:, n % 2, :]

        CONSTS = 5

        def tile_done(engine, done, before, t, last, blocks):
            if t < last:
                engine.wait_ge(done, before + t + 1)
            else:
                engine.wait_ge(used, blocks)

        block = ctx.enter_context(nc.Block())

        @block.sync
        def _(sp):
            for n in range(4):
                sp.dma_start(raw[:, n, :], wstream[n]).then_inc(loaded[n], 16)
            with sp.Fori(1, N_BLOCKS // 4) as i:
                for s in range(4):
                    sp.wait_ge(lo_ready, i * 4 + (s - 3))
                    sp.dma_start(raw[:, s, :], wstream[i * 4 + s]).then_inc(loaded[s], 16)
            for n in range(N_BLOCKS // 4 * 4, N_BLOCKS):
                sp.wait_ge(lo_ready, n - 3)
                sp.dma_start(raw[:, n % 4, :], wstream[n]).then_inc(loaded[n % 4], 16)

        @block.gpsimd
        def _(pool):
            def rows_in(dst, n_cols, col, done):
                pool.dma_start(dst[0:4, 0:n_cols], modraw[:, col:col + n_cols]).then_inc(done, 16)
                pool.dma_start(dst[4:5, 0:n_cols], bmod[:, col:col + n_cols]).then_inc(done, 16)

            def modrow_store(c, r):
                pool.wait_ge(modrow_ready, c + 1)
                pool.dma_start(modraw[:, bass.ds(c * 512, 512)], modrow[:, r, :]).then_inc(modrow_out[r], 16)

            with pool.Fori(0, 4) as i:
                for r in range(2):
                    modrow_store(i * 2 + r, r)
            for r in range(2):
                pool.wait_ge(modrow_out[r], 16 * 4)
            rows_in(rows1, 2 * D, 0, rows1_in)

            pool.wait_ge(h_ready, KD)
            pool.dma_start(vall[:, LT, :], vc).then_inc(na_consts_in, 16)
            pool.dma_start(kct, kcT).then_inc(na_consts_in, 16)
            pool.dma_start(capx, cap).then_inc(na_consts_in, 16)
            for g in range(2):
                pool.dma_start(latgt[:, g, :], latg[g:g + 1, :].to_broadcast([P, LORA])).then_inc(na_consts_in, 16)
            pool.wait_ge(na_consts_in, 80)
            pool.wait_ge(tbl_in, 16 * 2 * NH)

            def bias_table(a):
                pool.dma_start(TB, tbl[a]).then_inc(tb_in, 16)
                pool.wait_ge(tb_in, a * 16 + 16)
                nc.gpsimd.tensor_tensor(TB, TB, capx, ALU.add).then_inc(tb_ready, 1)

            def v_of_head(a, src):
                nc.gpsimd.tensor_copy(vh[:, :, :], src[:, :, bass.ds(a * P, P)]).then_inc(vh_ready, 1)

            bias_table(0)
            pool.wait_ge(v_evac, 2 * TT)
            v_of_head(0, vall)
            pool.wait_ge(v_evac, 2 * TT)
            pool.dma_start(s_v, vall[:, LT + 1, :]).then_inc(sv_out, 16)

            def na_out(a):
                pool.wait_ge(kst_ready, a + 1)
                pool.dma_start(s_k[:, bass.ds(a * P, P)], kst[:, :]).then_inc(kst_out, 16)

            def head_out(a):
                pool.wait_ge(o_evac, a + 1)
                pool.dma_start(oscr[a], ost[:, :]).then_inc(o_out, 16)

            modrow_store(8, 0)
            modrow_store(9, 1)
            with pool.Fori(1, NH) as i:
                modrow_store(i * 2 + 8, 0)
                pool.wait_ge(max_ready, i * 5 - 1)
                bias_table(i)
                na_out(i - 1)
                modrow_store(i * 2 + 9, 1)
                head_out(i - 1)
                pool.wait_ge(kst_out, i * 16)
                pool.wait_ge(o_out, i * 16)
                v_of_head(i, vall)
            na_out(NH - 1)
            head_out(NH - 1)

            pool.wait_ge(kvl_ready, TT)
            pool.dma_start(s_ckv, kvl[:, LT, :]).then_inc(skv_out, 16)
            pool.wait_ge(kr_ready, 1)
            pool.dma_start(s_kr, kr[:, LT, :]).then_inc(skv_out, 16)
            pool.wait_ge(used, B_QR)
            pool.dma_start(ckvs[:, :, :], ckvcT).then_inc(mla_in, 16)
            pool.dma_start(krT[:, LAT:LAT + CTX], krcT).then_inc(mla_in, 16)

            pool.wait_ge(vm_evac, 12)
            pool.wait_ge(kst_out, 16 * NH)
            for a in range(NH):
                if a:
                    head_out(NH + a - 1)
                pool.wait_ge(o_out, 16 * (NH + a))
                v_of_head(a, vm)
                if a == 0:
                    pool.wait_ge(qr_roped, TT)
                    pool.wait_ge(qrt_done, TT)
                    pool.wait_ge(skv_out, 32)
                    pool.dma_start(xs, xtok).then_inc(xs_in, 16)
            head_out(2 * NH - 1)
            pool.wait_ge(o_out, 16 * 2 * NH)
            for r in range(2):
                pool.wait_ge(modrow_out[r], 16 * MOD_CHUNKS // 2)
            for k in range(KD):
                if k >= 3:
                    pool.wait_ge(o_lo, k - 2)
                pool.dma_start(ostage[:, k % 3, :], oscr[k]).then_inc(o_in[k % 3], 16)
                if k == 3:
                    rows_in(rows2, D, 2 * D, rows2_in)
            rows_in(rows3, D, 3 * D, rows3_in)
            pool.wait_ge(g_psum, 4)
            rows_in(rows2, D, 4 * D, rows2_in)
            pool.wait_ge(mod2_psum, 1)
            rows_in(rows2, D, 5 * D, rows2_in)

            pool.wait_ge(h2_ready, KD)
            for c in range(4):
                if c:
                    pool.wait_ge(res_ready, c * TT)
                pool.dma_start(gb[:, :, :], lnrow[0:1, 0:2, c * 512:(c + 1) * 512].to_broadcast([P, 2, 512])
                               ).then_inc(ln_in, 16)
                pool.wait_ge(ln_in, 16 * (c + 1))
                nc.gpsimd.tensor_scalar(gb[:, :, :], gb[:, :, :], ALPHA, None, ALU.mult).then_inc(lng_ready, 1)
                pool.wait_ge(lng_ready, c * (TT + 1) + 1)
                for t in range(TT):
                    v = xs[:, t, c * 512:(c + 1) * 512]
                    nc.gpsimd.tensor_tensor(v, v, gb[:, 0, :], ALU.mult).then_inc(lng_ready, 1)
                    pool.wait_ge(lng_ready, c * (TT + 1) + 2 + t)
                    nc.gpsimd.tensor_tensor(v, v, gb[:, 1, :], ALU.add).then_inc(res_ready, 1)

            pool.wait_ge(used, N_BLOCKS - 8)
            pool.dma_start(lnb[:, :, :], lnrow[0:1, 2:4, :].to_broadcast([P, 2, D])).then_inc(lnb_in, 16)
            for t in range(TT):
                pool.wait_ge(y_ready, t + 1)
                pool.dma_start(y[t], xs[:, t, :]).then_inc(y_out, 16)
            pool.wait_ge(sv_out, 16)
            pool.wait_ge(kst_out, 16 * NH)
            pool.wait_ge(skv_out, 32)
            pool.wait_ge(y_out, 16 * TT)

        @block.scalar
        def _(act):
            own = Chain(act, act_own)

            for dst, src in ((idt[:, :], ident), (selt[:, :], sel), (condf[:, :, :], cond), (lncols[:, :, :], lncol),
                             (ropet[:, :, :, :], rope)):
                act.dma_start(dst, src).then_inc(consts_in, 16)
            act.dma_start(xstage, xT).then_inc(x_in, 16)
            for lo, n, src in ((0, PAD, 0), (PAD, NH * RPB, 0), (PAD + NH * RPB, PAD, 0)):
                act.dma_start(rpbpad[lo:lo + n], rpb[src:src + n]).then_inc(pad_in, 16)

            def split(i, per, n):
                if i is None and n >= N_BLOCKS:
                    return
                act.wait_ge(loaded[n % 4], at(i, per // 4 * 16, 16 * (n // 4 + 1)))
                if i is not None or n >= 2:
                    act.wait_ge(used, at(i, per, n - 1))
                nc.scalar.activation(whi[:, n % 2, :], raw[:, n % 4, :], ACT.Copy).then_inc(hi_ready, 1)

            act.wait_ge(consts_in, 16 * CONSTS)
            nc.scalar.activation(conds[:, 0], condf[:, :, :], ACT.Exp, scale=-1.0).then_inc(cond_exp, 1)
            split(None, 0, 0)
            split(None, 0, 1)

            act.wait_ge(pad_in, 48)
            for a in range(NH):
                for r in range(2):
                    src = bass.AP(tensor=rpbpad.tensor, offset=PAD + WC - 1 + a * RPB + (1 - r) * (2 * WC - 1),
                                  ap=[[2 * WC - 1, 14], [-1, GRID], [1, GRID]])
                    act.dma_start(tbl[a, r * GRID:(r + 1) * GRID, :].rearrange("p (j k) -> j p k", j=14),
                                  src).then_inc(tbl_in, 16)

            def mod_pair(i, first):
                for b in range(16):
                    if b % 8 == 7:
                        act.wait_ge(used, at(i, 16, b + 1))
                        r = b // 8
                        if not first:
                            act.wait_ge(modrow_out[r], at(i, 16, 0))
                        nc.scalar.activation(modrow[:, r, :], ps[7][0:4, :], ACT.Copy).then_inc(modrow_ready, 1)
                    split(i, 16, b + 2)

            mod_pair(None, True)
            with act.Fori(1, 4) as i:
                mod_pair(i, False)

            def h_part(k):
                act.wait_ge(h_scaled, k + 1)
                nc.scalar.activation(hh[:, k, :], xstage[:, k, :], ACT.Copy).then_inc(h_hi, 1)

            for b in range(16):
                if b < 7:
                    for k in (range(4) if b == 0 else range(2 * b + 2, 2 * b + 4)):
                        h_part(k)
                if b % 8 == 7:
                    c = b // 8
                    for t, bank in enumerate(TOK_BANKS):
                        tile_done(act, v_done, c * LT, t, LT, B_V + 8 * c + 8)
                        if c == 0 and t == 0:
                            act.wait_ge(h_ready, KD)
                        dst = t if t < LT else LT + 1
                        nc.scalar.activation(vall[:, dst, c * 512:(c + 1) * 512], ps[bank][:, :],
                                             ACT.Copy).then_inc(v_evac, 1)
                split(None, 0, B_V + b + 2)

            def stage(i, a, s, na):
                A = lambda c: at(i, 5, 5 * a + c)
                if s < 5:
                    act.wait_ge(scores_ready, A(s + 1))
                    if na and s < LT:
                        nc.scalar.activation(pb[:, s % 3, LAT:T], ps[5][:, 0:CTX], ACT.Copy,
                                             scale=NA_SCALE).then_inc(ctx_scores, 1)
                if 2 <= s < 7:
                    t = s - 2
                    act.wait_ge(pt_ready, A(t + 1))
                    if t == 0:
                        act.wait_ge(vh_ready, (a + 1) if i is None else i + a + 1)
                    if t < LT:
                        nc.scalar.activation(PT[:, 0:4, t * P:(t + 1) * P],
                                             ps[6][:, :].rearrange("p (k q) -> p k q", k=4), ACT.Copy)
                        if na and t == 3:
                            nc.scalar.activation(kst[:, :], ps[5][:, 2 * P:3 * P], ACT.Copy).then_inc(kst_ready, 1)
                        last = ps[5][:, P:2 * P] if na else ps[7][:, 0:P]
                        nc.scalar.activation(PT[:, 4, t * P:(t + 1) * P], last, ACT.Copy).then_inc(pt_free, 1)
                    else:
                        nc.scalar.activation(PTc[:, :], ps[6][:, 0:P], ACT.Copy).then_inc(pt_free, 1)
                if s < 5:
                    act.wait_ge(max_ready, A(s + 1))
                    nb = mx[:, s % 3, 3:4]
                    if na and s < LT:
                        nc.scalar.activation(pb[:, s % 3, :], pb[:, s % 3, :], ACT.Exp, bias=nb, scale=1.0,
                                             accum_out=rs[:, s % 3, 2:3]).then_inc(exp_ready, 1)
                    elif s < LT:
                        bk = 4 if s % 2 == 0 else 0
                        nc.scalar.activation(pb[:, s % 3, 0:LAT], ps[bk][:, :], ACT.Exp, bias=nb, scale=MLA_SCALE,
                                             accum_out=rs[:, s % 3, 0:1])
                        nc.scalar.activation(pb[:, s % 3, LAT:T], ps[bk + 1][:, 0:CTX], ACT.Exp, bias=nb,
                                             scale=MLA_SCALE, accum_out=rs[:, s % 3, 1:2]).then_inc(exp_ready, 1)
                    else:
                        nc.scalar.activation(pb[:, s % 3, 0:CTX], ps[4][:, 0:CTX], ACT.Exp, bias=nb,
                                             scale=NA_SCALE if na else MLA_SCALE,
                                             accum_out=rs[:, s % 3, 2:3]).then_inc(exp_ready, 1)
                if s == 7:
                    act.wait_ge(pv_ready, (a + 1) if i is None else i + a + 1)
                    nc.scalar.activation(ost[:, 0:LAT], ps[4][:, :], ACT.Copy)
                    nc.scalar.activation(ost[:, LAT:T], ps[5][:, 0:CTX], ACT.Copy).then_inc(o_evac, 1)

            def q_copy(blocks):
                act.wait_ge(used, blocks)
                nc.scalar.activation(qT[:, 0:HT], ps[0][:, 0:HT], ACT.Copy)
                nc.scalar.activation(qT[:, HT:T], ps[1][:, 0:HT], ACT.Copy).then_inc(q_evac, 1)

            def na_iter(i, stages):
                for b in range(NA_PER):
                    g, r = divmod(b, 5)
                    if b in (9, 19):
                        act.wait_ge(used, at(i, NA_PER, B_NA + b + 1))
                        row = 0 if b == 9 else 1
                        act.wait_ge(modrow_out[row], 64 if i is None else i * 16 + 64)
                        nc.scalar.activation(modrow[:, row, :], ps[7][0:4, :], ACT.Copy).then_inc(modrow_ready, 1)
                    if b == 15:
                        q_copy(at(i, NA_PER, B_NA + b + 1))
                    split(i, NA_PER, B_NA + b + 2)
                    if stages and r in (0, 4):
                        stage(i, -1, 2 * g + (r == 4), True)

            na_iter(None, False)
            with act.Fori(1, NH) as i:
                na_iter(i, True)

            def copy_chunk(dst, c, n=LORA):
                for t, bank in enumerate(TOK_BANKS):
                    tile_done(act, lat_done, c * LT, t, LT, B_KVL + min(8 * c + 8, 17))
                    if c == 0 and t == 0:
                        act.wait_ge(vh_ready, NH)
                        act.wait_ge(sv_out, 16)
                    nc.scalar.activation(dst[:, t, :], ps[bank][:, 0:n], ACT.Copy).then_inc(lat_evac, 1)

            def norm_chunk(dst, c):
                for t in range(TT):
                    if t == 0:
                        act.wait_ge(lat_evac, c * TT + TT)
                    own.link(nc.scalar.activation(sq, dst[:, t, :], ACT.Square, accum_out=small[:, t:t + 1]))
                if c:
                    act.wait_ge(kvl_ready, 1)
                nc.scalar.activation(small[:, 8:8 + TT], small[:, 0:TT], ACT.Sqrt, scale=1.0 / LORA,
                                     bias=RMS_EPS).then_inc(lat_rt, 1)

            for b in range(17):
                if b == 7:
                    copy_chunk(kvl, 0)
                if b == 15:
                    copy_chunk(ql, 1)
                if b == 16:
                    copy_chunk(kr, 2, ROPE)
                split(None, 0, B_KVL + b + 2)
                if b < 8:
                    stage(None, NH - 1, b, True)
                if b == 8:
                    norm_chunk(kvl, 0)
            norm_chunk(ql, 1)

            act.wait_ge(mla_in, 32)
            nc.scalar.activation(ckvh[:, :, LAT:LAT + CTX], ckvs[:, :, :], ACT.Copy).then_inc(tr_hi, 1)
            for j in range(2 * TT):
                t = j % TT
                act.wait_ge(tr_done, j + 1)
                src = ps[j % 4][:, :].rearrange("p (k q) -> p k q", k=KL)
                if j < TT:
                    o = t if t < LT else LT + 1
                    dst = ckvh[:, :, o * P:(o + 1) * P]
                else:
                    dst = qlh[:, :, t * P:(t + 1) * P]
                nc.scalar.activation(dst, src, ACT.Copy).then_inc(tr_hi, 1)
            act.wait_ge(tr_done, 2 * TT + 1)
            nc.scalar.activation(krT[:, 0:LAT], ps[4][0:ROPE, :], ACT.Copy)
            nc.scalar.activation(krT[:, LAT + CTX:KEYS], ps[5][0:ROPE, 0:CTX], ACT.Copy).then_inc(krt_evac, 1)
            split(None, 0, B_QR + 2)
            split(None, 0, B_QR + 3)
            for t in range(TT):
                act.wait_ge(qrt_done, t + 1)
                for half in range(2):
                    ins = nc.scalar.activation(qrT[:, 4 * half:4 * half + 4, t * P:(t + 1) * P],
                                               ps[5 + half][0:ROPE, :].rearrange("p (h q) -> p h q", h=4), ACT.Copy)
                ins.then_inc(qrt_evac, 1)
            for c in range(2):
                for t in range(6):
                    if t % 2 == 0:
                        tile_done(act, vm_done, c * 5, t, 5, B_VM + 2 * c + 2)
                        if c * 6 + t >= 1:
                            act.wait_ge(vm_evac, c * 6 + t)
                        nc.scalar.activation(vm[:, t, c * 512:(c + 1) * 512], ps[(TOK_BANKS + [4])[t]][:, :],
                                             ACT.Copy).then_inc(vm_evac, 1)
                split(None, 0, B_VM + 2 * c + 2)
                split(None, 0, B_VM + 2 * c + 3)

            for h in range(NH + 1):
                if h:
                    for s in range(5):
                        stage(None, NH + h - 1, s, False)
                if h < NH:
                    q_copy(B_HEAD + h + 1)
                    split(None, 0, B_HEAD + h + 2)
                if h:
                    for s in range(5, 8):
                        stage(None, NH + h - 1, s, False)

            def o_part(k):
                act.wait_ge(o_in[k % 3], 16 * (k // 3 + 1))
                nc.scalar.activation(oh[:, k, :], ostage[:, k % 3, :], ACT.Copy).then_inc(o_hi, 1)

            for b in range(32):
                if b < 7:
                    for k in (range(4) if b == 0 else range(2 * b + 2, 2 * b + 4)):
                        o_part(k)
                if b == 6:
                    act.wait_ge(g_psum, 1)
                    for c in range(2):
                        nc.scalar.activation(gate[:, c, 0:512], ps[4 + c][:, :], ACT.Copy).then_inc(g_evac, 1)
                if b in (8, 10, 12):
                    q = b // 2 - 3
                    act.wait_ge(g_psum, q + 1)
                    for c in range(2):
                        nc.scalar.activation(gate[:, c, q * 512:(q + 1) * 512], ps[4 + c][:, :],
                                             ACT.Copy).then_inc(g_evac, 1)
                split(None, 0, B_WO + b + 2)

            for t in range(TT):
                act.wait_ge(var_ready, t + 1)
                nc.scalar.activation(rstd[:, t:t + 1], mv[:, t, 1:2], ACT.Sqrt, bias=LN_EPS,
                                     scale=1.0).then_inc(sd_ready, 1)
            act.wait_ge(mod2_ready, 1)
            for k in range(KD):
                r = k % 2
                act.wait_ge(xt_ready, k + 1)
                if k >= 2:
                    act.wait_ge(h2_ready, k - 1)
                nc.scalar.activation(tmp[:, r, 0:LAT], ps[2 * r][:, :], ACT.Identity,
                                     scale=mod2[:, KD + k, 0:1], bias=mod2[:, k, 0:1])
                nc.scalar.activation(tmp[:, r, LAT:T], ps[2 * r + 1][:, 0:CTX], ACT.Identity,
                                     scale=mod2[:, KD + k, 1:2], bias=mod2[:, k, 1:2]).then_inc(h2_scaled, 1)

            def ff_group(i, g0):
                for b in range(FF_PER):
                    if b < 16:
                        j, q = divmod(b, 4)
                        if q == 3:
                            act.wait_ge(gate_done, at(i, GT, GT * g0 + j + 1))
                            nc.scalar.activation(ex[:, 0:HT], ps[UP_BANKS[0]][:, 0:HT], ACT.Exp, scale=-1.0)
                            nc.scalar.activation(ex[:, HT:T], ps[UP_BANKS[1]][:, 0:HT], ACT.Exp,
                                                 scale=-1.0).then_inc(fexp, 1)
                        split(i, FF_PER, B_FF + FF_PER * g0 + b + 2)
                        if q == 3:
                            act.wait_ge(f_ready, at(i, GT, GT * g0 + j + 1))
                            nc.scalar.activation(fh[:, j, :], tmp[:, 0, :], ACT.Copy).then_inc(f_hi, 1)
                    else:
                        split(i, FF_PER, B_FF + FF_PER * g0 + b + 2)

            ff_group(None, 0)
            with act.Fori(1, NG - 1) as i:
                ff_group(i, 0)
            ff_group(None, NG - 1)

            for t in range(TT):
                act.wait_ge(var_ready, TT + t + 1)
                nc.scalar.activation(rstd[:, t:t + 1], mv[:, t, 1:2], ACT.Sqrt, bias=LN_EPS,
                                     scale=1.0).then_inc(sd_ready, 1)

        @block.vector
        def _(dve):
            V = nc.vector
            own = Chain(dve, dve_own)

            def split(i, per, n):
                if i is None and n >= N_BLOCKS:
                    return
                dve.wait_ge(hi_ready, at(i, per, n + 1))
                V.tensor_tensor(wlo[:, n % 2, :], raw[:, n % 4, :], whi[:, n % 2, :].bitcast(f32),
                                ALU.subtract).then_inc(lo_ready, 1)

            own.link(V.memset(condw[:, :, :].bitcast(f32), 0.0))
            dve.wait_ge(consts_in, 16 * CONSTS)
            dve.wait_ge(cond_exp, 1)
            own.link(V.tensor_scalar(conds[:, 0], conds[:, 0], 1.0, None, ALU.add))
            own.link(V.reciprocal(conds[:, 0], conds[:, 0]))
            own.link(V.tensor_tensor(conds[:, 1], conds[:, 0], condf[:, :, :], ALU.mult))
            own.link(V.tensor_copy(condw[:, :, 0:2], conds[:, 1]))
            V.tensor_tensor(condw[:, :, 2:4], conds[:, 1], condw[:, :, 0:2].bitcast(f32),
                            ALU.subtract).then_inc(cond_ready, 1)
            split(None, 0, 0)
            split(None, 0, 1)
            for b in range(16):
                split(None, 0, b + 2)
            with dve.Fori(1, 4) as i:
                for b in range(16):
                    split(i, 16, b + 2)

            def mod_cols(dst, psum):
                V.tensor_copy(dst[:, 0:KD, :], psum[:, 0:2 * KD].rearrange("p (k c) -> p k c", c=2))
                own.link(V.tensor_scalar(dst[:, KD:2 * KD, :], psum[:, 2 * KD:4 * KD].rearrange("p (k c) -> p k c", c=2),
                                         1.0, None, ALU.add))

            dve.wait_ge(mod1_psum, 1)
            mod_cols(mod1, ps[6])
            dve.wait_ge(x_in, 16)

            def h_part(k):
                for lo, hi, c in ((0, LAT, 0), (LAT, T, 1)):
                    ins = V.tensor_scalar(xstage[:, k, lo:hi], xstage[:, k, lo:hi], mod1[:, KD + k, c:c + 1],
                                          mod1[:, k, c:c + 1], ALU.mult, ALU.add)
                ins.then_inc(h_scaled, 1)

            def h_rest(k):
                dve.wait_ge(h_hi, k + 1)
                V.tensor_tensor(hl[:, k, :], xstage[:, k, :], hh[:, k, :].bitcast(f32), ALU.subtract).then_inc(h_ready, 1)

            for b in range(16):
                if b < 7:
                    ks = list(range(4) if b == 0 else range(2 * b + 2, 2 * b + 4))
                    if b == 0:
                        h_part(0)
                    for k in ks:
                        if k + 1 < KD:
                            h_part(k + 1)
                        h_rest(k)
                split(None, 0, B_V + b + 2)

            def stage(i, a, s, na):
                A = lambda c: at(i, 5, 5 * a + c)
                if s < 5:
                    r = s % 3
                    dve.wait_ge(scores_ready, A(s + 1))
                    if na and s < LT:
                        if s == 0:
                            dve.wait_ge(tb_ready, (a + 1) if i is None else i + a + 1)
                        own.link(V.scalar_tensor_tensor(out=pb[:, r, 0:LAT], in0=ps[4][:, :], scalar=NA_SCALE,
                                                        in1=TB[:, (6 - 2 * s) * GRID:(14 - 2 * s) * GRID],
                                                        op0=ALU.mult, op1=ALU.add))
                        dve.wait_ge(ctx_scores, (4 * a + s + 1) if i is None else i * 4 + 4 * a + s + 1)
                        own.link(V.reduce_max(mx[:, r, 2:3], pb[:, r, :], AX.X))
                        scale = -1.0
                    elif s < LT:
                        bk = 4 if s % 2 == 0 else 0
                        V.reduce_max(mx[:, r, 0:1], ps[bk][:, :], AX.X)
                        own.link(V.reduce_max(mx[:, r, 1:2], ps[bk + 1][:, 0:CTX], AX.X))
                        own.link(V.tensor_tensor(mx[:, r, 2:3], mx[:, r, 0:1], mx[:, r, 1:2], ALU.max))
                        scale = -MLA_SCALE
                    else:
                        own.link(V.reduce_max(mx[:, r, 2:3], ps[4][:, 0:CTX], AX.X))
                        scale = -(NA_SCALE if na else MLA_SCALE)
                    V.tensor_scalar(mx[:, r, 3:4], mx[:, r, 2:3], scale, None, ALU.mult).then_inc(max_ready, 1)
                if 1 <= s < 6:
                    t = s - 1
                    r = t % 3
                    dve.wait_ge(exp_ready, A(t + 1))
                    if not na and t < LT:
                        own.link(V.tensor_tensor(rs[:, r, 2:3], rs[:, r, 0:1], rs[:, r, 1:2], ALU.add))
                    own.link(V.reciprocal(rs[:, r, 3:4], rs[:, r, 2:3]))
                    n = T if t < LT else CTX
                    V.tensor_scalar(pb[:, r, 0:n], pb[:, r, 0:n], rs[:, r, 3:4], None, ALU.mult).then_inc(p_ready, 1)

            def k_copy(blocks, n):
                dve.wait_ge(used, blocks)
                V.tensor_copy(kT[:, 0:n], ps[2][:, 0:n])
                V.tensor_copy(kT[:, n:2 * n], ps[3][:, 0:n]).then_inc(k_evac, 1)

            def na_iter(i, stages):
                for b in range(NA_PER):
                    g, r = divmod(b, 5)
                    if b == 15:
                        k_copy(at(i, NA_PER, B_NA + b + 1), HT)
                    split(i, NA_PER, B_NA + b + 2)
                    if stages and r in (0, 4):
                        stage(i, -1, 2 * g + (r == 4), True)

            na_iter(None, False)
            with dve.Fori(1, NH) as i:
                own.enter(i, 1, 14)
                na_iter(i, True)
                own.leave(NH - 1)

            def norm_chunk(dst, c, done):
                dve.wait_ge(lat_rt, c + 1)
                own.link(V.reciprocal(small[:, 16:16 + TT], small[:, 8:8 + TT]))
                for t in range(TT):
                    V.scalar_tensor_tensor(out=dst[:, t, :], in0=dst[:, t, :], scalar=small[:, 16 + t:17 + t],
                                           in1=latgt[:, 1 - c, :], op0=ALU.mult, op1=ALU.mult).then_inc(done, 1)

            def rotate(dst, src, tmp_, t, nh):
                cos = ropet[:, 0, t, :]
                sin = ropet[:, 1, t, :]
                v = lambda x: x.rearrange("p (h q u j) -> p h q u j", h=nh, q=2, u=2)
                sn = sin.rearrange("p (q u j) -> p q u j", q=2, u=2)
                for q in range(2):
                    for u in range(2):
                        ins = V.tensor_tensor(v(tmp_)[:, :, q, u, :], v(src)[:, :, q, 1 - u, :],
                                              sn[:, q, u, :].unsqueeze(1).to_broadcast([P, nh, 16]), ALU.mult)
                own.link(ins)
                own.link(V.tensor_tensor(dst.rearrange("p (h c) -> p h c", h=nh), src.rearrange("p (h c) -> p h c", h=nh),
                                         cos.unsqueeze(1).to_broadcast([P, nh, ROPE]), ALU.mult))
                return V.tensor_tensor(dst, dst, tmp_, ALU.add)

            for b in range(17):
                split(None, 0, B_KVL + b + 2)
                if b < 8:
                    stage(None, NH - 1, b, True)
                if b == 9:
                    norm_chunk(kvl, 0, kvl_ready)
            dve.wait_ge(lat_evac, 3 * TT)
            for t in range(LT):
                own.link(rotate(krr[:, t, :], kr[:, t, :], krr[:, LT, :], t, 1))
            V.tensor_copy(krr[:, LT, :], kr[:, LT, :]).then_inc(kr_ready, 1)
            norm_chunk(ql, 1, ql_ready)

            dve.wait_ge(tr_hi, 1)
            V.tensor_tensor(ckvl[:, :, LAT:LAT + CTX], ckvs[:, :, :], ckvh[:, :, LAT:LAT + CTX].bitcast(f32),
                            ALU.subtract).then_inc(tr_lo, 1)
            for j in range(2 * TT):
                t = j % TT
                dve.wait_ge(tr_hi, j + 2)
                src = ps[j % 4][:, :].rearrange("p (k q) -> p k q", k=KL)
                if j < TT:
                    o = t if t < LT else LT + 1
                    h_, l_ = ckvh[:, :, o * P:(o + 1) * P], ckvl[:, :, o * P:(o + 1) * P]
                else:
                    h_, l_ = qlh[:, :, t * P:(t + 1) * P], qll[:, :, t * P:(t + 1) * P]
                V.tensor_tensor(l_, src, h_.bitcast(f32), ALU.subtract).then_inc(tr_lo, 1)
            split(None, 0, B_QR + 2)
            split(None, 0, B_QR + 3)
            for t in range(TT):
                tile_done(dve, qr_done, 0, t, LT, B_QR + 2)
                if t >= 2:
                    dve.wait_ge(qrt_done, t - 1)
                if t:
                    dve.wait_ge(qr_roped, t)
                src = ps[TOK_BANKS[t]][:, :]
                if t < LT:
                    rotate(qr[:, t % 2, :], src, sq, t, NH).then_inc(qr_roped, 1)
                else:
                    V.tensor_copy(qr[:, t % 2, :], src).then_inc(qr_roped, 1)
            for c in range(2):
                for t in range(6):
                    if t % 2 == 1:
                        tile_done(dve, vm_done, c * 5, t, 5, B_VM + 2 * c + 2)
                        dve.wait_ge(vm_evac, c * 6 + t)
                        V.tensor_copy(vm[:, t, c * 512:(c + 1) * 512],
                                      ps[(TOK_BANKS + [4])[t]][:, :]).then_inc(vm_evac, 1)
                split(None, 0, B_VM + 2 * c + 2)
                split(None, 0, B_VM + 2 * c + 3)

            for h in range(NH + 1):
                if h:
                    for s in range(5):
                        stage(None, NH + h - 1, s, False)
                if h < NH:
                    k_copy(B_HEAD + h + 1, KEYS // 2)
                    split(None, 0, B_HEAD + h + 2)
                if h:
                    for s in range(5, 8):
                        stage(None, NH + h - 1, s, False)

            def o_part(k):
                dve.wait_ge(o_hi, k + 1)
                V.tensor_tensor(ol[:, k, :], ostage[:, k % 3, :], oh[:, k, :].bitcast(f32), ALU.subtract).then_inc(o_lo, 1)

            for b in range(32):
                if b < 7:
                    for k in (range(4) if b == 0 else range(2 * b + 2, 2 * b + 4)):
                        o_part(k)
                if b % 8 == 7:
                    c = b // 8
                    cols = slice(c * 512, (c + 1) * 512)
                    if c == 0:
                        dve.wait_ge(xs_in, 16)
                    if c == 0:
                        dve.wait_ge(g_evac, 2)
                    else:
                        dve.wait_ge(g_evac, 8)
                    for t, bank in enumerate(TOK_BANKS):
                        tile_done(dve, wo_done, c * LT, t, LT, B_WO + 8 * c + 8)
                        V.tensor_tensor(tmp[:, t % 2, 0:512], ps[bank][:, :], gate[:, t // LT, cols],
                                        ALU.mult).then_inc(wo_evac, 1)
                        dve.wait_ge(wo_evac, c * TT + t + 1)
                        own.link(V.scalar_tensor_tensor(out=xs[:, t, cols], in0=xs[:, t, cols], scalar=ALPHA,
                                                        in1=tmp[:, t % 2, 0:512], op0=ALU.mult, op1=ALU.add))
                        V.bn_stats(stat[:, t, c, :], xs[:, t, cols]).then_inc(dve_own, 1)
                        own.n += 1
                split(None, 0, B_WO + b + 2)

            def stats(t, n):
                dve.wait_ge(dve_own, own.n)
                V.bn_aggr(mv[:, t, :], stat[:, t, :, :].rearrange("p c s -> p (c s)")).then_inc(var_ready, 1)

            for t in range(TT):
                stats(t, 0)
            for t in range(TT):
                dve.wait_ge(sd_ready, t + 1)
                own.link(V.reciprocal(small[:, 24 + t:25 + t], rstd[:, t:t + 1]))
                V.tensor_scalar(xs[:, t, :], xs[:, t, :], mv[:, t, 0:1], small[:, 24 + t:25 + t], ALU.subtract,
                                ALU.mult).then_inc(xn_ready, 1)
                if t == 0:
                    dve.wait_ge(mod2_psum, 1)
                    mod_cols(mod2, ps[6])
                    bsc = small[:, 32:64].rearrange("p (k c) -> p k c", c=2)
                    lb = lncols[:, 1, :].unsqueeze(2).to_broadcast([P, KD, 2])
                    lg = lncols[:, 0, :].unsqueeze(2).to_broadcast([P, KD, 2])
                    own.link(V.tensor_tensor(bsc, mod2[:, KD:2 * KD, :], lb, ALU.mult))
                    own.link(V.tensor_tensor(mod2[:, 0:KD, :], mod2[:, 0:KD, :], bsc, ALU.add))
                    V.tensor_tensor(mod2[:, KD:2 * KD, :], mod2[:, KD:2 * KD, :], lg, ALU.mult).then_inc(mod2_ready, 1)
            for k in range(KD):
                r = k % 2
                dve.wait_ge(h2_scaled, k + 1)
                V.tensor_copy(oh[:, k, :], tmp[:, r, :]).then_inc(h2_hi, 1)
                dve.wait_ge(h2_hi, k + 1)
                V.tensor_tensor(ol[:, k, :], tmp[:, r, :], oh[:, k, :].bitcast(f32), ALU.subtract).then_inc(h2_ready, 1)
            for c in range(8):
                dve.wait_ge(g_psum, 5 + c // 2)
                V.tensor_copy(gate[:, c % 2, c // 2 * 512:(c // 2 + 1) * 512],
                              ps[4 + c % 2][:, :]).then_inc(g_evac, 1)

            def ff_group(i, g0, last=False):
                for b in range(FF_PER):
                    if b < 16:
                        j, q = divmod(b, 4)
                        if q == 3:
                            n = at(i, GT, GT * g0 + j + 1)
                            dve.wait_ge(fexp, n)
                            own.link(V.tensor_scalar(ex[:, :], ex[:, :], 1.0, None, ALU.add))
                            own.link(V.reciprocal(ex[:, :], ex[:, :]))
                            V.tensor_tensor(ex[:, 0:HT], ex[:, 0:HT], ps[UP_BANKS[0]][:, 0:HT], ALU.mult)
                            V.tensor_tensor(ex[:, HT:T], ex[:, HT:T], ps[UP_BANKS[1]][:, 0:HT],
                                            ALU.mult).then_inc(gate_used, 1)
                            dve.wait_ge(used, at(i, FF_PER, B_FF + FF_PER * g0 + b + 1))
                            dve.wait_ge(gate_used, n)
                            V.tensor_tensor(tmp[:, 0, 0:HT], ex[:, 0:HT], ps[UP_BANKS[2]][:, 0:HT], ALU.mult)
                            V.tensor_tensor(tmp[:, 0, HT:T], ex[:, HT:T], ps[UP_BANKS[3]][:, 0:HT],
                                            ALU.mult).then_inc(f_ready, 1)
                        split(i, FF_PER, B_FF + FF_PER * g0 + b + 2)
                        if q == 3:
                            dve.wait_ge(f_hi, n)
                            V.tensor_tensor(fl[:, j, :], tmp[:, 0, :], fh[:, j, :].bitcast(f32),
                                            ALU.subtract).then_inc(f_lo, 1)
                    else:
                        c, q = divmod(b - 16, 2)
                        if q == 1:
                            cols = slice(c * 512, (c + 1) * 512)
                            if i is None and g0 == 0 and c == 0:
                                dve.wait_ge(res_ready, 4 * TT)
                            for t, bank in enumerate(DOWN_BANKS):
                                n = at(i, 4 * TT, (4 * g0 + c) * TT + t + 1)
                                if t < LT:
                                    dve.wait_ge(down_done, at(i, 4 * LT, (4 * g0 + c) * LT + t + 1))
                                else:
                                    dve.wait_ge(used, at(i, FF_PER, B_FF + FF_PER * g0 + b + 1))
                                V.tensor_tensor(tmp[:, 1, 0:512], ps[bank][:, :], gate[:, t // LT, cols],
                                                ALU.mult).then_inc(down_evac, 1)
                                dve.wait_ge(down_evac, n)
                                own.link(V.tensor_tensor(xs[:, t, cols], xs[:, t, cols], tmp[:, 1, 0:512], ALU.add))
                                if last:
                                    V.bn_stats(stat[:, t, c, :], xs[:, t, cols]).then_inc(dve_own, 1)
                                    own.n += 1
                        split(i, FF_PER, B_FF + FF_PER * g0 + b + 2)

            ff_group(None, 0)
            with dve.Fori(1, NG - 1) as i:
                own.enter(i, 1, GT * 2 + 4 * TT)
                ff_group(i, 0)
                own.leave(NG - 2)
            ff_group(None, NG - 1, last=True)

            for t in range(TT):
                stats(t, 0)
            dve.wait_ge(lnb_in, 16)
            for t in range(TT):
                dve.wait_ge(sd_ready, TT + t + 1)
                own.link(V.reciprocal(small[:, 24 + t:25 + t], rstd[:, t:t + 1]))
                own.link(V.tensor_scalar(xs[:, t, :], xs[:, t, :], mv[:, t, 0:1], small[:, 24 + t:25 + t],
                                         ALU.subtract, ALU.mult))
                own.link(V.tensor_tensor(xs[:, t, :], xs[:, t, :], lnb[:, 0, :], ALU.mult))
                V.tensor_tensor(xs[:, t, :], xs[:, t, :], lnb[:, 1, :], ALU.add).then_inc(y_ready, 1)

        @block.tensor
        def _(pe):
            mm = nc.tensor.matmul

            def mm3(out, ah, al, bh, bl, first, last):
                mm(out, ah, bh, start=first, stop=False)
                mm(out, ah, bl, start=False, stop=False)
                return mm(out, al, bh, start=False, stop=last)

            def arrived(i, per, n):
                pe.wait_ge(lo_ready, at(i, per, n + 1))

            def tok_block(n, ah, al, k0, first, last, banks, before=None, after=None, cols=512, tile=None):
                for t, bank in enumerate(banks):
                    if before:
                        before(t)
                    o = (t if tile is None else tile[t]) * P
                    for kk in range(2):
                        w = slice(kk * cols, (kk + 1) * cols)
                        ins = mm3(ps[bank][:, 0:cols], ah[:, k0 + kk, o:o + P], al[:, k0 + kk, o:o + P],
                                  hi_of(n)[:, w], lo_of(n)[:, w], first and kk == 0, last and kk == 1)
                    if after and t < len(banks) - 1:
                        after(t, ins)
                return ins

            def feat_block(n, bh, bl, k0, first, last, before=None, after=None, widths=(HT, HT), banks=(0, 1, 2, 3), b2=None):
                for o in range(4):
                    if before:
                        before(o)
                    half, w = o % 2, widths[o // 2]
                    xh, xl = (bh, bl) if o < 2 or b2 is None else b2
                    for kk in range(4):
                        c = slice(kk * 256 + o // 2 * P, kk * 256 + o // 2 * P + P)
                        m = slice(half * w, (half + 1) * w)
                        ins = mm3(ps[banks[o]][:, 0:w], hi_of(n)[:, c], lo_of(n)[:, c], xh[:, k0 + kk, m],
                                  xl[:, k0 + kk, m], first and kk == 0, last and kk == 3)
                    if after and o < 3:
                        after(o, ins)
                return ins

            def mod_block(i, per, n, b, chunk_free):
                arrived(i, per, n)
                if b == 0 and chunk_free is not None:
                    pe.wait_ge(modrow_ready, chunk_free)
                for kk in range(2):
                    w = slice(kk * 512, (kk + 1) * 512)
                    mm(ps[7][:, :], condw[:, 2 * b + kk, :], hi_of(n)[:, w], start=(b == 0 and kk == 0), stop=False)
                    ins = mm(ps[7][:, :], condw[:, 2 * b + kk, :], lo_of(n)[:, w], start=False, stop=(b == 7 and kk == 1))
                ins.then_inc(used, 1)

            pe.wait_ge(cond_ready, 1)
            for b in range(16):
                mod_block(None, 0, b, b % 8, 1 if b == 8 else None)
            with pe.Fori(1, 4) as i:
                for b in range(16):
                    mod_block(i, 16, b, b % 8, i * 2 + b // 8)

            def mod_columns(shift, scale, done):
                for j in range(2 * KD):
                    rows = shift if j < KD else scale
                    ins = mm(ps[6][:, 2 * j:2 * j + 2], rows[:, j % KD * P:(j % KD + 1) * P], selt[:, 0:2],
                             start=True, stop=True)
                ins.then_inc(done, 1)

            pe.wait_ge(rows1_in, 32)
            mod_columns(rows1[:, 0:D], rows1[:, D:2 * D], mod1_psum)

            for c in range(2):
                for b in range(8):
                    n = B_V + 8 * c + b
                    arrived(None, 0, n)
                    if c == 0:
                        pe.wait_ge(h_ready, 2 * b + 2)
                        if b == 0:
                            pe.wait_ge(modrow_ready, 8)
                    tok_block(n, hh, hl, 2 * b, b == 0, b == 7, TOK_BANKS,
                              before=(lambda t: pe.wait_ge(v_evac, t + 1)) if c == 1 and b == 0 else None,
                              after=(lambda t, ins: ins.then_inc(v_done, 1)) if b == 7 else None
                              ).then_inc(used, 1)

            def stage(i, a, s, na, kcached=None, h=None):
                A = lambda c: at(i, 5, 5 * a + c)
                one = (lambda c: a + c if i is None else i + a + c)

                def scores():
                    if s < 5:
                        bk = 4 if na or s % 2 == 0 else 0
                        if s == 0:
                            pe.wait_ge(q_evac, one(1))
                            pe.wait_ge(k_evac, one(1))
                        if na and s:
                            pe.wait_ge(exp_ready, A(s))
                        elif s >= 2:
                            pe.wait_ge(exp_ready, A(s - 1))
                        if s == 0 and i is None:
                            pe.wait_ge(o_evac, a)
                        q = qT[:, s * P:(s + 1) * P]
                        if s < LT:
                            if na:
                                mm(ps[bk][:, :], q, kT[:, 0:LAT], start=True, stop=True)
                                mm(ps[bk + 1][:, 0:CTX], q, kcached, start=True, stop=True).then_inc(scores_ready, 1)
                            else:
                                qq = qrT[:, h, s * P:(s + 1) * P]
                                mm(ps[bk][:, :], q, kT[:, 0:LAT], start=True, stop=False)
                                mm(ps[bk][:, :], qq, krT[:, 0:LAT], start=False, stop=True)
                                mm(ps[bk + 1][:, 0:CTX], q, kT[:, LAT:T], start=True, stop=False)
                                mm(ps[bk + 1][:, 0:CTX], qq, krT[:, LAT:T], start=False, stop=True).then_inc(scores_ready, 1)
                        elif na:
                            mm(ps[4][:, 0:CTX], q, kT[:, LAT:T], start=True, stop=True).then_inc(scores_ready, 1)
                        else:
                            mm(ps[4][:, 0:CTX], q, kT[:, T:KEYS], start=True, stop=False)
                            mm(ps[4][:, 0:CTX], qrT[:, h, LAT:T], krT[:, T:KEYS], start=False,
                               stop=True).then_inc(scores_ready, 1)

                def transposes():
                    if 2 <= s < 7:
                        t = s - 2
                        pe.wait_ge(p_ready, A(t + 1))
                        if t:
                            pe.wait_ge(pt_free, A(t))
                        if t < LT:
                            for k in range(4):
                                nc.tensor.transpose(ps[6][:, k * P:(k + 1) * P], pb[:, t % 3, k * P:(k + 1) * P], idt[:, :])
                            if na and t == 3:
                                nc.tensor.transpose(ps[5][:, 2 * P:3 * P], kT[:, LAT:T], idt[:, :])
                            last = ps[5][:, P:2 * P] if na else ps[7][:, 0:P]
                            nc.tensor.transpose(last, pb[:, t % 3, LAT:T], idt[:, :]).then_inc(pt_ready, 1)
                        else:
                            nc.tensor.transpose(ps[6][:, 0:P], pb[:, t % 3, 0:P], idt[:, :]).then_inc(pt_ready, 1)

                for part in (transposes, scores) if na else (scores, transposes):
                    part()
                if s == 7:
                    pe.wait_ge(pt_free, A(5))
                    pe.wait_ge(vh_ready, one(1))
                    for k in range(5):
                        mm(ps[4][:, :], vh[:, k, :], PT[:, k, :], start=(k == 0), stop=(k == 4))
                    mm(ps[5][:, 0:CTX], vh[:, 5, :], PTc[:, :], start=True, stop=True).then_inc(pv_ready, 1)

            def na_iter(i, stages):
                for b in range(NA_PER):
                    g, r = divmod(b, 5)
                    n = B_NA + b
                    if r == 0:
                        arrived(i, NA_PER, n)
                        before = None
                        if b == 0:
                            if i is None:
                                before = lambda o: pe.wait_ge(v_evac, TT + 1 + o)
                            else:
                                before = lambda o: pe.wait_ge(q_evac if o < 2 else k_evac, i + 0)
                        feat_block(n, hh, hl, 4 * g, g == 0, g == 3, before=before).then_inc(used, 1)
                    else:
                        m = 4 * g + r - 1
                        if i is None and m == 0:
                            pe.wait_ge(v_evac, 2 * TT)
                        mod_block(i, NA_PER, n, m % 8, (8 + m // 8) if i is None else i * 2 + 8 + m // 8)
                    if stages and r in (0, 4):
                        s = 2 * g + (r == 4)
                        if s == 0:
                            na_first_wait(i)
                        stage(i, -1, s, True, kct[:, i - 1, :])

            def na_first_wait(i):
                pe.wait_ge(na_consts_in, 80)
                pe.wait_ge(vh_ready, i)

            na_iter(None, False)
            with pe.Fori(1, NH) as i:
                na_iter(i, True)

            for b in range(17):
                n = B_KVL + b
                arrived(None, 0, n)
                if b < 16:
                    c, q = divmod(b, 8)
                    before = None
                    if c == 0 and q == 0:
                        def before(t):
                            if t < 4:
                                pe.wait_ge(q_evac if t < 2 else k_evac, NH)
                            else:
                                pe.wait_ge(modrow_ready, MOD_CHUNKS)
                    elif q == 0:
                        before = lambda t: pe.wait_ge(lat_evac, t + 1)
                    ins = tok_block(n, hh, hl, 2 * q, q == 0, q == 7, TOK_BANKS, before=before,
                                    after=(lambda t, ins: ins.then_inc(lat_done, 1)) if q == 7 else None)
                    ins.then_inc(used, 1)
                else:
                    for t, bank in enumerate(TOK_BANKS):
                        pe.wait_ge(lat_evac, TT + t + 1)
                        for k in range(KD):
                            w = slice(k * ROPE, (k + 1) * ROPE)
                            ins = mm3(ps[bank][:, 0:ROPE], hh[:, k, t * P:(t + 1) * P], hl[:, k, t * P:(t + 1) * P],
                                      hi_of(n)[:, w], lo_of(n)[:, w], k == 0, k == KD - 1)
                        ins.then_inc(lat_done if t < LT else used, 1)
                if b < 8:
                    stage(None, NH - 1, b, True, kct[:, NH - 1, :])

            pe.wait_ge(lat_evac, 3 * TT)
            for j in range(2 * TT):
                t = j % TT
                src = kvl if j < TT else ql
                pe.wait_ge(kvl_ready if j < TT else ql_ready, t + 1)
                if j >= 4:
                    pe.wait_ge(tr_lo, j - 2)
                for k in range(KL):
                    ins = nc.tensor.transpose(ps[j % 4][:, k * P:(k + 1) * P], src[:, t, k * P:(k + 1) * P], idt[:, :])
                ins.then_inc(tr_done, 1)
            pe.wait_ge(kr_ready, 1)
            pe.wait_ge(o_evac, NH)
            for t in range(LT):
                nc.tensor.transpose(ps[4][0:ROPE, t * P:(t + 1) * P], krr[:, t, :], idt[:, :])
            nc.tensor.transpose(ps[5][0:ROPE, 0:P], krr[:, LT, :], idt[:, :]).then_inc(tr_done, 1)

            for q in range(2):
                n = B_QR + q
                arrived(None, 0, n)
                if q == 0:
                    pe.wait_ge(tr_lo, 2 * TT + 1)
                tok_block(n, qlh, qll, 2 * q, q == 0, q == 1, TOK_BANKS,
                          after=(lambda t, ins: ins.then_inc(qr_done, 1)) if q else None
                          ).then_inc(used, 1)
            for t in range(TT):
                pe.wait_ge(qr_roped, t + 1)
                pe.wait_ge(qrt_evac, t) if t else pe.wait_ge(krt_evac, 1)
                for h in range(NH):
                    ins = nc.tensor.transpose(ps[5 + h // 4][0:ROPE, h % 4 * P:(h % 4 + 1) * P],
                                              qr[:, t % 2, h * ROPE:(h + 1) * ROPE], idt[:, :])
                ins.then_inc(qrt_done, 1)

            for c in range(2):
                for q in range(2):
                    n = B_VM + 2 * c + q
                    arrived(None, 0, n)
                    before = None
                    if c and not q:
                        before = lambda t: pe.wait_ge(vm_evac, t + 1)
                    if q == 0 and c == 0:
                        pe.wait_ge(mla_in, 32)
                    tok_block(n, ckvh, ckvl, 2 * q, q == 0, q == 1, TOK_BANKS + [4], before=before,
                              after=(lambda t, ins: ins.then_inc(vm_done, 1)) if q else None
                              ).then_inc(used, 1)

            for h in range(NH + 1):
                if h:
                    for s in range(5):
                        stage(None, NH + h - 1, s, False, h=h - 1)
                if h < NH:
                    n = B_HEAD + h
                    arrived(None, 0, n)
                    if h == 0:
                        pe.wait_ge(vm_evac, 12)
                    else:
                        pe.wait_ge(exp_ready, 5 * (NH + h - 1) + 4)
                        pe.wait_ge(k_evac, NH + h)
                    feat_block(n, qlh, qll, 0, True, True, widths=(HT, KEYS // 2), b2=(ckvh, ckvl)).then_inc(used, 1)
                if h:
                    for s in range(5, 8):
                        stage(None, NH + h - 1, s, False)

            def gate_bcast(rows, q):
                for c in range(2):
                    ins = mm(ps[4 + c][:, :], selt[:, 2 + c * P:2 + (c + 1) * P], rows[:, q * 512:(q + 1) * 512],
                             start=True, stop=True)
                ins.then_inc(g_psum, 1)

            for b in range(32):
                n = B_WO + b
                arrived(None, 0, n)
                c, q = divmod(b, 8)
                if c == 0:
                    pe.wait_ge(o_lo, 2 * q + 2)
                ins = tok_block(n, oh, ol, 2 * q, q == 0, q == 7, TOK_BANKS,
                                before=(lambda t: pe.wait_ge(wo_evac, (c - 1) * TT + t + 1)) if c and not q else None,
                                after=(lambda t, ins: ins.then_inc(wo_done, 1)) if q == 7 else None)
                ins.then_inc(used, 1)
                if b == 5:
                    pe.wait_ge(rows2_in, 32)
                    pe.wait_ge(o_evac, 2 * NH)
                    gate_bcast(rows2, 0)
                if b in (7, 9, 11):
                    pe.wait_ge(g_evac, b - 5)
                    gate_bcast(rows2, (b - 5) // 2)
            pe.wait_ge(rows3_in, 32)
            pe.wait_ge(rows2_in, 64)
            mod_columns(rows3, rows2, mod2_psum)
            pe.wait_ge(xn_ready, TT)
            for k in range(KD):
                r = k % 2
                if k >= 2:
                    pe.wait_ge(h2_scaled, k - 1)
                for t in range(LT):
                    nc.tensor.transpose(ps[2 * r][:, t * P:(t + 1) * P], xs[:, t, k * P:(k + 1) * P], idt[:, :])
                nc.tensor.transpose(ps[2 * r + 1][:, 0:P], xs[:, LT, k * P:(k + 1) * P], idt[:, :]).then_inc(xt_ready, 1)

            pe.wait_ge(rows2_in, 96)
            for q in range(4):
                pe.wait_ge(g_evac, 8 + 2 * q)
                gate_bcast(rows2, q)

            def ff_group(i, g0):
                for b in range(FF_PER):
                    n = B_FF + FF_PER * g0 + b
                    arrived(i, FF_PER, n)
                    if b < 16:
                        j, q = divmod(b, 4)
                        before = None
                        if q == 0 and (i is not None or g0 or j):
                            def before(o, j=j):
                                pe.wait_ge(gate_used if o < 2 else f_ready, at(i, GT, GT * g0 + j))
                                if o == 3 and j == 0:
                                    pe.wait_ge(down_evac, at(i, 4 * TT, 4 * TT * g0))
                        if i is None and g0 == 0 and b == 0:
                            pe.wait_ge(h2_ready, KD)
                            pe.wait_ge(g_evac, 16)
                        ins = feat_block(n, oh, ol, 4 * q, q == 0, q == 3, before=before, banks=UP_BANKS,
                                         after=(lambda o, ins: ins.then_inc(gate_done, 1) if o == 1 else None) if q == 3 else None)
                        ins.then_inc(used, 1)
                    else:
                        c, q = divmod(b - 16, 2)

                        def before(t, c=c, q=q):
                            if q:
                                return
                            if c:
                                pe.wait_ge(down_evac, at(i, 4 * TT, (4 * g0 + c - 1) * TT + t + 1))
                            else:
                                if i is not None or g0:
                                    pe.wait_ge(down_evac, at(i, 4 * TT, (4 * g0 - 1) * TT + t + 1))
                                if t == 4:
                                    pe.wait_ge(f_ready, at(i, GT, GT * g0 + GT))
                        pe.wait_ge(f_lo, at(i, GT, GT * g0 + 2 * q + 2))
                        ins = tok_block(n, fh, fl, 2 * q, q == 0, q == 1, DOWN_BANKS, before=before,
                                        after=(lambda t, ins: ins.then_inc(down_done, 1)) if q else None)
                        ins.then_inc(used, 1)

            ff_group(None, 0)
            with pe.Fori(1, NG - 1) as i:
                ff_group(i, 0)
            ff_group(None, NG - 1)


_NAMES = ["wstream", "xT", "xtok", "cond", "bmod", "rpb", "kcT", "vc", "ckvcT", "krcT", "lncol", "lnrow", "latg",
          "rope", "cap", "ident", "sel"]
_OUTS = [("y", (TT, P, D)), ("s_k", (CTX, NH * P)), ("s_v", (CTX, NH * P)), ("s_ckv", (CTX, LORA)), ("s_kr", (CTX, ROPE))]


def _tok_blocks(np, w):
    K, N = w.shape
    return w.reshape(K // 256, 2, P, N // 512, 512).transpose(3, 0, 2, 1, 4).reshape(-1, P, 1024)


def _feat_blocks(np, wa, wb):
    K, H, _ = wa.shape
    w = np.stack([wa, wb], axis=2)
    return w.reshape(K // 512, 4, P, H, 256).transpose(3, 0, 2, 1, 4).reshape(-1, P, 1024)


def _layout(np, a):
    f = {k: np.asarray(v) for k, v in a.items()}
    w_in, w_mod, w_qb, w_kvb = f["w_in"][0], f["w_mod"][0], f["w_q_b"][0], f["w_kv_b"][0]
    na = NH * P
    mod = _tok_blocks(np, w_mod)
    v = _tok_blocks(np, w_in[:, 2 * na:3 * na])
    qk = _feat_blocks(np, w_in[:, 0:na].reshape(D, NH, P), w_in[:, na:2 * na].reshape(D, NH, P))
    lat = w_in[:, 3 * na:]
    qb = w_qb.reshape(LORA, NH, P + ROPE)
    kb = w_kvb.reshape(LORA, NH, 2 * P)
    parts = [mod[0:64], v]
    mods = mod[64:].reshape(NH, 4, 4, P, 1024)
    qks = qk.reshape(NH, 4, 1, P, 1024)
    parts.append(np.concatenate([qks, mods], axis=2).reshape(-1, P, 1024))
    parts.append(_tok_blocks(np, lat[:, LORA:2 * LORA]))
    parts.append(_tok_blocks(np, lat[:, 0:LORA]))
    parts.append(lat[:, 2 * LORA:].reshape(KD, P, ROPE).transpose(1, 0, 2).reshape(1, P, 1024))
    parts.append(_tok_blocks(np, qb[:, :, P:].reshape(LORA, NH * ROPE)))
    parts.append(_tok_blocks(np, kb[:, :, P:].reshape(LORA, NH * P)))
    parts.append(_feat_blocks(np, qb[:, :, 0:P], kb[:, :, 0:P]))
    parts.append(_tok_blocks(np, f["w_o"][0]))
    wgu = f["w_gu"][0].reshape(D, 2, FF // P, P)
    up = _feat_blocks(np, wgu[:, 0], wgu[:, 1]).reshape(NG, GT * 4, P, 1024)
    down = _tok_blocks(np, f["w_down"][0]).reshape(4, NG, 2, P, 1024).transpose(1, 0, 2, 3, 4).reshape(NG, 8, P, 1024)
    parts.append(np.concatenate([up, down], axis=1).reshape(-1, P, 1024))
    x = np.concatenate([f["x_sample"][0], f["x_prompt"][0]], axis=0)
    out = {
        "wstream": np.concatenate(parts, axis=0),
        "xT": x.reshape(T, KD, P).transpose(2, 1, 0),
        "xtok": x.reshape(TT, P, D).transpose(1, 0, 2),
        "cond": np.stack([f["c"][0], f["c_ctx"]], axis=-1).reshape(KD, P, 2).transpose(1, 0, 2),
        "bmod": f["b_mod"][0:1],
        "rpb": f["na_rpb"][0].reshape(NH * RPB),
        "kcT": f["cache_na_k"][0, 0].transpose(2, 1, 0),
        "vc": f["cache_na_v"][0, 0].reshape(CTX, NH * P),
        "ckvcT": f["cache_mla_ckv"][0, 0].reshape(CTX, KL, P).transpose(2, 1, 0),
        "krcT": f["cache_mla_krope"][0, 0].transpose(1, 0),
        "lncol": np.stack([f["ln1_g"][0].reshape(KD, P).transpose(1, 0), f["ln1_b"][0].reshape(KD, P).transpose(1, 0)], axis=1),
        "lnrow": np.stack([f["ln1_g"][0], f["ln1_b"][0], f["ln2_g"][0], f["ln2_b"][0]], axis=0)[None],
        "latg": np.stack([f["q_a_norm"][0], f["kv_a_norm"][0]], axis=0),
    }
    return out


def _constants(np):
    f32 = np.float32
    half = ROPE // 2
    pos = np.arange(LAT, dtype=np.int32)
    inv = (f32(10000.0) ** (-np.arange(0, half, 2, dtype=f32) / f32(half))).astype(f32)
    cs = []
    for p in (pos // GRID, pos % GRID):
        ang = p.astype(f32)[:, None] * inv
        cs.append((np.cos(ang), np.sin(ang)))
    cos = np.concatenate([cs[0][0], cs[0][0], cs[1][0], cs[1][0]], axis=1)
    sin = np.concatenate([-cs[0][1], cs[0][1], -cs[1][1], cs[1][1]], axis=1)
    rope = np.stack([cos, sin]).reshape(2, LT, P, ROPE).transpose(2, 0, 1, 3).astype(f32)
    col = np.arange(GRID)
    start = np.clip(col - WC // 2, 0, GRID - WC)
    win = (col[None, :] >= start[:, None]) & (col[None, :] < start[:, None] + WC)
    cap = np.where(win, f32(0.0), f32(BIG)).astype(f32)
    sel = np.zeros((5, 2 + 2 * P), f32)
    for r, (a, b) in enumerate([(1, 0), (0, 1), (1, 0), (0, 1), (1, 1)]):
        sel[r, 0], sel[r, 1] = a, b
        sel[r, 2:2 + P], sel[r, 2 + P:] = a, b
    return {"rope": rope, "cap": np.tile(cap, (2, 14)), "ident": np.eye(P, dtype=f32), "sel": sel}


def kernel(**inputs):
    import numpy as np
    import concourse.bacc as bacc
    from concourse.bass_utils import run_bass_kernel_spmd

    arrays = {**_layout(np, inputs), **_constants(np)}
    arrays = {k: np.ascontiguousarray(v) for k, v in arrays.items()}
    nc = bacc.Bacc("TRN2", target_bir_lowering=False, num_devices=1)
    ins = [nc.dram_tensor("in_" + n, arrays[n].shape, mybir.dt.float32, kind="ExternalInput").ap() for n in _NAMES]
    outs = [nc.dram_tensor("out_" + n, s, mybir.dt.float32, kind="ExternalOutput").ap() for n, s in _OUTS]
    build(nc, *ins, *outs)
    res = run_bass_kernel_spmd(nc, [{"in_" + n: arrays[n] for n in _NAMES}], core_ids=[0]).results[0]
    y = res["out_y"].reshape(T, D)
    return (y[LAT:].reshape(1, CTX, D), y[:LAT].reshape(1, LAT, D),
            res["out_s_k"].reshape(1, 1, CTX, NH, P), res["out_s_v"].reshape(1, 1, CTX, NH, P),
            res["out_s_ckv"].reshape(1, 1, CTX, LORA), res["out_s_kr"].reshape(1, 1, CTX, ROPE))
```

```python
import concourse.bass as bass
from concourse import mybir
from contextlib import ExitStack

P = 128
D = 2048
KD = D // P
LAT = 512
CTX = 128
T = LAT + CTX
TT = T // P
LT = LAT // P
HT = T // 2
NH = 8
GRID = 64
WR, WC = 8, 16
RPB = (2 * WR - 1) * (2 * WC - 1)
LORA = 512
KL = LORA // P
ROPE = 64
KEYS = LAT + CTX + CTX
FF = 5632
GT = 4
NG = FF // (GT * P)
ALPHA = 2.0 ** 0.25
LN_EPS = 1e-5
RMS_EPS = 1e-6
NA_SCALE = 128 ** -0.5
MLA_SCALE = 192 ** -0.5
BIG = -1.0e30

MOD_CHUNKS = 24
B_MOD = 0
B_V = B_MOD + 8 * 8
B_NA = B_V + 2 * 8
NA_PER = 4 * 5
B_KVL = B_NA + NH * NA_PER
B_QL = B_KVL + 8
B_KR = B_QL + 8
B_QR = B_KR + 1
B_VM = B_QR + 2
B_HEAD = B_VM + 4
B_WO = B_HEAD + NH
B_FF = B_WO + 4 * 8
FF_PER = GT * 4 + 4 * 2
N_BLOCKS = B_FF + NG * FF_PER

TOK_BANKS = [0, 1, 2, 3, 7]
UP_BANKS = [[0, 1, 2, 3], [5, 6, 7, 4]]
DOWN_BANKS = [0, 1, 2, 3, 4]


class Chain:

    def __init__(self, engine, sem):
        self.engine, self.sem, self.n, self.i, self.per = engine, sem, 0, None, 0

    def link(self, ins):
        ins.then_inc(self.sem, 1)
        self.n += 1
        self.engine.wait_ge(self.sem, self.n if self.i is None else self.i * self.per + self.n)

    def enter(self, i, first, per):
        self.start, self.i, self.per, self.first = self.n, i, per, first
        self.n -= first * per

    def leave(self, trips):
        assert self.n + self.first * self.per == self.start + self.per, self.n + self.first * self.per - self.start
        self.n, self.i = self.start + trips * self.per, None


def at(i, per, c):
    return c if i is None else i * per + c


def build(nc, wstream, xT, xtok, cond, bmod, rpb, kcT, vc, ckvcT, krcT, lncol, lnrow, latg, bcol, rope, cap, ident, sel,
          y, s_k, s_v, s_ckv, s_kr):
    f32, f32r = mybir.dt.float32, mybir.dt.float32r
    ALU, ACT, AX = mybir.AluOpType, mybir.ActivationFunctionType, mybir.AxisListType

    modraw = nc.dram_tensor("modraw", (4, 6 * D), f32, kind="Internal").ap()
    PAD = GRID - WC
    rpbpad = nc.dram_tensor("rpbpad", (PAD + NH * RPB + PAD,), f32, kind="Internal").ap()
    tbl = nc.dram_tensor("tbl", (NH, P, 14 * GRID), f32, kind="Internal").ap()
    oscr = nc.dram_tensor("oscr", (2 * NH, P, T), f32, kind="Internal").ap()

    ctx = ExitStack()
    with ctx:
        def sb(name, shape, dt=f32, scope=ctx):
            return scope.enter_context(nc.sbuf_tensor(name, shape, dt))

        def sem(name):
            return ctx.enter_context(nc.semaphore(name))

        raw = sb("raw", [P, 4, 1024])
        whi = sb("whi", [P, 2, 1024], f32r)
        wlo = sb("wlo", [P, 2, 1024], f32r)
        acc = sb("acc", [P, TT * D])
        idt = sb("idt", [P, P])
        selt = sb("selt", [5, 2 + 2 * P])
        bcols = sb("bcols", [P, 2 * KD])
        lncols = sb("lncols", [P, 2, KD])
        ropet = sb("ropet", [P, 2, LT, ROPE])
        mod1 = sb("mod1", [P, 2 * KD, 2])
        mod2 = sb("mod2", [P, 2 * KD, 2])
        small = sb("small", [P, 64])
        stat = sb("stat", [P, TT, 4, 6])
        mv = sb("mv", [P, TT, 2])
        rstd = sb("rstd", [P, TT])

        att = ExitStack()
        modrow = sb("modrow", [4, 2, 512], f32, att)
        qT = sb("qT", [P, T], f32, att)
        kT = sb("kT", [P, KEYS], f32, att)
        vh = sb("vh", [P, 6, P], f32, att)
        pb = sb("pb", [P, 3, T], f32, att)
        PT = sb("PT", [P, 5, LAT], f32, att)
        PTc = sb("PTc", [P, P], f32, att)
        ost = sb("ost", [P, T], f32, att)
        kst = sb("kst", [P, P], f32, att)
        mx = sb("mx", [P, 3, 4], f32, att)
        rs = sb("rs", [P, 3, 4], f32, att)

        s0 = ExitStack()
        mraw = sb("mraw", [P, 8, 1024], f32, s0)
        mhi = sb("mhi", [P, 4, 1024], f32r, s0)
        mlo = sb("mlo", [P, 4, 1024], f32r, s0)
        s0.close()
        s1 = ExitStack()
        hh = sb("hh", [P, KD, T], f32r, s1)
        hl = sb("hl", [P, KD, T], f32r, s1)
        condw = sb("condw", [P, KD, P], f32r, s1)
        condf = sb("condf", [P, KD, 2], f32, s1)
        conds = sb("conds", [P, 2, KD, 2], f32, s1)
        s1.close()

        s2 = ExitStack()
        ckvh = sb("ckvh", [P, KL, KEYS], f32r, s2)
        ckvl = sb("ckvl", [P, KL, KEYS], f32r, s2)
        qlh = sb("qlh", [P, KL, T], f32r, s2)
        qll = sb("qll", [P, KL, T], f32r, s2)
        qrT = sb("qrT", [ROPE, NH, T], f32, s2)
        krT = sb("krT", [ROPE, KEYS], f32, s2)
        ckvs = sb("ckvs", [P, KL, CTX], f32, s2)
        vm = sb("vm", [P, 6, NH * P], f32, s2)
        s2.close()
        att.close()

        s3 = ExitStack()
        oh = sb("oh", [P, KD, T], f32r, s3)
        ol = sb("ol", [P, KD, T], f32r, s3)
        gate = sb("gate", [P, 2, D], f32, s3)
        tmp = sb("tmp", [P, 2, T], f32, s3)
        s3b = ExitStack()
        ostage = sb("ostage", [P, 3, T], f32, s3b)
        rows2 = sb("rows2", [5, D], f32, s3b)
        rows3 = sb("rows3", [5, D], f32, s3b)
        s3b.close()
        s3c = ExitStack()
        fh = sb("fh", [P, GT, T], f32r, s3c)
        fl = sb("fl", [P, GT, T], f32r, s3c)
        ex = sb("ex", [P, T], f32, s3c)
        gb = sb("gb", [P, 2, 512], f32, s3c)
        s3c.close()
        s3.close()
        s4 = ExitStack()
        lnb = sb("lnb", [P, 2, D], f32, s4)
        s4.close()

        xstage = acc[:, :].rearrange("p (k t) -> p k t", k=KD)
        vall = acc[:, 0:6 * NH * P].rearrange("p (k d) -> p k d", k=6)
        A1 = 6 * NH * P
        kct = acc[:, A1:A1 + NH * CTX].rearrange("p (h t) -> p h t", h=NH)
        A2 = A1 + NH * CTX
        TB = acc[:, A2:A2 + 14 * GRID]
        A3 = A2 + 14 * GRID
        capx = acc[:, A3:A3 + 14 * GRID]
        A4 = A3 + 14 * GRID
        latgt = acc[:, A4:A4 + 2 * LORA].rearrange("p (g c) -> p g c", g=2)
        assert A4 + 2 * LORA <= TT * D
        kvl = acc[:, 0:TT * LORA].rearrange("p (t c) -> p t c", t=TT)
        ql = acc[:, TT * LORA:2 * TT * LORA].rearrange("p (t c) -> p t c", t=TT)
        A5 = 2 * TT * LORA
        kr = acc[:, A5:A5 + TT * ROPE].rearrange("p (t c) -> p t c", t=TT)
        krr = acc[:, A5 + TT * ROPE:A5 + 2 * TT * ROPE].rearrange("p (t c) -> p t c", t=TT)
        assert A5 + 2 * TT * ROPE <= A1
        sq = acc[:, A1:A1 + LORA]
        qr = acc[:, A2:A2 + TT * LORA].rearrange("p (t c) -> p t c", t=TT)
        assert A2 + TT * LORA <= TT * D
        krf = pb[0:ROPE, 0, :]
        xs = acc[:, :].rearrange("p (t c) -> p t c", t=TT)

        ps = [ctx.enter_context(nc.psum_tensor(f"ps{i}", [P, 512], f32)) for i in range(8)]

        mod_loaded = [sem(f"mod_loaded{i}") for i in range(8)]
        loaded = [sem(f"loaded{i}") for i in range(4)]
        hi_ready = sem("hi_ready")
        lo_ready = sem("lo_ready")
        used = sem("used")
        act_own = sem("act_own")
        dve_own = sem("dve_own")
        consts_in = sem("consts_in")
        x_in = sem("x_in")
        pad_in = sem("pad_in")
        tbl_in = sem("tbl_in")
        cond_exp = sem("cond_exp")
        cond_ready = sem("cond_ready")
        modrow_ready = sem("modrow_ready")
        modrow_out = [sem("modrow_out0"), sem("modrow_out1")]
        mod1_psum = sem("mod1_psum")
        mod1_ready = sem("mod1_ready")
        h_scaled = sem("h_scaled")
        h_hi = sem("h_hi")
        h_ready = sem("h_ready")
        na_consts_in = sem("na_consts_in")
        tb_in = sem("tb_in")
        tb_ready = sem("tb_ready")
        v_done = sem("v_done")
        v_evac = sem("v_evac")
        sv_out = sem("sv_out")
        vh_ready = sem("vh_ready")
        q_evac = sem("q_evac")
        k_evac = sem("k_evac")
        scores_ready = sem("scores_ready")
        ctx_scores = sem("ctx_scores")
        max_ready = sem("max_ready")
        exp_ready = sem("exp_ready")
        p_ready = sem("p_ready")
        pt_ready = sem("pt_ready")
        pt_free = sem("pt_free")
        kst_ready = sem("kst_ready")
        kst_out = sem("kst_out")
        pv_ready = sem("pv_ready")
        o_evac = sem("o_evac")
        o_out = sem("o_out")
        lat_done = sem("lat_done")
        lat_evac = sem("lat_evac")
        lat_rt = sem("lat_rt")
        kvl_ready = sem("kvl_ready")
        ql_ready = sem("ql_ready")
        krf_evac = sem("krf_evac")
        krf_turned = sem("krf_turned")
        kr_evac = sem("kr_evac")
        kr_ready = sem("kr_ready")
        skv_out = sem("skv_out")
        mla_in = sem("mla_in")
        tr_done = sem("tr_done")
        tr_hi = sem("tr_hi")
        tr_lo = sem("tr_lo")
        krt_evac = sem("krt_evac")
        qr_done = sem("qr_done")
        qr_evac = sem("qr_evac")
        qr_roped = sem("qr_roped")
        qrt_done = sem("qrt_done")
        qrt_evac = sem("qrt_evac")
        vm_done = sem("vm_done")
        vm_evac = sem("vm_evac")
        xs_in = sem("xs_in")
        o_in = [sem(f"o_in{i}") for i in range(3)]
        o_hi = sem("o_hi")
        o_lo = sem("o_lo")
        rows2_in = sem("rows2_in")
        rows3_in = sem("rows3_in")
        g_psum = sem("g_psum")
        g_evac = sem("g_evac")
        wo_done = sem("wo_done")
        wo_evac = sem("wo_evac")
        mod2_psum = sem("mod2_psum")
        mod2_ready = sem("mod2_ready")
        var_ready = sem("var_ready")
        sd_ready = sem("sd_ready")
        xn_ready = sem("xn_ready")
        xt_ready = sem("xt_ready")
        h2_scaled = sem("h2_scaled")
        h2_hi = sem("h2_hi")
        h2_ready = sem("h2_ready")
        ln_in = sem("ln_in")
        lng_ready = sem("lng_ready")
        res_ready = sem("res_ready")
        gate_done = sem("gate_done")
        fexp = sem("fexp")
        gate_used = sem("gate_used")
        f_ready = sem("f_ready")
        f_hi = sem("f_hi")
        f_lo = sem("f_lo")
        down_done = sem("down_done")
        down_evac = sem("down_evac")
        lnb_in = sem("lnb_in")
        y_ready = sem("y_ready")
        y_out = sem("y_out")

        def hi_of(n):
            return whi[:, n % 2, :]

        def lo_of(n):
            return wlo[:, n % 2, :]

        MOD_BANKS = [7, 5]
        CONSTS = 6

        def tile_done(engine, done, before, t, last, blocks):
            if t < last:
                engine.wait_ge(done, before + t + 1)
            else:
                engine.wait_ge(used, blocks)

        block = ctx.enter_context(nc.Block())

        @block.sync
        def _(sp):
            for n in range(8):
                sp.dma_start(mraw[:, n, :], wstream[n]).then_inc(mod_loaded[n], 16)
            with sp.Fori(1, B_V // 8) as i:
                for s in range(8):
                    sp.wait_ge(lo_ready, i * 8 + (s - 7))
                    sp.dma_start(mraw[:, s, :], wstream[i * 8 + s]).then_inc(mod_loaded[s], 16)
            for n in range(B_V, B_V + 4):
                sp.dma_start(raw[:, n % 4, :], wstream[n]).then_inc(loaded[n % 4], 16)
            with sp.Fori(B_V // 4 + 1, N_BLOCKS // 4) as i:
                for s in range(4):
                    sp.wait_ge(lo_ready, i * 4 + (s - 3))
                    sp.dma_start(raw[:, s, :], wstream[i * 4 + s]).then_inc(loaded[s], 16)
            for n in range(N_BLOCKS // 4 * 4, N_BLOCKS):
                sp.wait_ge(lo_ready, n - 3)
                sp.dma_start(raw[:, n % 4, :], wstream[n]).then_inc(loaded[n % 4], 16)

        @block.gpsimd
        def _(pool):
            def rows_in(dst, n_cols, col, done):
                pool.dma_start(dst[0:4, 0:n_cols], modraw[:, col:col + n_cols]).then_inc(done, 16)
                pool.dma_start(dst[4:5, 0:n_cols], bmod[:, col:col + n_cols]).then_inc(done, 16)

            def modrow_store(c, r):
                pool.wait_ge(modrow_ready, c + 1)
                pool.dma_start(modraw[:, bass.ds(c * 512, 512)], modrow[:, r, :]).then_inc(modrow_out[r], 16)

            for lo, n, src in ((0, PAD, 0), (PAD, NH * RPB, 0), (PAD + NH * RPB, PAD, 0)):
                pool.dma_start(rpbpad[lo:lo + n], rpb[src:src + n]).then_inc(pad_in, 16)
            pool.wait_ge(pad_in, 48)
            pool.wait_ge(mod1_psum, 8)
            for a in range(NH):
                for r in range(2):
                    src = bass.AP(tensor=rpbpad.tensor, offset=PAD + WC - 1 + a * RPB + (1 - r) * (2 * WC - 1),
                                  ap=[[2 * WC - 1, 14], [-1, GRID], [1, GRID]])
                    pool.dma_start(tbl[a, r * GRID:(r + 1) * GRID, :].rearrange("p (j k) -> j p k", j=14),
                                   src).then_inc(tbl_in, 16)

            pool.wait_ge(h_ready, KD)
            pool.dma_start(vall[:, LT, :], vc).then_inc(na_consts_in, 16)
            pool.dma_start(kct, kcT).then_inc(na_consts_in, 16)
            pool.dma_start(capx, cap).then_inc(na_consts_in, 16)
            for g in range(2):
                pool.dma_start(latgt[:, g, :], latg[g:g + 1, :].to_broadcast([P, LORA])).then_inc(na_consts_in, 16)
            pool.wait_ge(na_consts_in, 80)
            pool.wait_ge(tbl_in, 16 * 2 * NH)

            def bias_table(a):
                pool.dma_start(TB, tbl[a]).then_inc(tb_in, 16)
                pool.wait_ge(tb_in, a * 16 + 16)
                nc.gpsimd.tensor_tensor(TB, TB, capx, ALU.add).then_inc(tb_ready, 1)

            def v_of_head(a, src):
                nc.gpsimd.tensor_copy(vh[:, :, :], src[:, :, bass.ds(a * P, P)]).then_inc(vh_ready, 1)

            bias_table(0)
            pool.wait_ge(v_evac, 2 * TT)
            v_of_head(0, vall)
            pool.wait_ge(v_evac, 2 * TT)
            pool.dma_start(s_v, vall[:, LT + 1, :]).then_inc(sv_out, 16)

            def na_out(a):
                pool.wait_ge(kst_ready, a + 1)
                pool.dma_start(s_k[:, bass.ds(a * P, P)], kst[:, :]).then_inc(kst_out, 16)

            def head_out(a):
                pool.wait_ge(o_evac, a + 1)
                pool.dma_start(oscr[a], ost[:, :]).then_inc(o_out, 16)

            modrow_store(8, 0)
            modrow_store(9, 1)
            with pool.Fori(1, NH) as i:
                modrow_store(i * 2 + 8, 0)
                pool.wait_ge(max_ready, i * 5 - 1)
                bias_table(i)
                na_out(i - 1)
                modrow_store(i * 2 + 9, 1)
                head_out(i - 1)
                pool.wait_ge(kst_out, i * 16)
                pool.wait_ge(o_out, i * 16)
                v_of_head(i, vall)
            na_out(NH - 1)
            head_out(NH - 1)

            pool.wait_ge(kvl_ready, TT)
            pool.dma_start(s_ckv, kvl[:, LT, :]).then_inc(skv_out, 16)
            pool.wait_ge(kr_ready, 1)
            pool.dma_start(s_kr, kr[:, LT, :]).then_inc(skv_out, 16)
            pool.wait_ge(used, B_QR)
            pool.dma_start(ckvs[:, :, :], ckvcT).then_inc(mla_in, 16)
            pool.dma_start(krT[:, LAT:LAT + CTX], krcT).then_inc(mla_in, 16)

            pool.wait_ge(vm_evac, 12)
            pool.wait_ge(kst_out, 16 * NH)
            for a in range(NH):
                if a:
                    head_out(NH + a - 1)
                pool.wait_ge(o_out, 16 * (NH + a))
                v_of_head(a, vm)
                if a == 0:
                    pool.wait_ge(qr_roped, TT)
                    pool.wait_ge(qrt_done, TT)
                    pool.wait_ge(skv_out, 32)
                    pool.dma_start(xs, xtok).then_inc(xs_in, 16)
            head_out(2 * NH - 1)
            pool.wait_ge(o_out, 16 * 2 * NH)
            for r in range(2):
                pool.wait_ge(modrow_out[r], 16 * NH)
            for k in range(KD):
                if k >= 3:
                    pool.wait_ge(o_lo, k - 2)
                pool.dma_start(ostage[:, k % 3, :], oscr[k]).then_inc(o_in[k % 3], 16)
                if k == 3:
                    rows_in(rows2, D, 2 * D, rows2_in)
            rows_in(rows3, D, 3 * D, rows3_in)
            pool.wait_ge(g_psum, 4)
            rows_in(rows2, D, 4 * D, rows2_in)
            pool.wait_ge(mod2_psum, 1)
            rows_in(rows2, D, 5 * D, rows2_in)

            pool.wait_ge(h2_ready, KD)
            for c in range(4):
                if c:
                    pool.wait_ge(res_ready, c * TT)
                pool.dma_start(gb[:, :, :], lnrow[0:1, 0:2, c * 512:(c + 1) * 512].to_broadcast([P, 2, 512])
                               ).then_inc(ln_in, 16)
                pool.wait_ge(ln_in, 16 * (c + 1))
                nc.gpsimd.tensor_scalar(gb[:, :, :], gb[:, :, :], ALPHA, None, ALU.mult).then_inc(lng_ready, 1)
                pool.wait_ge(lng_ready, c * (TT + 1) + 1)
                for t in range(TT):
                    v = xs[:, t, c * 512:(c + 1) * 512]
                    nc.gpsimd.tensor_tensor(v, v, gb[:, 0, :], ALU.mult).then_inc(lng_ready, 1)
                    pool.wait_ge(lng_ready, c * (TT + 1) + 2 + t)
                    nc.gpsimd.tensor_tensor(v, v, gb[:, 1, :], ALU.add).then_inc(res_ready, 1)

            pool.wait_ge(used, N_BLOCKS - 8)
            pool.dma_start(lnb[:, :, :], lnrow[0:1, 2:4, :].to_broadcast([P, 2, D])).then_inc(lnb_in, 16)
            for t in range(TT):
                pool.wait_ge(y_ready, t + 1)
                pool.dma_start(y[t], xs[:, t, :]).then_inc(y_out, 16)
            pool.wait_ge(sv_out, 16)
            pool.wait_ge(kst_out, 16 * NH)
            pool.wait_ge(skv_out, 32)
            pool.wait_ge(y_out, 16 * TT)

        @block.scalar
        def _(act):
            own = Chain(act, act_own)

            for dst, src in ((idt[:, :], ident), (selt[:, :], sel), (condf[:, :, :], cond), (lncols[:, :, :], lncol),
                             (ropet[:, :, :, :], rope), (bcols[:, :], bcol)):
                act.dma_start(dst, src).then_inc(consts_in, 16)
            act.dma_start(xstage, xT).then_inc(x_in, 16)
            def split(i, per, n):
                if i is None and n >= N_BLOCKS:
                    return
                act.wait_ge(loaded[n % 4], at(i, per // 4 * 16, 16 * ((n - B_V) // 4 + 1)))
                if i is not None or n >= B_V + 2:
                    act.wait_ge(used, at(i, per, n - 1))
                nc.scalar.activation(whi[:, n % 2, :], raw[:, n % 4, :], ACT.Copy).then_inc(hi_ready, 1)

            act.wait_ge(consts_in, 16 * CONSTS)
            nc.scalar.activation(conds[:, 0], condf[:, :, :], ACT.Exp, scale=-1.0).then_inc(cond_exp, 1)

            def mod_split(i, n):
                act.wait_ge(mod_loaded[n % 8], at(i, 32, 16 * (n // 8 + 1)))
                if i is not None or n >= 4:
                    act.wait_ge(used, at(i, 16, n - 3))
                nc.scalar.activation(mhi[:, n % 4, :], mraw[:, n % 8, :], ACT.Copy).then_inc(hi_ready, 1)

            def mod_pair(i, p):
                for b in range(16):
                    c = 2 * p + b // 8
                    if b % 8 == 7:
                        act.wait_ge(used, at(i, 16, 8 * c + 8))
                        if i is not None or c >= 2:
                            act.wait_ge(mod1_psum, at(i, 2, c - 1))
                        nc.scalar.activation(modrow[:, b // 8, :], ps[MOD_BANKS[b // 8]][0:4, :],
                                             ACT.Copy).then_inc(modrow_ready, 1)
                    n = 16 * p + b + 4
                    if i is not None or n < B_V:
                        mod_split(i, n)
                    elif n < B_V + 2:
                        split(None, 0, n)

            for n in range(4):
                mod_split(None, n)
            mod_pair(None, 0)
            with act.Fori(1, 3) as i:
                mod_pair(i, 0)
            mod_pair(None, 3)

            def h_part(k):
                act.wait_ge(h_scaled, k + 1)
                nc.scalar.activation(hh[:, k, :], xstage[:, k, :], ACT.Copy).then_inc(h_hi, 1)

            for b in range(16):
                if b < 7:
                    for k in (range(4) if b == 0 else range(2 * b + 2, 2 * b + 4)):
                        h_part(k)
                if b % 8 == 7:
                    c = b // 8
                    for t, bank in enumerate(TOK_BANKS):
                        tile_done(act, v_done, c * LT, t, LT, B_V + 8 * c + 8)
                        if c == 0 and t == 0:
                            act.wait_ge(h_ready, KD)
                        dst = t if t < LT else LT + 1
                        nc.scalar.activation(vall[:, dst, c * 512:(c + 1) * 512], ps[bank][:, :],
                                             ACT.Copy).then_inc(v_evac, 1)
                split(None, 0, B_V + b + 2)

            def stage(i, a, s, na):
                A = lambda c: at(i, 5, 5 * a + c)
                if s < 5:
                    act.wait_ge(scores_ready, A(s + 1))
                    if na and s < LT:
                        nc.scalar.activation(pb[:, s % 3, LAT:T], ps[5][:, 0:CTX], ACT.Copy,
                                             scale=NA_SCALE).then_inc(ctx_scores, 1)
                if 2 <= s < 7:
                    t = s - 2
                    act.wait_ge(pt_ready, A(t + 1))
                    if t == 0:
                        act.wait_ge(vh_ready, (a + 1) if i is None else i + a + 1)
                    if t < LT:
                        nc.scalar.activation(PT[:, 0:4, t * P:(t + 1) * P],
                                             ps[6][:, :].rearrange("p (k q) -> p k q", k=4), ACT.Copy)
                        if na and t == 3:
                            nc.scalar.activation(kst[:, :], ps[5][:, 2 * P:3 * P], ACT.Copy).then_inc(kst_ready, 1)
                        last = ps[5][:, P:2 * P] if na else ps[7][:, 0:P]
                        nc.scalar.activation(PT[:, 4, t * P:(t + 1) * P], last, ACT.Copy).then_inc(pt_free, 1)
                    else:
                        nc.scalar.activation(PTc[:, :], ps[6][:, 0:P], ACT.Copy).then_inc(pt_free, 1)
                if s < 5:
                    act.wait_ge(max_ready, A(s + 1))
                    nb = mx[:, s % 3, 3:4]
                    if na and s < LT:
                        nc.scalar.activation(pb[:, s % 3, :], pb[:, s % 3, :], ACT.Exp, bias=nb, scale=1.0,
                                             accum_out=rs[:, s % 3, 2:3]).then_inc(exp_ready, 1)
                    elif s < LT:
                        bk = 4 if s % 2 == 0 else 0
                        nc.scalar.activation(pb[:, s % 3, 0:LAT], ps[bk][:, :], ACT.Exp, bias=nb, scale=MLA_SCALE,
                                             accum_out=rs[:, s % 3, 0:1])
                        nc.scalar.activation(pb[:, s % 3, LAT:T], ps[bk + 1][:, 0:CTX], ACT.Exp, bias=nb,
                                             scale=MLA_SCALE, accum_out=rs[:, s % 3, 1:2]).then_inc(exp_ready, 1)
                    else:
                        nc.scalar.activation(pb[:, s % 3, 0:CTX], ps[4][:, 0:CTX], ACT.Exp, bias=nb,
                                             scale=NA_SCALE if na else MLA_SCALE,
                                             accum_out=rs[:, s % 3, 2:3]).then_inc(exp_ready, 1)
                if s == 7:
                    act.wait_ge(pv_ready, (a + 1) if i is None else i + a + 1)
                    nc.scalar.activation(ost[:, 0:LAT], ps[4][:, :], ACT.Copy)
                    nc.scalar.activation(ost[:, LAT:T], ps[5][:, 0:CTX], ACT.Copy).then_inc(o_evac, 1)

            def q_copy(blocks):
                act.wait_ge(used, blocks)
                nc.scalar.activation(qT[:, 0:HT], ps[0][:, 0:HT], ACT.Copy)
                nc.scalar.activation(qT[:, HT:T], ps[1][:, 0:HT], ACT.Copy).then_inc(q_evac, 1)

            def na_iter(i, stages):
                for b in range(NA_PER):
                    g, r = divmod(b, 5)
                    if b in (9, 19):
                        act.wait_ge(used, at(i, NA_PER, B_NA + b + 1))
                        row = 0 if b == 9 else 1
                        if i is None:
                            act.wait_ge(mod1_psum, 8)
                        else:
                            act.wait_ge(modrow_out[row], i * 16)
                        nc.scalar.activation(modrow[:, row, :], ps[7][0:4, :], ACT.Copy).then_inc(modrow_ready, 1)
                    if b == 15:
                        q_copy(at(i, NA_PER, B_NA + b + 1))
                    split(i, NA_PER, B_NA + b + 2)
                    if stages and r in (1, 3):
                        stage(i, -1, 2 * g + (r == 3), True)

            na_iter(None, False)
            with act.Fori(1, NH) as i:
                na_iter(i, True)

            def copy_chunk(dst, c):
                for t, bank in enumerate(TOK_BANKS):
                    tile_done(act, lat_done, c * LT, t, LT, B_KVL + 8 * c + 8)
                    if c == 0 and t == 0:
                        act.wait_ge(vh_ready, NH)
                        act.wait_ge(sv_out, 16)
                    nc.scalar.activation(dst[:, t, :], ps[bank][:, :], ACT.Copy).then_inc(lat_evac, 1)

            def norm_chunk(dst, c):
                for t in range(TT):
                    if t == 0:
                        act.wait_ge(lat_evac, c * TT + TT)
                    own.link(nc.scalar.activation(sq, dst[:, t, :], ACT.Square, accum_out=small[:, t:t + 1]))
                if c:
                    act.wait_ge(kvl_ready, 1)
                nc.scalar.activation(small[:, 8:8 + TT], small[:, 0:TT], ACT.Sqrt, scale=1.0 / LORA,
                                     bias=RMS_EPS).then_inc(lat_rt, 1)

            for b in range(17):
                if b == 7:
                    copy_chunk(kvl, 0)
                if b == 15:
                    copy_chunk(ql, 1)
                if b == 16:
                    norm_chunk(ql, 1)
                    act.wait_ge(used, B_KR + 1)
                    for half in range(2):
                        ins = nc.scalar.activation(krf[:, half * HT:(half + 1) * HT], ps[half][0:ROPE, 0:HT], ACT.Copy)
                    ins.then_inc(krf_evac, 1)
                    act.wait_ge(krf_turned, 1)
                    nc.scalar.activation(kr, ps[4][:, 0:TT * ROPE].rearrange("p (t c) -> p t c", t=TT),
                                         ACT.Copy).then_inc(kr_evac, 1)
                split(None, 0, B_KVL + b + 2)
                if b < 8:
                    stage(None, NH - 1, b, True)
                if b == 8:
                    norm_chunk(kvl, 0)

            act.wait_ge(mla_in, 32)
            nc.scalar.activation(ckvh[:, :, LAT:LAT + CTX], ckvs[:, :, :], ACT.Copy).then_inc(tr_hi, 1)
            for j in range(2 * TT):
                t = j % TT
                act.wait_ge(tr_done, j + 1)
                src = ps[j % 4][:, :].rearrange("p (k q) -> p k q", k=KL)
                if j < TT:
                    o = t if t < LT else LT + 1
                    dst = ckvh[:, :, o * P:(o + 1) * P]
                else:
                    dst = qlh[:, :, t * P:(t + 1) * P]
                nc.scalar.activation(dst, src, ACT.Copy).then_inc(tr_hi, 1)
            act.wait_ge(tr_done, 2 * TT + 1)
            nc.scalar.activation(krT[:, 0:LAT], ps[4][0:ROPE, :], ACT.Copy)
            nc.scalar.activation(krT[:, LAT + CTX:KEYS], ps[5][0:ROPE, 0:CTX], ACT.Copy).then_inc(krt_evac, 1)
            split(None, 0, B_QR + 2)
            split(None, 0, B_QR + 3)
            for t, bank in enumerate(TOK_BANKS):
                tile_done(act, qr_done, 0, t, LT, B_QR + 2)
                if t == 0:
                    act.wait_ge(tr_lo, 2 * TT + 1)
                nc.scalar.activation(ql[:, t, :], ps[bank][:, :], ACT.Copy).then_inc(qr_evac, 1)
            for c in range(2):
                split(None, 0, B_VM + 2 * c + 2)
                for t, bank in enumerate(TOK_BANKS + [4]):
                    tile_done(act, vm_done, c * 5, t, 5, B_VM + 2 * c + 2)
                    nc.scalar.activation(vm[:, t, c * 512:(c + 1) * 512], ps[bank][:, :], ACT.Copy).then_inc(vm_evac, 1)
                split(None, 0, B_VM + 2 * c + 3)
                if c == 0:
                    for t in range(TT):
                        act.wait_ge(qrt_done, t + 1)
                        for half in range(2):
                            ins = nc.scalar.activation(qrT[:, 4 * half:4 * half + 4, t * P:(t + 1) * P],
                                                       ps[5 + half][0:ROPE, :].rearrange("p (h q) -> p h q", h=4), ACT.Copy)
                        ins.then_inc(qrt_evac, 1)

            for h in range(NH + 1):
                if h:
                    for s in range(5):
                        stage(None, NH + h - 1, s, False)
                if h < NH:
                    q_copy(B_HEAD + h + 1)
                    split(None, 0, B_HEAD + h + 2)
                if h:
                    for s in range(5, 8):
                        stage(None, NH + h - 1, s, False)

            def o_part(k):
                act.wait_ge(o_in[k % 3], 16 * (k // 3 + 1))
                nc.scalar.activation(oh[:, k, :], ostage[:, k % 3, :], ACT.Copy).then_inc(o_hi, 1)

            for b in range(32):
                if b < 7:
                    for k in (range(4) if b == 0 else range(2 * b + 2, 2 * b + 4)):
                        o_part(k)
                if b == 6:
                    act.wait_ge(g_psum, 1)
                    for c in range(2):
                        nc.scalar.activation(gate[:, c, 0:512], ps[4 + c][:, :], ACT.Copy).then_inc(g_evac, 1)
                if b in (8, 10, 12):
                    q = b // 2 - 3
                    act.wait_ge(g_psum, q + 1)
                    for c in range(2):
                        nc.scalar.activation(gate[:, c, q * 512:(q + 1) * 512], ps[4 + c][:, :],
                                             ACT.Copy).then_inc(g_evac, 1)
                split(None, 0, B_WO + b + 2)

            for t in range(TT):
                act.wait_ge(var_ready, t + 1)
                nc.scalar.activation(rstd[:, t:t + 1], mv[:, t, 1:2], ACT.Sqrt, bias=LN_EPS,
                                     scale=1.0).then_inc(sd_ready, 1)
            act.wait_ge(mod2_ready, 1)
            for k in range(KD):
                r = k % 2
                act.wait_ge(xt_ready, k + 1)
                if k >= 2:
                    act.wait_ge(h2_ready, k - 1)
                nc.scalar.activation(tmp[:, r, 0:LAT], ps[2 * r][:, :], ACT.Identity,
                                     scale=mod2[:, KD + k, 0:1], bias=mod2[:, k, 0:1])
                nc.scalar.activation(tmp[:, r, LAT:T], ps[2 * r + 1][:, 0:CTX], ACT.Identity,
                                     scale=mod2[:, KD + k, 1:2], bias=mod2[:, k, 1:2]).then_inc(h2_scaled, 1)

            def ff_group(i, g0):
                for b in range(FF_PER):
                    if b < 16:
                        j, q = divmod(b, 4)
                        if q == 3:
                            act.wait_ge(gate_done, at(i, GT, GT * g0 + j + 1))
                            nc.scalar.activation(ex[:, 0:HT], ps[UP_BANKS[j % 2][0]][:, 0:HT], ACT.Exp, scale=-1.0)
                            nc.scalar.activation(ex[:, HT:T], ps[UP_BANKS[j % 2][1]][:, 0:HT], ACT.Exp,
                                                 scale=-1.0).then_inc(fexp, 1)
                        split(i, FF_PER, B_FF + FF_PER * g0 + b + 2)
                        if q == 3:
                            act.wait_ge(f_ready, at(i, GT, GT * g0 + j + 1))
                            nc.scalar.activation(fh[:, j, :], tmp[:, 0, :], ACT.Copy).then_inc(f_hi, 1)
                    else:
                        split(i, FF_PER, B_FF + FF_PER * g0 + b + 2)

            ff_group(None, 0)
            with act.Fori(1, NG - 1) as i:
                ff_group(i, 0)
            ff_group(None, NG - 1)

            for t in range(TT):
                act.wait_ge(var_ready, TT + t + 1)
                nc.scalar.activation(rstd[:, t:t + 1], mv[:, t, 1:2], ACT.Sqrt, bias=LN_EPS,
                                     scale=1.0).then_inc(sd_ready, 1)

        @block.vector
        def _(dve):
            V = nc.vector
            own = Chain(dve, dve_own)

            def split(i, per, n):
                if i is None and n >= N_BLOCKS:
                    return
                dve.wait_ge(hi_ready, at(i, per, n + 1))
                V.tensor_tensor(wlo[:, n % 2, :], raw[:, n % 4, :], whi[:, n % 2, :].bitcast(f32),
                                ALU.subtract).then_inc(lo_ready, 1)

            own.link(V.memset(condw[:, :, :].bitcast(f32), 0.0))
            dve.wait_ge(consts_in, 16 * CONSTS)
            dve.wait_ge(cond_exp, 1)
            own.link(V.tensor_scalar(conds[:, 0], conds[:, 0], 1.0, None, ALU.add))
            own.link(V.reciprocal(conds[:, 0], conds[:, 0]))
            own.link(V.tensor_tensor(conds[:, 1], conds[:, 0], condf[:, :, :], ALU.mult))
            own.link(V.tensor_copy(condw[:, :, 0:2], conds[:, 1]))
            V.tensor_tensor(condw[:, :, 2:4], conds[:, 1], condw[:, :, 0:2].bitcast(f32),
                            ALU.subtract).then_inc(cond_ready, 1)

            def mod_split(i, n):
                dve.wait_ge(hi_ready, at(i, 16, n + 1))
                V.tensor_tensor(mlo[:, n % 4, :], mraw[:, n % 8, :], mhi[:, n % 4, :].bitcast(f32),
                                ALU.subtract).then_inc(lo_ready, 1)

            for n in range(16):
                mod_split(None, n)
            with dve.Fori(1, 4) as i:
                for n in range(16):
                    mod_split(i, n)
            split(None, 0, B_V)
            split(None, 0, B_V + 1)

            def mod_cols(dst, psum):
                V.tensor_copy(dst[:, 0:KD, :], psum[:, 0:2 * KD].rearrange("p (k c) -> p k c", c=2))
                own.link(V.tensor_scalar(dst[:, KD:2 * KD, :], psum[:, 2 * KD:4 * KD].rearrange("p (k c) -> p k c", c=2),
                                         1.0, None, ALU.add))

            dve.wait_ge(mod1_psum, 8)
            psum1 = ps[6][:, 0:4 * KD].rearrange("p (k c) -> p k c", c=2)
            bc = bcols[:, :].unsqueeze(2).to_broadcast([P, 2 * KD, 2])
            V.tensor_tensor(mod1[:, 0:KD, :], psum1[:, 0:KD, :], bc[:, 0:KD, :], ALU.add)
            own.link(V.scalar_tensor_tensor(out=mod1[:, KD:2 * KD, :], in0=psum1[:, KD:2 * KD, :], scalar=1.0,
                                            in1=bc[:, KD:2 * KD, :], op0=ALU.add, op1=ALU.add))
            dve.wait_ge(x_in, 16)

            def h_part(k):
                for lo, hi, c in ((0, LAT, 0), (LAT, T, 1)):
                    ins = V.tensor_scalar(xstage[:, k, lo:hi], xstage[:, k, lo:hi], mod1[:, KD + k, c:c + 1],
                                          mod1[:, k, c:c + 1], ALU.mult, ALU.add)
                ins.then_inc(h_scaled, 1)

            def h_rest(k):
                dve.wait_ge(h_hi, k + 1)
                V.tensor_tensor(hl[:, k, :], xstage[:, k, :], hh[:, k, :].bitcast(f32), ALU.subtract).then_inc(h_ready, 1)

            for b in range(16):
                if b < 7:
                    ks = list(range(4) if b == 0 else range(2 * b + 2, 2 * b + 4))
                    if b == 0:
                        h_part(0)
                    for k in ks:
                        if k + 1 < KD:
                            h_part(k + 1)
                        h_rest(k)
                split(None, 0, B_V + b + 2)

            def stage(i, a, s, na):
                A = lambda c: at(i, 5, 5 * a + c)
                if s < 5:
                    r = s % 3
                    dve.wait_ge(scores_ready, A(s + 1))
                    if na and s < LT:
                        if s == 0:
                            dve.wait_ge(tb_ready, (a + 1) if i is None else i + a + 1)
                        own.link(V.scalar_tensor_tensor(out=pb[:, r, 0:LAT], in0=ps[4][:, :], scalar=NA_SCALE,
                                                        in1=TB[:, (6 - 2 * s) * GRID:(14 - 2 * s) * GRID],
                                                        op0=ALU.mult, op1=ALU.add))
                        dve.wait_ge(ctx_scores, (4 * a + s + 1) if i is None else i * 4 + 4 * a + s + 1)
                        own.link(V.reduce_max(mx[:, r, 2:3], pb[:, r, :], AX.X))
                        scale = -1.0
                    elif s < LT:
                        bk = 4 if s % 2 == 0 else 0
                        V.reduce_max(mx[:, r, 0:1], ps[bk][:, :], AX.X)
                        own.link(V.reduce_max(mx[:, r, 1:2], ps[bk + 1][:, 0:CTX], AX.X))
                        own.link(V.tensor_tensor(mx[:, r, 2:3], mx[:, r, 0:1], mx[:, r, 1:2], ALU.max))
                        scale = -MLA_SCALE
                    else:
                        own.link(V.reduce_max(mx[:, r, 2:3], ps[4][:, 0:CTX], AX.X))
                        scale = -(NA_SCALE if na else MLA_SCALE)
                    V.tensor_scalar(mx[:, r, 3:4], mx[:, r, 2:3], scale, None, ALU.mult).then_inc(max_ready, 1)
                if 1 <= s < 6:
                    t = s - 1
                    r = t % 3
                    dve.wait_ge(exp_ready, A(t + 1))
                    if not na and t < LT:
                        own.link(V.tensor_tensor(rs[:, r, 2:3], rs[:, r, 0:1], rs[:, r, 1:2], ALU.add))
                    own.link(V.reciprocal(rs[:, r, 3:4], rs[:, r, 2:3]))
                    n = T if t < LT else CTX
                    V.tensor_scalar(pb[:, r, 0:n], pb[:, r, 0:n], rs[:, r, 3:4], None, ALU.mult).then_inc(p_ready, 1)

            def k_copy(blocks, n):
                dve.wait_ge(used, blocks)
                V.tensor_copy(kT[:, 0:n], ps[2][:, 0:n])
                V.tensor_copy(kT[:, n:2 * n], ps[3][:, 0:n]).then_inc(k_evac, 1)

            def na_iter(i, stages):
                for b in range(NA_PER):
                    g, r = divmod(b, 5)
                    if b == 15:
                        k_copy(at(i, NA_PER, B_NA + b + 1), HT)
                    split(i, NA_PER, B_NA + b + 2)
                    if stages and r in (1, 3):
                        stage(i, -1, 2 * g + (r == 3), True)

            na_iter(None, False)
            with dve.Fori(1, NH) as i:
                own.enter(i, 1, 14)
                na_iter(i, True)
                own.leave(NH - 1)

            def norm_chunk(dst, c, done):
                dve.wait_ge(lat_rt, c + 1)
                own.link(V.reciprocal(small[:, 16:16 + TT], small[:, 8:8 + TT]))
                for t in range(TT):
                    V.scalar_tensor_tensor(out=dst[:, t, :], in0=dst[:, t, :], scalar=small[:, 16 + t:17 + t],
                                           in1=latgt[:, 1 - c, :], op0=ALU.mult, op1=ALU.mult).then_inc(done, 1)

            def rotate(dst, src, tmp_, t, nh):
                cos = ropet[:, 0, t, :]
                sin = ropet[:, 1, t, :]
                v = lambda x: x.rearrange("p (h q u j) -> p h q u j", h=nh, q=2, u=2)
                sn = sin.rearrange("p (q u j) -> p q u j", q=2, u=2)
                for q in range(2):
                    for u in range(2):
                        ins = V.tensor_tensor(v(tmp_)[:, :, q, u, :], v(src)[:, :, q, 1 - u, :],
                                              sn[:, q, u, :].unsqueeze(1).to_broadcast([P, nh, 16]), ALU.mult)
                own.link(ins)
                own.link(V.tensor_tensor(dst.rearrange("p (h c) -> p h c", h=nh), src.rearrange("p (h c) -> p h c", h=nh),
                                         cos.unsqueeze(1).to_broadcast([P, nh, ROPE]), ALU.mult))
                return V.tensor_tensor(dst, dst, tmp_, ALU.add)

            for b in range(17):
                split(None, 0, B_KVL + b + 2)
                if b < 8:
                    stage(None, NH - 1, b, True)
                if b == 9:
                    norm_chunk(kvl, 0, kvl_ready)
            norm_chunk(ql, 1, ql_ready)
            dve.wait_ge(kr_evac, 1)
            for t in range(LT):
                own.link(rotate(krr[:, t, :], kr[:, t, :], krr[:, LT, :], t, 1))
            V.tensor_copy(krr[:, LT, :], kr[:, LT, :]).then_inc(kr_ready, 1)

            dve.wait_ge(tr_hi, 1)
            V.tensor_tensor(ckvl[:, :, LAT:LAT + CTX], ckvs[:, :, :], ckvh[:, :, LAT:LAT + CTX].bitcast(f32),
                            ALU.subtract).then_inc(tr_lo, 1)
            for j in range(2 * TT):
                t = j % TT
                dve.wait_ge(tr_hi, j + 2)
                src = ps[j % 4][:, :].rearrange("p (k q) -> p k q", k=KL)
                if j < TT:
                    o = t if t < LT else LT + 1
                    h_, l_ = ckvh[:, :, o * P:(o + 1) * P], ckvl[:, :, o * P:(o + 1) * P]
                else:
                    h_, l_ = qlh[:, :, t * P:(t + 1) * P], qll[:, :, t * P:(t + 1) * P]
                V.tensor_tensor(l_, src, h_.bitcast(f32), ALU.subtract).then_inc(tr_lo, 1)
            split(None, 0, B_QR + 2)
            split(None, 0, B_QR + 3)
            for t in range(TT):
                dve.wait_ge(qr_evac, t + 1)
                if t < LT:
                    if t:
                        dve.wait_ge(qr_roped, t)
                    rotate(qr[:, t, :], ql[:, t, :], sq, t, NH).then_inc(qr_roped, 1)
                else:
                    V.tensor_copy(qr[:, t, :], ql[:, t, :]).then_inc(qr_roped, 1)
                if t in (1, 3):
                    split(None, 0, B_VM + 2 + t // 2)
            for n in range(B_VM + 4, B_VM + 6):
                split(None, 0, n)

            for h in range(NH + 1):
                if h:
                    for s in range(5):
                        stage(None, NH + h - 1, s, False)
                if h < NH:
                    k_copy(B_HEAD + h + 1, KEYS // 2)
                    split(None, 0, B_HEAD + h + 2)
                if h:
                    for s in range(5, 8):
                        stage(None, NH + h - 1, s, False)

            def o_part(k):
                dve.wait_ge(o_hi, k + 1)
                V.tensor_tensor(ol[:, k, :], ostage[:, k % 3, :], oh[:, k, :].bitcast(f32), ALU.subtract).then_inc(o_lo, 1)

            for b in range(32):
                if b < 7:
                    for k in (range(4) if b == 0 else range(2 * b + 2, 2 * b + 4)):
                        o_part(k)
                if b % 8 == 7:
                    c = b // 8
                    cols = slice(c * 512, (c + 1) * 512)
                    if c == 0:
                        dve.wait_ge(xs_in, 16)
                    if c == 0:
                        dve.wait_ge(g_evac, 2)
                    else:
                        dve.wait_ge(g_evac, 8)
                    for t, bank in enumerate(TOK_BANKS):
                        tile_done(dve, wo_done, c * LT, t, LT, B_WO + 8 * c + 8)
                        V.tensor_tensor(tmp[:, t % 2, 0:512], ps[bank][:, :], gate[:, t // LT, cols],
                                        ALU.mult).then_inc(wo_evac, 1)
                        dve.wait_ge(wo_evac, c * TT + t + 1)
                        own.link(V.scalar_tensor_tensor(out=xs[:, t, cols], in0=xs[:, t, cols], scalar=ALPHA,
                                                        in1=tmp[:, t % 2, 0:512], op0=ALU.mult, op1=ALU.add))
                        V.bn_stats(stat[:, t, c, :], xs[:, t, cols]).then_inc(dve_own, 1)
                        own.n += 1
                split(None, 0, B_WO + b + 2)

            def stats(t, n):
                dve.wait_ge(dve_own, own.n)
                V.bn_aggr(mv[:, t, :], stat[:, t, :, :].rearrange("p c s -> p (c s)")).then_inc(var_ready, 1)

            for t in range(TT):
                stats(t, 0)
            for t in range(TT):
                dve.wait_ge(sd_ready, t + 1)
                own.link(V.reciprocal(small[:, 24 + t:25 + t], rstd[:, t:t + 1]))
                V.tensor_scalar(xs[:, t, :], xs[:, t, :], mv[:, t, 0:1], small[:, 24 + t:25 + t], ALU.subtract,
                                ALU.mult).then_inc(xn_ready, 1)
                if t == 0:
                    dve.wait_ge(mod2_psum, 1)
                    mod_cols(mod2, ps[6])
                    bsc = small[:, 32:64].rearrange("p (k c) -> p k c", c=2)
                    lb = lncols[:, 1, :].unsqueeze(2).to_broadcast([P, KD, 2])
                    lg = lncols[:, 0, :].unsqueeze(2).to_broadcast([P, KD, 2])
                    own.link(V.tensor_tensor(bsc, mod2[:, KD:2 * KD, :], lb, ALU.mult))
                    own.link(V.tensor_tensor(mod2[:, 0:KD, :], mod2[:, 0:KD, :], bsc, ALU.add))
                    V.tensor_tensor(mod2[:, KD:2 * KD, :], mod2[:, KD:2 * KD, :], lg, ALU.mult).then_inc(mod2_ready, 1)
            for k in range(KD):
                r = k % 2
                dve.wait_ge(h2_scaled, k + 1)
                V.tensor_copy(oh[:, k, :], tmp[:, r, :]).then_inc(h2_hi, 1)
                dve.wait_ge(h2_hi, k + 1)
                V.tensor_tensor(ol[:, k, :], tmp[:, r, :], oh[:, k, :].bitcast(f32), ALU.subtract).then_inc(h2_ready, 1)
            for c in range(8):
                dve.wait_ge(g_psum, 5 + c // 2)
                V.tensor_copy(gate[:, c % 2, c // 2 * 512:(c // 2 + 1) * 512],
                              ps[4 + c % 2][:, :]).then_inc(g_evac, 1)

            def ff_group(i, g0, last=False):
                for b in range(FF_PER):
                    if b < 16:
                        j, q = divmod(b, 4)
                        if q == 3:
                            n = at(i, GT, GT * g0 + j + 1)
                            dve.wait_ge(fexp, n)
                            own.link(V.tensor_scalar(ex[:, :], ex[:, :], 1.0, None, ALU.add))
                            own.link(V.reciprocal(ex[:, :], ex[:, :]))
                            V.tensor_tensor(ex[:, 0:HT], ex[:, 0:HT], ps[UP_BANKS[j % 2][0]][:, 0:HT], ALU.mult)
                            V.tensor_tensor(ex[:, HT:T], ex[:, HT:T], ps[UP_BANKS[j % 2][1]][:, 0:HT],
                                            ALU.mult).then_inc(gate_used, 1)
                            dve.wait_ge(used, at(i, FF_PER, B_FF + FF_PER * g0 + b + 1))
                            dve.wait_ge(gate_used, n)
                            V.tensor_tensor(tmp[:, 0, 0:HT], ex[:, 0:HT], ps[UP_BANKS[j % 2][2]][:, 0:HT], ALU.mult)
                            V.tensor_tensor(tmp[:, 0, HT:T], ex[:, HT:T], ps[UP_BANKS[j % 2][3]][:, 0:HT],
                                            ALU.mult).then_inc(f_ready, 1)
                        split(i, FF_PER, B_FF + FF_PER * g0 + b + 2)
                        if q == 3:
                            dve.wait_ge(f_hi, n)
                            V.tensor_tensor(fl[:, j, :], tmp[:, 0, :], fh[:, j, :].bitcast(f32),
                                            ALU.subtract).then_inc(f_lo, 1)
                    else:
                        c, q = divmod(b - 16, 2)
                        if q == 1:
                            cols = slice(c * 512, (c + 1) * 512)
                            if i is None and g0 == 0 and c == 0:
                                dve.wait_ge(res_ready, 4 * TT)
                            for t, bank in enumerate(DOWN_BANKS):
                                n = at(i, 4 * TT, (4 * g0 + c) * TT + t + 1)
                                if t < LT:
                                    dve.wait_ge(down_done, at(i, 4 * LT, (4 * g0 + c) * LT + t + 1))
                                else:
                                    dve.wait_ge(used, at(i, FF_PER, B_FF + FF_PER * g0 + b + 1))
                                V.tensor_tensor(tmp[:, 1, 0:512], ps[bank][:, :], gate[:, t // LT, cols],
                                                ALU.mult).then_inc(down_evac, 1)
                                dve.wait_ge(down_evac, n)
                                own.link(V.tensor_tensor(xs[:, t, cols], xs[:, t, cols], tmp[:, 1, 0:512], ALU.add))
                                if last:
                                    V.bn_stats(stat[:, t, c, :], xs[:, t, cols]).then_inc(dve_own, 1)
                                    own.n += 1
                        split(i, FF_PER, B_FF + FF_PER * g0 + b + 2)

            ff_group(None, 0)
            with dve.Fori(1, NG - 1) as i:
                own.enter(i, 1, GT * 2 + 4 * TT)
                ff_group(i, 0)
                own.leave(NG - 2)
            ff_group(None, NG - 1, last=True)

            for t in range(TT):
                stats(t, 0)
            dve.wait_ge(lnb_in, 16)
            for t in range(TT):
                dve.wait_ge(sd_ready, TT + t + 1)
                own.link(V.reciprocal(small[:, 24 + t:25 + t], rstd[:, t:t + 1]))
                own.link(V.tensor_scalar(xs[:, t, :], xs[:, t, :], mv[:, t, 0:1], small[:, 24 + t:25 + t],
                                         ALU.subtract, ALU.mult))
                own.link(V.tensor_tensor(xs[:, t, :], xs[:, t, :], lnb[:, 0, :], ALU.mult))
                V.tensor_tensor(xs[:, t, :], xs[:, t, :], lnb[:, 1, :], ALU.add).then_inc(y_ready, 1)

        @block.tensor
        def _(pe):
            mm = nc.tensor.matmul

            def mm3(out, ah, al, bh, bl, first, last):
                mm(out, ah, bh, start=first, stop=False)
                mm(out, ah, bl, start=False, stop=False)
                return mm(out, al, bh, start=False, stop=last)

            def arrived(i, per, n):
                pe.wait_ge(lo_ready, at(i, per, n + 1))

            def tok_block(n, ah, al, k0, first, last, banks, before=None, after=None, cols=512, tile=None):
                for t, bank in enumerate(banks):
                    if before:
                        before(t)
                    o = (t if tile is None else tile[t]) * P
                    for kk in range(2):
                        w = slice(kk * cols, (kk + 1) * cols)
                        ins = mm3(ps[bank][:, 0:cols], ah[:, k0 + kk, o:o + P], al[:, k0 + kk, o:o + P],
                                  hi_of(n)[:, w], lo_of(n)[:, w], first and kk == 0, last and kk == 1)
                    if after and t < len(banks) - 1:
                        after(t, ins)
                return ins

            def feat_block(n, bh, bl, k0, first, last, before=None, after=None, widths=(HT, HT), banks=(0, 1, 2, 3), b2=None):
                for o in range(4):
                    if before:
                        before(o)
                    half, w = o % 2, widths[o // 2]
                    xh, xl = (bh, bl) if o < 2 or b2 is None else b2
                    for kk in range(4):
                        c = slice(kk * 256 + o // 2 * P, kk * 256 + o // 2 * P + P)
                        m = slice(half * w, (half + 1) * w)
                        ins = mm3(ps[banks[o]][:, 0:w], hi_of(n)[:, c], lo_of(n)[:, c], xh[:, k0 + kk, m],
                                  xl[:, k0 + kk, m], first and kk == 0, last and kk == 3)
                    if after and o < 3:
                        after(o, ins)
                return ins

            def mod_block(i, per, n, b, chunk_free, bank=7, hi=None, lo=None):
                arrived(i, per, n)
                if b == 0 and chunk_free is not None:
                    pe.wait_ge(modrow_ready, chunk_free)
                hi, lo = (hi_of(n), lo_of(n)) if hi is None else (hi, lo)
                for kk in range(2):
                    w = slice(kk * 512, (kk + 1) * 512)
                    mm(ps[bank][:, :], condw[:, 2 * b + kk, :], hi[:, w], start=(b == 0 and kk == 0), stop=False)
                    ins = mm(ps[bank][:, :], condw[:, 2 * b + kk, :], lo[:, w], start=False, stop=(b == 7 and kk == 1))
                ins.then_inc(used, 1)

            pe.wait_ge(cond_ready, 1)

            def turn_rows(i, c):
                pe.wait_ge(modrow_ready, at(i, 2, c + 1))
                for j in range(4):
                    o = at(i, 16, 8 * c + 2 * j)
                    ins = mm(ps[6][:, bass.ds(o, 2)], modrow[:, c % 2, j * P:(j + 1) * P], selt[0:4, 0:2],
                             start=True, stop=True)
                ins.then_inc(mod1_psum, 1)

            def mod_pair(i):
                for b in range(16):
                    c = b // 8
                    mod_block(i, 16, b, b % 8, None if i is None else i * 2 + c - 1, MOD_BANKS[c],
                              mhi[:, b % 4, :], mlo[:, b % 4, :])
                    if b % 8 == 2 and (i is not None or c):
                        turn_rows(i, c - 1)

            mod_pair(None)
            with pe.Fori(1, 4) as i:
                mod_pair(i)
            turn_rows(None, 7)

            def mod_columns(shift, scale, done):
                for j in range(2 * KD):
                    rows = shift if j < KD else scale
                    ins = mm(ps[6][:, 2 * j:2 * j + 2], rows[:, j % KD * P:(j % KD + 1) * P], selt[:, 0:2],
                             start=True, stop=True)
                ins.then_inc(done, 1)

            for c in range(2):
                for b in range(8):
                    n = B_V + 8 * c + b
                    arrived(None, 0, n)
                    if c == 0:
                        pe.wait_ge(h_ready, 2 * b + 2)
                        if b == 0:
                            pe.wait_ge(modrow_ready, 8)
                    tok_block(n, hh, hl, 2 * b, b == 0, b == 7, TOK_BANKS,
                              before=(lambda t: pe.wait_ge(v_evac, t + 1)) if c == 1 and b == 0 else None,
                              after=(lambda t, ins: ins.then_inc(v_done, 1)) if b == 7 else None
                              ).then_inc(used, 1)

            def stage(i, a, s, na, kcached=None, h=None):
                A = lambda c: at(i, 5, 5 * a + c)
                one = (lambda c: a + c if i is None else i + a + c)

                def scores():
                    if s < 5:
                        bk = 4 if na or s % 2 == 0 else 0
                        if s == 0:
                            pe.wait_ge(q_evac, one(1))
                            pe.wait_ge(k_evac, one(1))
                        if na and s:
                            pe.wait_ge(exp_ready, A(s))
                        elif s >= 2:
                            pe.wait_ge(exp_ready, A(s - 1))
                        if s == 0 and i is None:
                            pe.wait_ge(o_evac, a)
                        q = qT[:, s * P:(s + 1) * P]
                        if s < LT:
                            if na:
                                mm(ps[bk][:, :], q, kT[:, 0:LAT], start=True, stop=True)
                                mm(ps[bk + 1][:, 0:CTX], q, kcached, start=True, stop=True).then_inc(scores_ready, 1)
                            else:
                                qq = qrT[:, h, s * P:(s + 1) * P]
                                mm(ps[bk][:, :], q, kT[:, 0:LAT], start=True, stop=False)
                                mm(ps[bk][:, :], qq, krT[:, 0:LAT], start=False, stop=True)
                                mm(ps[bk + 1][:, 0:CTX], q, kT[:, LAT:T], start=True, stop=False)
                                mm(ps[bk + 1][:, 0:CTX], qq, krT[:, LAT:T], start=False, stop=True).then_inc(scores_ready, 1)
                        elif na:
                            mm(ps[4][:, 0:CTX], q, kT[:, LAT:T], start=True, stop=True).then_inc(scores_ready, 1)
                        else:
                            mm(ps[4][:, 0:CTX], q, kT[:, T:KEYS], start=True, stop=False)
                            mm(ps[4][:, 0:CTX], qrT[:, h, LAT:T], krT[:, T:KEYS], start=False,
                               stop=True).then_inc(scores_ready, 1)

                def transposes():
                    if 2 <= s < 7:
                        t = s - 2
                        pe.wait_ge(p_ready, A(t + 1))
                        if t:
                            pe.wait_ge(pt_free, A(t))
                        if t < LT:
                            for k in range(4):
                                nc.tensor.transpose(ps[6][:, k * P:(k + 1) * P], pb[:, t % 3, k * P:(k + 1) * P], idt[:, :])
                            if na and t == 3:
                                nc.tensor.transpose(ps[5][:, 2 * P:3 * P], kT[:, LAT:T], idt[:, :])
                            last = ps[5][:, P:2 * P] if na else ps[7][:, 0:P]
                            nc.tensor.transpose(last, pb[:, t % 3, LAT:T], idt[:, :]).then_inc(pt_ready, 1)
                        else:
                            nc.tensor.transpose(ps[6][:, 0:P], pb[:, t % 3, 0:P], idt[:, :]).then_inc(pt_ready, 1)

                for part in (transposes, scores) if na else (scores, transposes):
                    part()
                if s == 7:
                    pe.wait_ge(pt_free, A(5))
                    pe.wait_ge(vh_ready, one(1))
                    for k in range(5):
                        mm(ps[4][:, :], vh[:, k, :], PT[:, k, :], start=(k == 0), stop=(k == 4))
                    mm(ps[5][:, 0:CTX], vh[:, 5, :], PTc[:, :], start=True, stop=True).then_inc(pv_ready, 1)

            def na_iter(i, stages):
                for b in range(NA_PER):
                    g, r = divmod(b, 5)
                    n = B_NA + b
                    if r == 0:
                        arrived(i, NA_PER, n)
                        before = None
                        if b == 0:
                            if i is None:
                                before = lambda o: pe.wait_ge(v_evac, TT + 1 + o)
                            else:
                                before = lambda o: pe.wait_ge(q_evac if o < 2 else k_evac, i + 0)
                        feat_block(n, hh, hl, 4 * g, g == 0, g == 3, before=before).then_inc(used, 1)
                    else:
                        m = 4 * g + r - 1
                        if i is None and m == 0:
                            pe.wait_ge(v_evac, 2 * TT)
                        mod_block(i, NA_PER, n, m % 8, (8 + m // 8) if i is None else i * 2 + 8 + m // 8)
                    if stages and r in (1, 3):
                        s = 2 * g + (r == 3)
                        if s == 0:
                            na_first_wait(i)
                        stage(i, -1, s, True, kct[:, i - 1, :])

            def na_first_wait(i):
                pe.wait_ge(na_consts_in, 80)
                pe.wait_ge(vh_ready, i)

            na_iter(None, False)
            with pe.Fori(1, NH) as i:
                na_iter(i, True)

            for b in range(17):
                n = B_KVL + b
                arrived(None, 0, n)
                if b < 16:
                    c, q = divmod(b, 8)
                    before = None
                    if c == 0 and q == 0:
                        def before(t):
                            if t < 4:
                                pe.wait_ge(q_evac if t < 2 else k_evac, NH)
                            else:
                                pe.wait_ge(modrow_ready, MOD_CHUNKS)
                    elif q == 0:
                        before = lambda t: pe.wait_ge(lat_evac, t + 1)
                    ins = tok_block(n, hh, hl, 2 * q, q == 0, q == 7, TOK_BANKS, before=before,
                                    after=(lambda t, ins: ins.then_inc(lat_done, 1)) if q == 7 else None)
                    ins.then_inc(used, 1)
                else:
                    for half in range(2):
                        pe.wait_ge(lat_evac, TT + half + 1)
                        m = slice(half * HT, (half + 1) * HT)
                        for k in range(KD):
                            w = slice(k * ROPE, (k + 1) * ROPE)
                            ins = mm3(ps[half][0:ROPE, 0:HT], hi_of(n)[:, w], lo_of(n)[:, w], hh[:, k, m], hl[:, k, m],
                                      k == 0, k == KD - 1)
                    ins.then_inc(used, 1)
                    pe.wait_ge(krf_evac, 1)
                    pe.wait_ge(o_evac, NH)
                    for t in range(TT):
                        ins = nc.tensor.transpose(ps[4][:, t * ROPE:(t + 1) * ROPE], krf[:, t * P:(t + 1) * P],
                                                  idt[0:ROPE, 0:ROPE])
                    ins.then_inc(krf_turned, 1)
                if b < 8:
                    stage(None, NH - 1, b, True, kct[:, NH - 1, :])

            pe.wait_ge(lat_evac, 2 * TT)
            for j in range(2 * TT):
                t = j % TT
                src = kvl if j < TT else ql
                pe.wait_ge(kvl_ready if j < TT else ql_ready, t + 1)
                if j >= 4:
                    pe.wait_ge(tr_lo, j - 2)
                for k in range(KL):
                    ins = nc.tensor.transpose(ps[j % 4][:, k * P:(k + 1) * P], src[:, t, k * P:(k + 1) * P], idt[:, :])
                ins.then_inc(tr_done, 1)
            pe.wait_ge(kr_ready, 1)
            for t in range(LT):
                nc.tensor.transpose(ps[4][0:ROPE, t * P:(t + 1) * P], krr[:, t, :], idt[:, :])
            nc.tensor.transpose(ps[5][0:ROPE, 0:P], krr[:, LT, :], idt[:, :]).then_inc(tr_done, 1)

            for q in range(2):
                n = B_QR + q
                arrived(None, 0, n)
                if q == 0:
                    pe.wait_ge(tr_lo, 2 * TT + 1)
                tok_block(n, qlh, qll, 2 * q, q == 0, q == 1, TOK_BANKS,
                          after=(lambda t, ins: ins.then_inc(qr_done, 1)) if q else None
                          ).then_inc(used, 1)

            def turn_q(t):
                pe.wait_ge(qr_roped, t + 1)
                if t:
                    pe.wait_ge(qrt_evac, t)
                for h in range(NH):
                    ins = nc.tensor.transpose(ps[5 + h // 4][0:ROPE, h % 4 * P:(h % 4 + 1) * P],
                                              qr[:, t, h * ROPE:(h + 1) * ROPE], idt[:, :])
                ins.then_inc(qrt_done, 1)

            for c in range(2):
                for q in range(2):
                    n = B_VM + 2 * c + q
                    arrived(None, 0, n)
                    before = None
                    if not c and not q:
                        pe.wait_ge(mla_in, 32)

                        def before(t):
                            pe.wait_ge(qr_evac, t + 1) if t < TT else pe.wait_ge(krt_evac, 1)
                    elif not q:
                        def before(t):
                            pe.wait_ge(vm_evac, t + 1)
                            if t:
                                turn_q(t - 1)
                    tok_block(n, ckvh, ckvl, 2 * q, q == 0, q == 1, TOK_BANKS + [4], before=before,
                              after=(lambda t, ins: ins.then_inc(vm_done, 1)) if q else None
                              ).then_inc(used, 1)

            for h in range(NH + 1):
                if h:
                    for s in range(5):
                        stage(None, NH + h - 1, s, False, h=h - 1)
                if h < NH:
                    n = B_HEAD + h
                    arrived(None, 0, n)
                    if h == 0:
                        pe.wait_ge(vm_evac, 12)
                        pe.wait_ge(qrt_evac, TT)
                    else:
                        pe.wait_ge(exp_ready, 5 * (NH + h - 1) + 4)
                        pe.wait_ge(k_evac, NH + h)
                    feat_block(n, qlh, qll, 0, True, True, widths=(HT, KEYS // 2), b2=(ckvh, ckvl)).then_inc(used, 1)
                if h:
                    for s in range(5, 8):
                        stage(None, NH + h - 1, s, False)

            def gate_bcast(rows, q):
                for c in range(2):
                    ins = mm(ps[4 + c][:, :], selt[:, 2 + c * P:2 + (c + 1) * P], rows[:, q * 512:(q + 1) * 512],
                             start=True, stop=True)
                ins.then_inc(g_psum, 1)

            for b in range(32):
                n = B_WO + b
                arrived(None, 0, n)
                c, q = divmod(b, 8)
                if c == 0:
                    pe.wait_ge(o_lo, 2 * q + 2)
                ins = tok_block(n, oh, ol, 2 * q, q == 0, q == 7, TOK_BANKS,
                                before=(lambda t: pe.wait_ge(wo_evac, (c - 1) * TT + t + 1)) if c and not q else None,
                                after=(lambda t, ins: ins.then_inc(wo_done, 1)) if q == 7 else None)
                ins.then_inc(used, 1)
                if b == 5:
                    pe.wait_ge(rows2_in, 32)
                    pe.wait_ge(o_evac, 2 * NH)
                    gate_bcast(rows2, 0)
                if b in (7, 9, 11):
                    pe.wait_ge(g_evac, b - 5)
                    gate_bcast(rows2, (b - 5) // 2)
            pe.wait_ge(rows3_in, 32)
            pe.wait_ge(rows2_in, 64)
            mod_columns(rows3, rows2, mod2_psum)
            pe.wait_ge(xn_ready, TT)
            for k in range(KD):
                r = k % 2
                if k >= 2:
                    pe.wait_ge(h2_scaled, k - 1)
                for t in range(LT):
                    nc.tensor.transpose(ps[2 * r][:, t * P:(t + 1) * P], xs[:, t, k * P:(k + 1) * P], idt[:, :])
                nc.tensor.transpose(ps[2 * r + 1][:, 0:P], xs[:, LT, k * P:(k + 1) * P], idt[:, :]).then_inc(xt_ready, 1)

            pe.wait_ge(rows2_in, 96)
            for q in range(4):
                pe.wait_ge(g_evac, 8 + 2 * q)
                gate_bcast(rows2, q)

            def ff_group(i, g0):
                for b in range(FF_PER):
                    n = B_FF + FF_PER * g0 + b
                    arrived(i, FF_PER, n)
                    if b < 16:
                        j, q = divmod(b, 4)
                        def before(o, j=j, q=q):
                            if q:
                                return
                            later = i is not None or g0
                            if j >= 2 or (j == 1 and later):
                                pe.wait_ge(gate_used if o < 2 else f_ready, at(i, GT, GT * g0 + j - 1))
                            if later and (j == 0 or (j == 1 and o == 3)):
                                pe.wait_ge(down_evac, at(i, 4 * TT, (4 * g0 - 1) * TT + DOWN_BANKS.index(UP_BANKS[j][o]) + 1))
                        if i is None and g0 == 0 and b == 0:
                            pe.wait_ge(h2_ready, KD)
                            pe.wait_ge(g_evac, 16)
                        ins = feat_block(n, oh, ol, 4 * q, q == 0, q == 3, before=before, banks=UP_BANKS[j % 2],
                                         after=(lambda o, ins: ins.then_inc(gate_done, 1) if o == 1 else None) if q == 3 else None)
                        ins.then_inc(used, 1)
                    else:
                        c, q = divmod(b - 16, 2)

                        def before(t, c=c, q=q):
                            if q:
                                return
                            if c:
                                pe.wait_ge(down_evac, at(i, 4 * TT, (4 * g0 + c - 1) * TT + t + 1))
                            else:
                                pe.wait_ge(gate_used if t < 2 else f_ready, at(i, GT, GT * g0 + (3 if t < 4 else 4)))
                        pe.wait_ge(f_lo, at(i, GT, GT * g0 + 2 * q + 2))
                        ins = tok_block(n, fh, fl, 2 * q, q == 0, q == 1, DOWN_BANKS, before=before,
                                        after=(lambda t, ins: ins.then_inc(down_done, 1)) if q else None)
                        ins.then_inc(used, 1)

            ff_group(None, 0)
            with pe.Fori(1, NG - 1) as i:
                ff_group(i, 0)
            ff_group(None, NG - 1)


_NAMES = ["wstream", "xT", "xtok", "cond", "bmod", "rpb", "kcT", "vc", "ckvcT", "krcT", "lncol", "lnrow", "latg",
          "bcol", "rope", "cap", "ident", "sel"]
_OUTS = [("y", (TT, P, D)), ("s_k", (CTX, NH * P)), ("s_v", (CTX, NH * P)), ("s_ckv", (CTX, LORA)), ("s_kr", (CTX, ROPE))]


def _tok_blocks(np, w):
    K, N = w.shape
    return w.reshape(K // 256, 2, P, N // 512, 512).transpose(3, 0, 2, 1, 4).reshape(-1, P, 1024)


def _feat_blocks(np, wa, wb):
    K, H, _ = wa.shape
    w = np.stack([wa, wb], axis=2)
    return w.reshape(K // 512, 4, P, H, 256).transpose(3, 0, 2, 1, 4).reshape(-1, P, 1024)


def _layout(np, a):
    f = {k: np.asarray(v) for k, v in a.items()}
    w_in, w_mod, w_qb, w_kvb = f["w_in"][0], f["w_mod"][0], f["w_q_b"][0], f["w_kv_b"][0]
    na = NH * P
    mod = _tok_blocks(np, w_mod)
    v = _tok_blocks(np, w_in[:, 2 * na:3 * na])
    qk = _feat_blocks(np, w_in[:, 0:na].reshape(D, NH, P), w_in[:, na:2 * na].reshape(D, NH, P))
    lat = w_in[:, 3 * na:]
    qb = w_qb.reshape(LORA, NH, P + ROPE)
    kb = w_kvb.reshape(LORA, NH, 2 * P)
    parts = [mod[0:64], v]
    mods = mod[64:].reshape(NH, 4, 4, P, 1024)
    qks = qk.reshape(NH, 4, 1, P, 1024)
    parts.append(np.concatenate([qks, mods], axis=2).reshape(-1, P, 1024))
    parts.append(_tok_blocks(np, lat[:, LORA:2 * LORA]))
    parts.append(_tok_blocks(np, lat[:, 0:LORA]))
    parts.append(lat[:, 2 * LORA:].reshape(KD, P, ROPE).transpose(1, 0, 2).reshape(1, P, 1024))
    parts.append(_tok_blocks(np, qb[:, :, P:].reshape(LORA, NH * ROPE)))
    parts.append(_tok_blocks(np, kb[:, :, P:].reshape(LORA, NH * P)))
    parts.append(_feat_blocks(np, qb[:, :, 0:P], kb[:, :, 0:P]))
    parts.append(_tok_blocks(np, f["w_o"][0]))
    wgu = f["w_gu"][0].reshape(D, 2, FF // P, P)
    up = _feat_blocks(np, wgu[:, 0], wgu[:, 1]).reshape(NG, GT * 4, P, 1024)
    down = _tok_blocks(np, f["w_down"][0]).reshape(4, NG, 2, P, 1024).transpose(1, 0, 2, 3, 4).reshape(NG, 8, P, 1024)
    parts.append(np.concatenate([up, down], axis=1).reshape(-1, P, 1024))
    x = np.concatenate([f["x_sample"][0], f["x_prompt"][0]], axis=0)
    out = {
        "wstream": np.concatenate(parts, axis=0),
        "xT": x.reshape(T, KD, P).transpose(2, 1, 0),
        "xtok": x.reshape(TT, P, D).transpose(1, 0, 2),
        "cond": np.stack([f["c"][0], f["c_ctx"]], axis=-1).reshape(KD, P, 2).transpose(1, 0, 2),
        "bmod": f["b_mod"][0:1],
        "bcol": f["b_mod"][0, 0:2 * D].reshape(2 * KD, P).transpose(1, 0),
        "rpb": f["na_rpb"][0].reshape(NH * RPB),
        "kcT": f["cache_na_k"][0, 0].transpose(2, 1, 0),
        "vc": f["cache_na_v"][0, 0].reshape(CTX, NH * P),
        "ckvcT": f["cache_mla_ckv"][0, 0].reshape(CTX, KL, P).transpose(2, 1, 0),
        "krcT": f["cache_mla_krope"][0, 0].transpose(1, 0),
        "lncol": np.stack([f["ln1_g"][0].reshape(KD, P).transpose(1, 0), f["ln1_b"][0].reshape(KD, P).transpose(1, 0)], axis=1),
        "lnrow": np.stack([f["ln1_g"][0], f["ln1_b"][0], f["ln2_g"][0], f["ln2_b"][0]], axis=0)[None],
        "latg": np.stack([f["q_a_norm"][0], f["kv_a_norm"][0]], axis=0),
    }
    return out


def _constants(np):
    f32 = np.float32
    half = ROPE // 2
    pos = np.arange(LAT, dtype=np.int32)
    inv = (f32(10000.0) ** (-np.arange(0, half, 2, dtype=f32) / f32(half))).astype(f32)
    cs = []
    for p in (pos // GRID, pos % GRID):
        ang = p.astype(f32)[:, None] * inv
        cs.append((np.cos(ang), np.sin(ang)))
    cos = np.concatenate([cs[0][0], cs[0][0], cs[1][0], cs[1][0]], axis=1)
    sin = np.concatenate([-cs[0][1], cs[0][1], -cs[1][1], cs[1][1]], axis=1)
    rope = np.stack([cos, sin]).reshape(2, LT, P, ROPE).transpose(2, 0, 1, 3).astype(f32)
    col = np.arange(GRID)
    start = np.clip(col - WC // 2, 0, GRID - WC)
    win = (col[None, :] >= start[:, None]) & (col[None, :] < start[:, None] + WC)
    cap = np.where(win, f32(0.0), f32(BIG)).astype(f32)
    sel = np.zeros((5, 2 + 2 * P), f32)
    for r, (a, b) in enumerate([(1, 0), (0, 1), (1, 0), (0, 1), (1, 1)]):
        sel[r, 0], sel[r, 1] = a, b
        sel[r, 2:2 + P], sel[r, 2 + P:] = a, b
    return {"rope": rope, "cap": np.tile(cap, (2, 14)), "ident": np.eye(P, dtype=f32), "sel": sel}


def kernel(**inputs):
    import numpy as np
    import concourse.bacc as bacc
    from concourse.bass_utils import run_bass_kernel_spmd

    arrays = {**_layout(np, inputs), **_constants(np)}
    arrays = {k: np.ascontiguousarray(v) for k, v in arrays.items()}
    nc = bacc.Bacc("TRN2", target_bir_lowering=False, num_devices=1)
    ins = [nc.dram_tensor("in_" + n, arrays[n].shape, mybir.dt.float32, kind="ExternalInput").ap() for n in _NAMES]
    outs = [nc.dram_tensor("out_" + n, s, mybir.dt.float32, kind="ExternalOutput").ap() for n, s in _OUTS]
    build(nc, *ins, *outs)
    res = run_bass_kernel_spmd(nc, [{"in_" + n: arrays[n] for n in _NAMES}], core_ids=[0]).results[0]
    y = res["out_y"].reshape(T, D)
    return (y[LAT:].reshape(1, CTX, D), y[:LAT].reshape(1, LAT, D),
            res["out_s_k"].reshape(1, 1, CTX, NH, P), res["out_s_v"].reshape(1, 1, CTX, NH, P),
            res["out_s_ckv"].reshape(1, 1, CTX, LORA), res["out_s_kr"].reshape(1, 1, CTX, ROPE))
```

```python
import concourse.bass as bass
from concourse import mybir
from contextlib import ExitStack

P = 128
D = 2048
KD = D // P
LAT = 512
CTX = 128
T = LAT + CTX
TT = T // P
LT = LAT // P
HT = T // 2
NH = 8
GRID = 64
WR, WC = 8, 16
RPB = (2 * WR - 1) * (2 * WC - 1)
LORA = 512
KL = LORA // P
ROPE = 64
KEYS = LAT + CTX + CTX
FF = 5632
GT = 4
NG = FF // (GT * P)
ALPHA = 2.0 ** 0.25
LN_EPS = 1e-5
RMS_EPS = 1e-6
NA_SCALE = 128 ** -0.5
MLA_SCALE = 192 ** -0.5
BIG = -1.0e30

MOD_CHUNKS = 24
B_MOD = 0
B_V = B_MOD + 8 * 8
B_NA = B_V + 2 * 8
NA_PER = 4 * 5
B_KVL = B_NA + NH * NA_PER
B_QL = B_KVL + 8
B_KR = B_QL + 8
B_QR = B_KR + 1
B_VM = B_QR + 2
B_HEAD = B_VM + 4
B_WO = B_HEAD + NH
B_FF = B_WO + 4 * 8
FF_PER = GT * 4 + 4 * 2
N_BLOCKS = B_FF + NG * FF_PER
B_LAST = N_BLOCKS - 8

TOK_BANKS = [0, 1, 2, 3, 7]
UP_BANKS = [[0, 1, 2, 3], [5, 6, 7, 4]]
DOWN_BANKS = [0, 1, 2, 3, 4]
LAST_BANKS = UP_BANKS[0] + UP_BANKS[1]


class Chain:

    def __init__(self, engine, sem):
        self.engine, self.sem, self.n, self.i, self.per = engine, sem, 0, None, 0

    def link(self, ins):
        ins.then_inc(self.sem, 1)
        self.n += 1
        self.engine.wait_ge(self.sem, self.n if self.i is None else self.i * self.per + self.n)

    def enter(self, i, first, per):
        self.start, self.i, self.per, self.first = self.n, i, per, first
        self.n -= first * per

    def leave(self, trips):
        assert self.n + self.first * self.per == self.start + self.per, self.n + self.first * self.per - self.start
        self.n, self.i = self.start + trips * self.per, None


def at(i, per, c):
    return c if i is None else i * per + c


def build(nc, wstream, xT, xtok, cond, bmod, rpb, kcT, vc, ckvcT, krcT, lncol, lnrow, latg, bcol, rope, cap, ident, sel,
          y, s_k, s_v, s_ckv, s_kr):
    f32, f32r = mybir.dt.float32, mybir.dt.float32r
    ALU, ACT, AX = mybir.AluOpType, mybir.ActivationFunctionType, mybir.AxisListType

    modraw = nc.dram_tensor("modraw", (4, 6 * D), f32, kind="Internal").ap()
    PAD = GRID - WC
    rpbpad = nc.dram_tensor("rpbpad", (PAD + NH * RPB + PAD,), f32, kind="Internal").ap()
    tbl = nc.dram_tensor("tbl", (NH, P, 14 * GRID), f32, kind="Internal").ap()
    oscr = nc.dram_tensor("oscr", (2 * NH, P, T), f32, kind="Internal").ap()

    ctx = ExitStack()
    with ctx:
        def sb(name, shape, dt=f32, scope=ctx):
            return scope.enter_context(nc.sbuf_tensor(name, shape, dt))

        def sem(name):
            return ctx.enter_context(nc.semaphore(name))

        raw = sb("raw", [P, 4, 1024])
        whi = sb("whi", [P, 2, 1024], f32r)
        wlo = sb("wlo", [P, 2, 1024], f32r)
        acc = sb("acc", [P, TT * D])
        idt = sb("idt", [P, P])
        selt = sb("selt", [5, 2 + 2 * P])
        bcols = sb("bcols", [P, 2 * KD])
        lncols = sb("lncols", [P, 2, KD])
        ropet = sb("ropet", [P, 2, LT, ROPE])
        mod1 = sb("mod1", [P, 2 * KD, 2])
        mod2 = sb("mod2", [P, 2 * KD, 2])
        small = sb("small", [P, 64])
        stat = sb("stat", [P, TT, 4, 6])
        mv = sb("mv", [P, TT, 2])
        rstd = sb("rstd", [P, TT])
        norm = sb("norm", [P, TT, 2])

        att = ExitStack()
        modrow = sb("modrow", [4, 2, 512], f32, att)
        qT = sb("qT", [P, T], f32, att)
        kT = sb("kT", [P, KEYS], f32, att)
        vh = sb("vh", [P, 6, P], f32, att)
        pb = sb("pb", [P, 3, T], f32, att)
        PT = sb("PT", [P, 5, LAT], f32, att)
        PTc = sb("PTc", [P, P], f32, att)
        ost = sb("ost", [P, T], f32, att)
        kst = sb("kst", [P, P], f32, att)
        mx = sb("mx", [P, 3, 4], f32, att)
        rs = sb("rs", [P, 3, 4], f32, att)

        s0 = ExitStack()
        mraw = sb("mraw", [P, 8, 1024], f32, s0)
        mhi = sb("mhi", [P, 4, 1024], f32r, s0)
        mlo = sb("mlo", [P, 4, 1024], f32r, s0)
        s0.close()
        s1 = ExitStack()
        hh = sb("hh", [P, KD, T], f32r, s1)
        hl = sb("hl", [P, KD, T], f32r, s1)
        whi2 = sb("whi2", [P, 2, 1024], f32r, s1)
        wlo2 = sb("wlo2", [P, 2, 1024], f32r, s1)
        condw = sb("condw", [P, KD, 4], f32r, s1)
        condf = sb("condf", [P, KD, 2], f32, s1)
        conds = sb("conds", [P, 2, KD, 2], f32, s1)
        s1.close()

        s2 = ExitStack()
        ckvh = sb("ckvh", [P, KL, KEYS], f32r, s2)
        ckvl = sb("ckvl", [P, KL, KEYS], f32r, s2)
        qlh = sb("qlh", [P, KL, T], f32r, s2)
        qll = sb("qll", [P, KL, T], f32r, s2)
        qrT = sb("qrT", [ROPE, NH, T], f32, s2)
        krT = sb("krT", [ROPE, KEYS], f32, s2)
        ckvs = sb("ckvs", [P, KL, CTX], f32, s2)
        vm = sb("vm", [P, 6, NH * P], f32, s2)
        s2.close()
        att.close()

        s5 = ExitStack()
        lasth = sb("lasth", [P, 8, 1024], f32r, s5)
        lng = sb("lng", [P, D], f32, s5)
        lastl = sb("lastl", [P, 8, 1024], f32r, s5)
        lnb = sb("lnb", [P, D], f32, s5)
        s5.close()
        s3 = ExitStack()
        oh = sb("oh", [P, KD, T], f32r, s3)
        ol = sb("ol", [P, KD, T], f32r, s3)
        gate = sb("gate", [P, 2, D], f32, s3)
        tmp = sb("tmp", [P, 2, T], f32, s3)
        s3b = ExitStack()
        ostage = sb("ostage", [P, 3, T], f32, s3b)
        rows2 = sb("rows2", [5, D], f32, s3b)
        rows3 = sb("rows3", [5, D], f32, s3b)
        s3b.close()
        s3c = ExitStack()
        fh = sb("fh", [P, GT, T], f32r, s3c)
        fl = sb("fl", [P, GT, T], f32r, s3c)
        ex = sb("ex", [P, T], f32, s3c)
        gb = sb("gb", [P, 2, 512], f32, s3c)
        s3c.close()
        s3.close()

        xstage = acc[:, :].rearrange("p (k t) -> p k t", k=KD)
        vall = acc[:, 0:6 * NH * P].rearrange("p (k d) -> p k d", k=6)
        A1 = 6 * NH * P
        kct = acc[:, A1:A1 + NH * CTX].rearrange("p (h t) -> p h t", h=NH)
        A2 = A1 + NH * CTX
        TB = acc[:, A2:A2 + 14 * GRID]
        A3 = A2 + 14 * GRID
        capx = acc[:, A3:A3 + 14 * GRID]
        A4 = A3 + 14 * GRID
        latgt = acc[:, A4:A4 + 2 * LORA].rearrange("p (g c) -> p g c", g=2)
        assert A4 + 2 * LORA <= TT * D
        kvl = acc[:, 0:TT * LORA].rearrange("p (t c) -> p t c", t=TT)
        ql = acc[:, TT * LORA:2 * TT * LORA].rearrange("p (t c) -> p t c", t=TT)
        A5 = 2 * TT * LORA
        kr = acc[:, A5:A5 + TT * ROPE].rearrange("p (t c) -> p t c", t=TT)
        krr = acc[:, A5 + TT * ROPE:A5 + 2 * TT * ROPE].rearrange("p (t c) -> p t c", t=TT)
        assert A5 + 2 * TT * ROPE <= A1
        sq = acc[:, A1:A1 + LORA]
        qr = acc[:, A2:A2 + TT * LORA].rearrange("p (t c) -> p t c", t=TT)
        assert A2 + TT * LORA <= TT * D
        krf = pb[0:ROPE, 0, :]
        xs = acc[:, :].rearrange("p (t c) -> p t c", t=TT)

        ps = [ctx.enter_context(nc.psum_tensor(f"ps{i}", [P, 512], f32)) for i in range(8)]

        mod_loaded = [sem(f"mod_loaded{i}") for i in range(8)]
        loaded = [sem(f"loaded{i}") for i in range(4)]
        hi_ready = sem("hi_ready")
        lo_ready = sem("lo_ready")
        used = sem("used")
        act_own = sem("act_own")
        dve_own = sem("dve_own")
        consts_in = sem("consts_in")
        x_in = [sem(f"x_in{i}") for i in range(8)]
        pad_in = sem("pad_in")
        tbl_in = sem("tbl_in")
        cond_exp = sem("cond_exp")
        cond_ready = sem("cond_ready")
        modrow_ready = sem("modrow_ready")
        modrow_out = [sem("modrow_out0"), sem("modrow_out1")]
        mod1_psum = sem("mod1_psum")
        mod1_ready = sem("mod1_ready")
        h_scaled = sem("h_scaled")
        h_hi = sem("h_hi")
        h_ready = sem("h_ready")
        na_consts_in = sem("na_consts_in")
        tb_in = sem("tb_in")
        tb_ready = sem("tb_ready")
        v_done = sem("v_done")
        v_evac = sem("v_evac")
        sv_out = sem("sv_out")
        vh_ready = sem("vh_ready")
        q_done = sem("q_done")
        q_evac = sem("q_evac")
        k_evac = sem("k_evac")
        scores_ready = sem("scores_ready")
        ctx_scores = sem("ctx_scores")
        max_ready = sem("max_ready")
        exp_ready = sem("exp_ready")
        p_ready = sem("p_ready")
        pt_ready = sem("pt_ready")
        pt_free = sem("pt_free")
        kst_ready = sem("kst_ready")
        kst_out = sem("kst_out")
        pv_ready = sem("pv_ready")
        o_evac = sem("o_evac")
        o_out = sem("o_out")
        lat_done = sem("lat_done")
        lat_evac = sem("lat_evac")
        lat_rt = sem("lat_rt")
        kvl_ready = sem("kvl_ready")
        ql_ready = sem("ql_ready")
        krf_evac = sem("krf_evac")
        krf_turned = sem("krf_turned")
        kr_evac = sem("kr_evac")
        kr_ready = sem("kr_ready")
        skv_out = sem("skv_out")
        mla_in = sem("mla_in")
        tr_done = sem("tr_done")
        tr_hi = sem("tr_hi")
        tr_lo = sem("tr_lo")
        krt_evac = sem("krt_evac")
        qr_done = sem("qr_done")
        qr_evac = sem("qr_evac")
        qr_roped = sem("qr_roped")
        qrt_done = sem("qrt_done")
        qrt_evac = sem("qrt_evac")
        vm_done = sem("vm_done")
        vm_evac = sem("vm_evac")
        xs_in = sem("xs_in")
        o_in = [sem(f"o_in{i}") for i in range(3)]
        o_hi = sem("o_hi")
        o_lo = sem("o_lo")
        rows2_in = sem("rows2_in")
        rows3_in = sem("rows3_in")
        g_psum = sem("g_psum")
        g_evac = sem("g_evac")
        wo_done = sem("wo_done")
        wo_evac = sem("wo_evac")
        mod2_psum = sem("mod2_psum")
        mod2_ready = sem("mod2_ready")
        var_ready = sem("var_ready")
        sd_ready = sem("sd_ready")
        norm_ready = sem("norm_ready")
        xn_ready = sem("xn_ready")
        xt_ready = sem("xt_ready")
        h2_scaled = sem("h2_scaled")
        h2_hi = sem("h2_hi")
        h2_ready = sem("h2_ready")
        ln_in = sem("ln_in")
        lng_ready = sem("lng_ready")
        res_ready = sem("res_ready")
        gate_done = sem("gate_done")
        fexp = sem("fexp")
        gate_used = sem("gate_used")
        f_ready = sem("f_ready")
        f_hi = sem("f_hi")
        f_lo = sem("f_lo")
        down_done = sem("down_done")
        down_evac = sem("down_evac")
        last_done = sem("last_done")
        yg_ready = sem("yg_ready")
        lnb_in = sem("lnb_in")
        y_ready = sem("y_ready")
        yp_ready = sem("yp_ready")
        y_out = sem("y_out")

        def slots(n):
            return 4 if n < B_QR else 2

        def hi_of(n):
            if n >= B_LAST + 2:
                return lasth[:, n - B_LAST, :]
            return (whi2 if n % slots(n) >= 2 else whi)[:, n % 2, :]

        def lo_of(n):
            if n >= B_LAST + 2:
                return lastl[:, n - B_LAST, :]
            return (wlo2 if n % slots(n) >= 2 else wlo)[:, n % 2, :]

        MOD_BANKS = [7, 5]
        CONSTS = 6
        YG = [1024] * LT + [512]
        YP = [D] * LT + [512]

        def tile_done(engine, done, before, t, last, blocks):
            if t < last:
                engine.wait_ge(done, before + t + 1)
            else:
                engine.wait_ge(used, blocks)

        block = ctx.enter_context(nc.Block())

        @block.sync
        def _(sp):
            for n in range(8):
                sp.dma_start(mraw[:, n, :], wstream[n]).then_inc(mod_loaded[n], 16)
            with sp.Fori(1, B_V // 8) as i:
                for s in range(8):
                    sp.wait_ge(lo_ready, i * 8 + (s - 7))
                    sp.dma_start(mraw[:, s, :], wstream[i * 8 + s]).then_inc(mod_loaded[s], 16)
            for g in range(8):
                sp.dma_start(xstage[:, 2 * g:2 * g + 2, :], xT[:, 2 * g:2 * g + 2, :]).then_inc(x_in[g], 16)
                if g < 4:
                    sp.dma_start(raw[:, g, :], wstream[B_V + g]).then_inc(loaded[g], 16)
            with sp.Fori(B_V // 4 + 1, N_BLOCKS // 4) as i:
                for s in range(4):
                    sp.wait_ge(lo_ready, i * 4 + (s - 3))
                    sp.dma_start(raw[:, s, :], wstream[i * 4 + s]).then_inc(loaded[s], 16)
            for n in range(N_BLOCKS // 4 * 4, N_BLOCKS):
                sp.wait_ge(lo_ready, n - 3)
                sp.dma_start(raw[:, n % 4, :], wstream[n]).then_inc(loaded[n % 4], 16)

        @block.gpsimd
        def _(pool):
            def rows_in(dst, n_cols, col, done):
                pool.dma_start(dst[0:4, 0:n_cols], modraw[:, col:col + n_cols]).then_inc(done, 16)
                pool.dma_start(dst[4:5, 0:n_cols], bmod[:, col:col + n_cols]).then_inc(done, 16)

            def modrow_store(c, r):
                pool.wait_ge(modrow_ready, c + 1)
                pool.dma_start(modraw[:, bass.ds(c * 512, 512)], modrow[:, r, :]).then_inc(modrow_out[r], 16)

            for lo, n, src in ((0, PAD, 0), (PAD, NH * RPB, 0), (PAD + NH * RPB, PAD, 0)):
                pool.dma_start(rpbpad[lo:lo + n], rpb[src:src + n]).then_inc(pad_in, 16)
            pool.wait_ge(pad_in, 48)
            pool.wait_ge(mod1_psum, 8)
            for a in range(NH):
                for r in range(2):
                    src = bass.AP(tensor=rpbpad.tensor, offset=PAD + WC - 1 + a * RPB + (1 - r) * (2 * WC - 1),
                                  ap=[[2 * WC - 1, 14], [-1, GRID], [1, GRID]])
                    pool.dma_start(tbl[a, r * GRID:(r + 1) * GRID, :].rearrange("p (j k) -> j p k", j=14),
                                   src).then_inc(tbl_in, 16)

            pool.wait_ge(h_ready, KD)
            pool.dma_start(vall[:, LT, :], vc).then_inc(na_consts_in, 16)
            pool.dma_start(kct, kcT).then_inc(na_consts_in, 16)
            pool.dma_start(capx, cap).then_inc(na_consts_in, 16)
            for g in range(2):
                pool.dma_start(latgt[:, g, :], latg[g:g + 1, :].to_broadcast([P, LORA])).then_inc(na_consts_in, 16)
            pool.wait_ge(na_consts_in, 80)
            pool.wait_ge(tbl_in, 16 * 2 * NH)

            def bias_table(a):
                pool.dma_start(TB, tbl[a]).then_inc(tb_in, 16)
                pool.wait_ge(tb_in, a * 16 + 16)
                nc.gpsimd.tensor_tensor(TB, TB, capx, ALU.add).then_inc(tb_ready, 1)

            def v_of_head(a, src):
                nc.gpsimd.tensor_copy(vh[:, :, :], src[:, :, bass.ds(a * P, P)]).then_inc(vh_ready, 1)

            bias_table(0)
            pool.wait_ge(v_evac, 2 * TT)
            v_of_head(0, vall)
            pool.wait_ge(v_evac, 2 * TT)
            pool.dma_start(s_v, vall[:, LT + 1, :]).then_inc(sv_out, 16)

            def na_out(a):
                pool.wait_ge(kst_ready, a + 1)
                pool.dma_start(s_k[:, bass.ds(a * P, P)], kst[:, :]).then_inc(kst_out, 16)

            def head_out(a):
                pool.wait_ge(o_evac, a + 1)
                pool.dma_start(oscr[a], ost[:, :]).then_inc(o_out, 16)

            modrow_store(8, 0)
            modrow_store(9, 1)
            with pool.Fori(1, NH) as i:
                modrow_store(i * 2 + 8, 0)
                pool.wait_ge(max_ready, i * 5 - 1)
                bias_table(i)
                na_out(i - 1)
                modrow_store(i * 2 + 9, 1)
                head_out(i - 1)
                pool.wait_ge(kst_out, i * 16)
                pool.wait_ge(o_out, i * 16)
                v_of_head(i, vall)
            na_out(NH - 1)
            head_out(NH - 1)

            pool.wait_ge(kvl_ready, TT)
            pool.dma_start(s_ckv, kvl[:, LT, :]).then_inc(skv_out, 16)
            pool.wait_ge(used, B_QR)
            pool.dma_start(ckvs[:, :, :], ckvcT).then_inc(mla_in, 16)
            pool.dma_start(krT[:, LAT:LAT + CTX], krcT).then_inc(mla_in, 16)
            pool.wait_ge(kr_evac, 1)
            pool.dma_start(s_kr, kr[:, LT, :]).then_inc(skv_out, 16)

            pool.wait_ge(vm_evac, 12)
            pool.wait_ge(kst_out, 16 * NH)
            for a in range(NH):
                if a:
                    head_out(NH + a - 1)
                pool.wait_ge(pv_ready, NH + a)
                v_of_head(a, vm)
                if a == 0:
                    pool.wait_ge(qr_roped, TT)
                    pool.wait_ge(qrt_done, TT)
                    pool.wait_ge(skv_out, 32)
                    pool.dma_start(xs, xtok).then_inc(xs_in, 16)
            for r in range(2):
                pool.wait_ge(modrow_out[r], 16 * NH)
            pool.wait_ge(o_out, 16 * (2 * NH - 1))
            pool.wait_ge(vh_ready, 2 * NH)
            for k in range(KD):
                if k == 3:
                    head_out(2 * NH - 1)
                    pool.wait_ge(o_out, 16 * 2 * NH)
                if k >= 3:
                    pool.wait_ge(o_lo, k - 2)
                pool.dma_start(ostage[:, k % 3, :], oscr[k]).then_inc(o_in[k % 3], 16)
                if k == 3:
                    rows_in(rows2, D, 2 * D, rows2_in)
            rows_in(rows3, D, 3 * D, rows3_in)
            pool.wait_ge(g_psum, 4)
            rows_in(rows2, D, 4 * D, rows2_in)
            pool.wait_ge(mod2_psum, 1)
            rows_in(rows2, D, 5 * D, rows2_in)

            pool.wait_ge(h2_ready, KD)
            for c in range(4):
                if c:
                    pool.wait_ge(res_ready, c * TT)
                pool.dma_start(gb[:, :, :], lnrow[0:1, 0:2, c * 512:(c + 1) * 512].to_broadcast([P, 2, 512])
                               ).then_inc(ln_in, 16)
                pool.wait_ge(ln_in, 16 * (c + 1))
                nc.gpsimd.tensor_scalar(gb[:, :, :], gb[:, :, :], ALPHA, None, ALU.mult).then_inc(lng_ready, 1)
                pool.wait_ge(lng_ready, c * (TT + 1) + 1)
                for t in range(TT):
                    v = xs[:, t, c * 512:(c + 1) * 512]
                    nc.gpsimd.tensor_tensor(v, v, gb[:, 0, :], ALU.mult).then_inc(lng_ready, 1)
                    pool.wait_ge(lng_ready, c * (TT + 1) + 2 + t)
                    nc.gpsimd.tensor_tensor(v, v, gb[:, 1, :], ALU.add).then_inc(res_ready, 1)

            pool.wait_ge(used, B_LAST)
            for g, dst in ((2, lng), (3, lnb)):
                pool.dma_start(dst[:, :], lnrow[0:1, g, :].to_broadcast([P, D])).then_inc(lnb_in, 16)
            pool.wait_ge(lnb_in, 32)
            for t in range(TT):
                pool.wait_ge(xn_ready, TT + t + 1)
                v = xs[:, t, 0:YG[t]]
                nc.gpsimd.tensor_tensor(v, v, lng[:, 0:YG[t]], ALU.mult).then_inc(yp_ready, 1)
                pool.wait_ge(yg_ready, t + 1)
                pool.wait_ge(yp_ready, 2 * t + 1)
                nc.gpsimd.tensor_tensor(xs[:, t, 0:YP[t]], xs[:, t, 0:YP[t]], lnb[:, 0:YP[t]], ALU.add).then_inc(yp_ready, 1)
                pool.wait_ge(yp_ready, 2 * t + 2)
                if YP[t] < D:
                    pool.wait_ge(y_ready, 1)
                pool.dma_start(y[t], xs[:, t, :]).then_inc(y_out, 16)
            pool.wait_ge(sv_out, 16)
            pool.wait_ge(kst_out, 16 * NH)
            pool.wait_ge(skv_out, 32)
            pool.wait_ge(y_out, 16 * TT)

        @block.scalar
        def _(act):
            own = Chain(act, act_own)

            for dst, src in ((idt[:, :], ident), (selt[:, :], sel), (condf[:, :, :], cond), (lncols[:, :, :], lncol),
                             (ropet[:, :, :, :], rope), (bcols[:, :], bcol)):
                act.dma_start(dst, src).then_inc(consts_in, 16)
            def split(i, per, n):
                if i is None and n >= N_BLOCKS:
                    return
                act.wait_ge(loaded[n % 4], at(i, per // 4 * 16, 16 * ((n - B_V) // 4 + 1)))
                if i is not None or n >= B_V + 4:
                    act.wait_ge(used, at(i, per, n - 3 if n < B_QR else B_QR if n < B_QR + 2 else min(n - 1, B_LAST)))
                nc.scalar.activation(hi_of(n), raw[:, n % 4, :], ACT.Copy).then_inc(hi_ready, 1)

            act.wait_ge(consts_in, 16 * CONSTS)
            nc.scalar.activation(conds[:, 0], condf[:, :, :], ACT.Exp, scale=-1.0).then_inc(cond_exp, 1)

            def mod_split(i, n):
                act.wait_ge(mod_loaded[n % 8], at(i, 32, 16 * (n // 8 + 1)))
                if i is not None or n >= 4:
                    act.wait_ge(used, at(i, 16, n - 3))
                nc.scalar.activation(mhi[:, n % 4, :], mraw[:, n % 8, :], ACT.Copy).then_inc(hi_ready, 1)

            def mod_pair(i, p):
                for b in range(16):
                    c = 2 * p + b // 8
                    if b % 8 == 7:
                        act.wait_ge(used, at(i, 16, 8 * c + 8))
                        if i is not None or c >= 2:
                            act.wait_ge(mod1_psum, at(i, 2, c - 1))
                        nc.scalar.activation(modrow[:, b // 8, :], ps[MOD_BANKS[b // 8]][0:4, :],
                                             ACT.Copy).then_inc(modrow_ready, 1)
                    n = 16 * p + b + 4
                    if i is not None or n < B_V:
                        mod_split(i, n)

            for n in range(4):
                mod_split(None, n)
            mod_pair(None, 0)
            with act.Fori(1, 3) as i:
                mod_pair(i, 0)
            mod_pair(None, 3)
            split(None, 0, B_V)

            def h_part(k):
                act.wait_ge(h_scaled, k + 1)
                nc.scalar.activation(hh[:, k, :], xstage[:, k, :], ACT.Copy).then_inc(h_hi, 1)

            for b in range(16):
                if b < 6:
                    for k in (range(6) if b == 0 else range(2 * b + 4, 2 * b + 6)):
                        h_part(k)
                        if b == 0 and 0 < k < 4:
                            split(None, 0, B_V + k)
                if b % 8 == 7:
                    c = b // 8
                    for t, bank in enumerate(TOK_BANKS):
                        tile_done(act, v_done, c * LT, t, LT, B_V + 8 * c + 8)
                        if c == 0 and t == 0:
                            act.wait_ge(h_ready, KD)
                        dst = t if t < LT else LT + 1
                        nc.scalar.activation(vall[:, dst, c * 512:(c + 1) * 512], ps[bank][:, :],
                                             ACT.Copy).then_inc(v_evac, 1)
                split(None, 0, B_V + b + 4)

            def stage(i, a, s, na, parts=(0, 1)):
                A = lambda c: at(i, 5, 5 * a + c)
                if s < 5 and 0 in parts:
                    act.wait_ge(scores_ready, A(s + 1))
                    if na and s < LT:
                        nc.scalar.activation(pb[:, s % 3, LAT:T], ps[5][:, 0:CTX], ACT.Copy,
                                             scale=NA_SCALE).then_inc(ctx_scores, 1)
                if 2 <= s < 7 and 0 in parts:
                    t = s - 2
                    act.wait_ge(pt_ready, A(t + 1))
                    if t == 0 and na:
                        act.wait_ge(vh_ready, (a + 1) if i is None else i + a + 1)
                    if t < LT:
                        nc.scalar.activation(PT[:, 0:4, t * P:(t + 1) * P],
                                             ps[6][:, :].rearrange("p (k q) -> p k q", k=4), ACT.Copy)
                        if na and t == 3:
                            nc.scalar.activation(kst[:, :], ps[5][:, 2 * P:3 * P], ACT.Copy).then_inc(kst_ready, 1)
                        last = ps[5][:, P:2 * P] if na else ps[7][:, 0:P]
                        nc.scalar.activation(PT[:, 4, t * P:(t + 1) * P], last, ACT.Copy).then_inc(pt_free, 1)
                    else:
                        nc.scalar.activation(PTc[:, :], ps[6][:, 0:P], ACT.Copy).then_inc(pt_free, 1)
                if s < 5 and 1 in parts:
                    act.wait_ge(max_ready, A(s + 1))
                    nb = mx[:, s % 3, 3:4]
                    if na and s < LT:
                        nc.scalar.activation(pb[:, s % 3, :], pb[:, s % 3, :], ACT.Exp, bias=nb, scale=1.0,
                                             accum_out=rs[:, s % 3, 2:3]).then_inc(exp_ready, 1)
                    elif s < LT:
                        bk = 4 if s % 2 == 0 else 0
                        nc.scalar.activation(pb[:, s % 3, 0:LAT], ps[bk][:, :], ACT.Exp, bias=nb, scale=MLA_SCALE,
                                             accum_out=rs[:, s % 3, 0:1])
                        nc.scalar.activation(pb[:, s % 3, LAT:T], ps[bk + 1][:, 0:CTX], ACT.Exp, bias=nb,
                                             scale=MLA_SCALE, accum_out=rs[:, s % 3, 1:2]).then_inc(exp_ready, 1)
                    else:
                        nc.scalar.activation(pb[:, s % 3, 0:CTX], ps[4][:, 0:CTX], ACT.Exp, bias=nb,
                                             scale=NA_SCALE if na else MLA_SCALE,
                                             accum_out=rs[:, s % 3, 2:3]).then_inc(exp_ready, 1)
                if s == 7 and 1 in parts:
                    act.wait_ge(pv_ready, (a + 1) if i is None else i + a + 1)
                    if not na:
                        act.wait_ge(o_out, 16 * a)
                    bk = 4 if na else 6
                    nc.scalar.activation(ost[:, 0:LAT], ps[bk][:, :], ACT.Copy)
                    nc.scalar.activation(ost[:, LAT:T], ps[bk + 1][:, 0:CTX], ACT.Copy).then_inc(o_evac, 1)

            def q_copy(blocks):
                act.wait_ge(used, blocks)
                nc.scalar.activation(qT[:, 0:HT], ps[0][:, 0:HT], ACT.Copy)
                nc.scalar.activation(qT[:, HT:T], ps[1][:, 0:HT], ACT.Copy).then_inc(q_evac, 1)

            def na_iter(i, stages):
                for b in range(NA_PER):
                    g, r = divmod(b, 5)
                    if b in (9, 19):
                        act.wait_ge(used, at(i, NA_PER, B_NA + b + 1))
                        row = 0 if b == 9 else 1
                        if i is None:
                            act.wait_ge(mod1_psum, 8)
                        else:
                            act.wait_ge(modrow_out[row], i * 16)
                        nc.scalar.activation(modrow[:, row, :], ps[7][0:4, :], ACT.Copy).then_inc(modrow_ready, 1)
                    if b == 15:
                        q_copy(at(i, NA_PER, B_NA + b + 1))
                    if stages and b == NA_PER - 1:
                        stage(i, -1, 7, True)
                    split(i, NA_PER, B_NA + b + 4)
                    if stages and r in (1, 2):
                        stage(i, -1, 2 * g, True, (r - 1,))
                    elif stages and r == 4 and b < NA_PER - 1:
                        stage(i, -1, 2 * g + 1, True)

            na_iter(None, False)
            with act.Fori(1, NH) as i:
                na_iter(i, True)

            def copy_chunk(dst, c):
                for t, bank in enumerate(TOK_BANKS):
                    tile_done(act, lat_done, c * LT, t, LT, B_KVL + 8 * c + 8)
                    if c == 0 and t == 0:
                        act.wait_ge(vh_ready, NH)
                        act.wait_ge(sv_out, 16)
                    nc.scalar.activation(dst[:, t, :], ps[bank][:, :], ACT.Copy).then_inc(lat_evac, 1)

            def norm_chunk(dst, c):
                for t in range(TT):
                    if t == 0:
                        act.wait_ge(lat_evac, c * TT + TT)
                    own.link(nc.scalar.activation(sq, dst[:, t, :], ACT.Square, accum_out=small[:, t:t + 1]))
                if c:
                    act.wait_ge(kvl_ready, 1)
                nc.scalar.activation(small[:, 8:8 + TT], small[:, 0:TT], ACT.Sqrt, scale=1.0 / LORA,
                                     bias=RMS_EPS).then_inc(lat_rt, 1)

            for b in range(17):
                if b == 7:
                    copy_chunk(kvl, 0)
                if b == 15:
                    copy_chunk(ql, 1)
                if b == 16:
                    norm_chunk(ql, 1)
                    act.wait_ge(used, B_KR + 1)
                    for half in range(2):
                        ins = nc.scalar.activation(krf[:, half * HT:(half + 1) * HT], ps[half][0:ROPE, 0:HT], ACT.Copy)
                    ins.then_inc(krf_evac, 1)
                    act.wait_ge(krf_turned, 1)
                    nc.scalar.activation(kr, ps[4][:, 0:TT * ROPE].rearrange("p (t c) -> p t c", t=TT),
                                         ACT.Copy).then_inc(kr_evac, 1)
                if B_KVL + b + 4 < B_QR:
                    split(None, 0, B_KVL + b + 4)
                if b < 8:
                    stage(None, NH - 1, b, True)
                if b == 8:
                    norm_chunk(kvl, 0)

            split(None, 0, B_QR)
            split(None, 0, B_QR + 1)

            for j in range(2 * TT):
                t = j % TT
                act.wait_ge(tr_done, j + 1)
                src = ps[j % 4][:, :].rearrange("p (k q) -> p k q", k=KL)
                if j < TT:
                    o = t if t < LT else LT + 1
                    dst = ckvh[:, :, o * P:(o + 1) * P]
                else:
                    dst = qlh[:, :, t * P:(t + 1) * P]
                nc.scalar.activation(dst, src, ACT.Copy).then_inc(tr_hi, 1)
            act.wait_ge(mla_in, 32)
            nc.scalar.activation(ckvh[:, :, LAT:LAT + CTX], ckvs[:, :, :], ACT.Copy).then_inc(tr_hi, 1)
            split(None, 0, B_QR + 2)
            for t, bank in enumerate(TOK_BANKS):
                tile_done(act, qr_done, 0, t, LT, B_QR + 2)
                if t == 0:
                    act.wait_ge(tr_lo, 2 * TT)
                nc.scalar.activation(ql[:, t, :], ps[bank][:, :], ACT.Copy).then_inc(qr_evac, 1)
            split(None, 0, B_QR + 3)
            act.wait_ge(tr_done, 2 * TT + 1)
            nc.scalar.activation(krT[:, 0:LAT], ps[4][0:ROPE, :], ACT.Copy)
            nc.scalar.activation(krT[:, LAT + CTX:KEYS], ps[5][0:ROPE, 0:CTX], ACT.Copy).then_inc(krt_evac, 1)
            for c in range(2):
                split(None, 0, B_VM + 2 * c + 2)
                for t, bank in enumerate(TOK_BANKS + [4]):
                    tile_done(act, vm_done, c * 5, t, 5, B_VM + 2 * c + 2)
                    nc.scalar.activation(vm[:, t, c * 512:(c + 1) * 512], ps[bank][:, :], ACT.Copy).then_inc(vm_evac, 1)
                split(None, 0, B_VM + 2 * c + 3)
                if c == 0:
                    for t in range(TT):
                        act.wait_ge(qrt_done, t + 1)
                        for half in range(2):
                            ins = nc.scalar.activation(qrT[:, 4 * half:4 * half + 4, t * P:(t + 1) * P],
                                                       ps[5 + half][0:ROPE, :].rearrange("p (h q) -> p h q", h=4), ACT.Copy)
                        ins.then_inc(qrt_evac, 1)

            def o_part(k):
                act.wait_ge(o_in[k % 3], 16 * (k // 3 + 1))
                nc.scalar.activation(oh[:, k, :], ostage[:, k % 3, :], ACT.Copy).then_inc(o_hi, 1)

            for h in range(NH + 1):
                last, cur, more = NH + h - 1, NH + h, h < NH
                if more:
                    act.wait_ge(q_done, h + 1)
                    nc.scalar.activation(qT[:, 0:HT], ps[2][:, 0:HT], ACT.Copy)
                    nc.scalar.activation(qT[:, HT:T], ps[3][:, 0:HT], ACT.Copy)
                    act.wait_ge(used, B_HEAD + h + 1)
                    nc.scalar.activation(kT[:, KEYS // 2:KEYS], ps[1][:, 0:KEYS // 2], ACT.Copy).then_inc(q_evac, 1)
                if h:
                    stage(None, last, 5, False)
                    stage(None, last, 6, False)
                if more:
                    stage(None, cur, 0, False)
                    split(None, 0, B_HEAD + h + 2)
                    stage(None, cur, 1, False)
                else:
                    for k in range(3):
                        o_part(k)
                if h:
                    stage(None, last, 7, False)
                if more:
                    for s in range(2, 4):
                        stage(None, cur, s, False)
                    stage(None, cur, 4, False, (1,))
                    stage(None, cur, 4, False, (0,))

            def normalise(n):
                t = n % TT
                act.wait_ge(var_ready, n + 1)
                nc.scalar.activation(rstd[:, t:t + 1], mv[:, t, 1:2], ACT.Sqrt, bias=LN_EPS,
                                     scale=1.0).then_inc(sd_ready, 1)
                if n in (3, 4):
                    return
                act.wait_ge(norm_ready, n + 1)
                nc.scalar.activation(xs[:, t, :], xs[:, t, :], ACT.Identity, scale=norm[:, t, 0:1],
                                     bias=norm[:, t, 1:2]).then_inc(xn_ready, 1)

            def gate_copy(q, second=False):
                act.wait_ge(g_psum, q + 1 + 4 * second)
                if second:
                    act.wait_ge(wo_evac, (q + 1) * TT)
                for c in range(2):
                    nc.scalar.activation(gate[:, c, q * 512:(q + 1) * 512], ps[4 + c][:, :], ACT.Copy).then_inc(g_evac, 1)

            for b in range(32):
                if b < 7:
                    for k in ((3,) if b == 0 else range(2 * b + 2, 2 * b + 4)):
                        o_part(k)
                if b == 6:
                    gate_copy(0)
                if b in (8, 10, 12):
                    gate_copy(b // 2 - 3)
                if b in (27, 29, 31):
                    gate_copy((b - 27) // 2, True)
                if b == 31:
                    for t in range(TT):
                        normalise(t)
                else:
                    split(None, 0, B_WO + b + 2)

            act.wait_ge(mod2_ready, 1)

            def h2_part(k):
                r = k % 2
                act.wait_ge(xt_ready, k + 1)
                if k >= 2:
                    act.wait_ge(h2_ready, k - 1)
                nc.scalar.activation(tmp[:, r, 0:LAT], ps[6 - 2 * r][:, :], ACT.Identity,
                                     scale=mod2[:, KD + k, 0:1], bias=mod2[:, k, 0:1])
                nc.scalar.activation(tmp[:, r, LAT:T], ps[7 - 2 * r][:, 0:CTX], ACT.Identity,
                                     scale=mod2[:, KD + k, 1:2], bias=mod2[:, k, 1:2]).then_inc(h2_scaled, 1)

            for k in range(4):
                h2_part(k)
                if k == 0:
                    gate_copy(3, True)
            split(None, 0, B_FF + 1)

            def ff_group(i, g0):
                for b in range(16 if g0 == NG - 1 else FF_PER):
                    if b < 16:
                        j, q = divmod(b, 4)
                        if i is None and g0 == 0 and b < 3:
                            for k in range(4 * b + 4, 4 * b + 8):
                                h2_part(k)
                        if q == 3:
                            act.wait_ge(gate_done, at(i, GT, GT * g0 + j + 1))
                            nc.scalar.activation(ex[:, 0:HT], ps[UP_BANKS[j % 2][0]][:, 0:HT], ACT.Exp, scale=-1.0)
                            nc.scalar.activation(ex[:, HT:T], ps[UP_BANKS[j % 2][1]][:, 0:HT], ACT.Exp,
                                                 scale=-1.0).then_inc(fexp, 1)
                        split(i, FF_PER, B_FF + FF_PER * g0 + b + 2)
                        if q == 3:
                            act.wait_ge(f_ready, at(i, GT, GT * g0 + j + 1))
                            nc.scalar.activation(fh[:, j, :], tmp[:, 0, :], ACT.Copy).then_inc(f_hi, 1)
                    else:
                        split(i, FF_PER, B_FF + FF_PER * g0 + b + 2)

            ff_group(None, 0)
            with act.Fori(1, NG - 1) as i:
                ff_group(i, 0)
            ff_group(None, NG - 1)

            for n in range(B_LAST + 2, N_BLOCKS):
                split(None, 0, n)

            for t in range(TT):
                normalise(TT + t)

        @block.vector
        def _(dve):
            V = nc.vector
            own = Chain(dve, dve_own)

            def split(i, per, n):
                if i is None and n >= N_BLOCKS:
                    return
                dve.wait_ge(hi_ready, at(i, per, n + 1))
                V.tensor_tensor(lo_of(n), raw[:, n % 4, :], hi_of(n).bitcast(f32),
                                ALU.subtract).then_inc(lo_ready, 1)

            dve.wait_ge(consts_in, 16 * CONSTS)
            dve.wait_ge(cond_exp, 1)
            own.link(V.tensor_scalar(conds[:, 0], conds[:, 0], 1.0, None, ALU.add))
            own.link(V.reciprocal(conds[:, 0], conds[:, 0]))
            own.link(V.tensor_tensor(conds[:, 1], conds[:, 0], condf[:, :, :], ALU.mult))
            own.link(V.tensor_copy(condw[:, :, 0:2], conds[:, 1]))
            V.tensor_tensor(condw[:, :, 2:4], conds[:, 1], condw[:, :, 0:2].bitcast(f32),
                            ALU.subtract).then_inc(cond_ready, 1)

            def mod_split(i, n):
                dve.wait_ge(hi_ready, at(i, 16, n + 1))
                V.tensor_tensor(mlo[:, n % 4, :], mraw[:, n % 8, :], mhi[:, n % 4, :].bitcast(f32),
                                ALU.subtract).then_inc(lo_ready, 1)

            for n in range(16):
                mod_split(None, n)
            with dve.Fori(1, 4) as i:
                for n in range(16):
                    mod_split(i, n)
            split(None, 0, B_V)

            def mod_cols(dst, psum):
                V.tensor_copy(dst[:, 0:KD, :], psum[:, 0:2 * KD].rearrange("p (k c) -> p k c", c=2))
                own.link(V.tensor_scalar(dst[:, KD:2 * KD, :], psum[:, 2 * KD:4 * KD].rearrange("p (k c) -> p k c", c=2),
                                         1.0, None, ALU.add))

            dve.wait_ge(mod1_psum, 8)
            psum1 = ps[6][:, 0:4 * KD].rearrange("p (k c) -> p k c", c=2)
            bc = bcols[:, :].unsqueeze(2).to_broadcast([P, 2 * KD, 2])
            V.tensor_tensor(mod1[:, 0:KD, :], psum1[:, 0:KD, :], bc[:, 0:KD, :], ALU.add)
            own.link(V.scalar_tensor_tensor(out=mod1[:, KD:2 * KD, :], in0=psum1[:, KD:2 * KD, :], scalar=1.0,
                                            in1=bc[:, KD:2 * KD, :], op0=ALU.add, op1=ALU.add))

            def h_part(k):
                dve.wait_ge(x_in[k // 2], 16)
                for lo, hi, c in ((0, LAT, 0), (LAT, T, 1)):
                    ins = V.tensor_scalar(xstage[:, k, lo:hi], xstage[:, k, lo:hi], mod1[:, KD + k, c:c + 1],
                                          mod1[:, k, c:c + 1], ALU.mult, ALU.add)
                ins.then_inc(h_scaled, 1)

            def h_rest(k):
                dve.wait_ge(h_hi, k + 1)
                V.tensor_tensor(hl[:, k, :], xstage[:, k, :], hh[:, k, :].bitcast(f32), ALU.subtract).then_inc(h_ready, 1)

            for b in range(16):
                if b < 6:
                    ks = list(range(6) if b == 0 else range(2 * b + 4, 2 * b + 6))
                    if b == 0:
                        h_part(0)
                    for k in ks:
                        if k + 1 < KD:
                            h_part(k + 1)
                        h_rest(k)
                        if b == 0 and 0 < k < 4:
                            split(None, 0, B_V + k)
                split(None, 0, B_V + b + 4)

            def stage(i, a, s, na, parts=(0, 1)):
                A = lambda c: at(i, 5, 5 * a + c)
                if s < 5 and 0 in parts:
                    r = s % 3
                    dve.wait_ge(scores_ready, A(s + 1))
                    if na and s < LT:
                        if s == 0:
                            dve.wait_ge(tb_ready, (a + 1) if i is None else i + a + 1)
                        own.link(V.scalar_tensor_tensor(out=pb[:, r, 0:LAT], in0=ps[4][:, :], scalar=NA_SCALE,
                                                        in1=TB[:, (6 - 2 * s) * GRID:(14 - 2 * s) * GRID],
                                                        op0=ALU.mult, op1=ALU.add))
                        dve.wait_ge(ctx_scores, (4 * a + s + 1) if i is None else i * 4 + 4 * a + s + 1)
                        own.link(V.reduce_max(mx[:, r, 2:3], pb[:, r, :], AX.X))
                        scale = -1.0
                    elif s < LT:
                        bk = 4 if s % 2 == 0 else 0
                        V.reduce_max(mx[:, r, 0:1], ps[bk][:, :], AX.X)
                        own.link(V.reduce_max(mx[:, r, 1:2], ps[bk + 1][:, 0:CTX], AX.X))
                        own.link(V.tensor_tensor(mx[:, r, 2:3], mx[:, r, 0:1], mx[:, r, 1:2], ALU.max))
                        scale = -MLA_SCALE
                    else:
                        own.link(V.reduce_max(mx[:, r, 2:3], ps[4][:, 0:CTX], AX.X))
                        scale = -(NA_SCALE if na else MLA_SCALE)
                    V.tensor_scalar(mx[:, r, 3:4], mx[:, r, 2:3], scale, None, ALU.mult).then_inc(max_ready, 1)
                if 1 <= s < 6 and 1 in parts:
                    t = s - 1
                    r = t % 3
                    dve.wait_ge(exp_ready, A(t + 1))
                    if not na and t < LT:
                        own.link(V.tensor_tensor(rs[:, r, 2:3], rs[:, r, 0:1], rs[:, r, 1:2], ALU.add))
                    own.link(V.reciprocal(rs[:, r, 3:4], rs[:, r, 2:3]))
                    n = T if t < LT else CTX
                    V.tensor_scalar(pb[:, r, 0:n], pb[:, r, 0:n], rs[:, r, 3:4], None, ALU.mult).then_inc(p_ready, 1)

            def k_copy(blocks, n):
                dve.wait_ge(used, blocks)
                V.tensor_copy(kT[:, 0:n], ps[2][:, 0:n])
                V.tensor_copy(kT[:, n:2 * n], ps[3][:, 0:n]).then_inc(k_evac, 1)

            def na_iter(i, stages):
                for b in range(NA_PER):
                    g, r = divmod(b, 5)
                    if b == 15:
                        k_copy(at(i, NA_PER, B_NA + b + 1), HT)
                    split(i, NA_PER, B_NA + b + 4)
                    if stages and r in (1, 4):
                        stage(i, -1, 2 * g + (r == 4), True, (0,))
                    if stages and r in (0, 3):
                        stage(i, -1, 2 * g + (r == 3), True, (1,))

            na_iter(None, False)
            with dve.Fori(1, NH) as i:
                own.enter(i, 1, 14)
                na_iter(i, True)
                own.leave(NH - 1)

            def norm_chunk(dst, c, done):
                dve.wait_ge(lat_rt, c + 1)
                own.link(V.reciprocal(small[:, 16:16 + TT], small[:, 8:8 + TT]))
                for t in range(TT):
                    V.scalar_tensor_tensor(out=dst[:, t, :], in0=dst[:, t, :], scalar=small[:, 16 + t:17 + t],
                                           in1=latgt[:, 1 - c, :], op0=ALU.mult, op1=ALU.mult).then_inc(done, 1)

            def rotate(dst, src, tmp_, t, nh):
                cos = ropet[:, 0, t, :]
                sin = ropet[:, 1, t, :]
                v = lambda x: x.rearrange("p (h q u j) -> p h q u j", h=nh, q=2, u=2)
                sn = sin.rearrange("p (q u j) -> p q u j", q=2, u=2)
                for q in range(2):
                    for u in range(2):
                        ins = V.tensor_tensor(v(tmp_)[:, :, q, u, :], v(src)[:, :, q, 1 - u, :],
                                              sn[:, q, u, :].unsqueeze(1).to_broadcast([P, nh, 16]), ALU.mult)
                own.link(ins)
                own.link(V.tensor_tensor(dst.rearrange("p (h c) -> p h c", h=nh), src.rearrange("p (h c) -> p h c", h=nh),
                                         cos.unsqueeze(1).to_broadcast([P, nh, ROPE]), ALU.mult))
                return V.tensor_tensor(dst, dst, tmp_, ALU.add)

            for b in range(17):
                if B_KVL + b + 4 < B_QR:
                    split(None, 0, B_KVL + b + 4)
                if b < 8:
                    stage(None, NH - 1, b, True)
                if b == 9:
                    norm_chunk(kvl, 0, kvl_ready)
            norm_chunk(ql, 1, ql_ready)
            split(None, 0, B_QR)
            split(None, 0, B_QR + 1)
            for j in range(2 * TT):
                t = j % TT
                dve.wait_ge(tr_hi, j + 1)
                src = ps[j % 4][:, :].rearrange("p (k q) -> p k q", k=KL)
                if j < TT:
                    o = t if t < LT else LT + 1
                    h_, l_ = ckvh[:, :, o * P:(o + 1) * P], ckvl[:, :, o * P:(o + 1) * P]
                else:
                    h_, l_ = qlh[:, :, t * P:(t + 1) * P], qll[:, :, t * P:(t + 1) * P]
                V.tensor_tensor(l_, src, h_.bitcast(f32), ALU.subtract).then_inc(tr_lo, 1)
            dve.wait_ge(kr_evac, 1)
            for t in range(LT):
                own.link(rotate(krr[:, t, :], kr[:, t, :], krr[:, LT, :], t, 1))
            V.tensor_copy(krr[:, LT, :], kr[:, LT, :]).then_inc(kr_ready, 1)
            dve.wait_ge(tr_hi, 2 * TT + 1)
            V.tensor_tensor(ckvl[:, :, LAT:LAT + CTX], ckvs[:, :, :], ckvh[:, :, LAT:LAT + CTX].bitcast(f32),
                            ALU.subtract).then_inc(tr_lo, 1)
            split(None, 0, B_QR + 2)
            for t in range(TT):
                dve.wait_ge(qr_evac, t + 1)
                if t < LT:
                    if t:
                        dve.wait_ge(qr_roped, t)
                    rotate(qr[:, t, :], ql[:, t, :], sq, t, NH).then_inc(qr_roped, 1)
                else:
                    V.tensor_copy(qr[:, t, :], ql[:, t, :]).then_inc(qr_roped, 1)
                if t in (0, 1, 3):
                    split(None, 0, B_VM + 1 + (t + 1) // 2)
            for n in range(B_VM + 4, B_VM + 6):
                split(None, 0, n)

            for h in range(NH + 1):
                if h:
                    stage(None, NH + h - 1, 5, False)
                if h < NH:
                    dve.wait_ge(used, B_HEAD + h + 1)
                    V.tensor_copy(kT[:, 0:KEYS // 2], ps[0][:, 0:KEYS // 2]).then_inc(k_evac, 1)
                    for s in range(5):
                        stage(None, NH + h, s, False)
                        if s == 1:
                            split(None, 0, B_HEAD + h + 2)

            def o_part(k):
                dve.wait_ge(o_hi, k + 1)
                V.tensor_tensor(ol[:, k, :], ostage[:, k % 3, :], oh[:, k, :].bitcast(f32), ALU.subtract).then_inc(o_lo, 1)

            def stats(t):
                V.bn_aggr(mv[:, t, :], stat[:, t, :, :].rearrange("p c s -> p (c s)")).then_inc(var_ready, 1)

            def scales(n):
                t = n % TT
                dve.wait_ge(sd_ready, n + 1)
                own.link(V.reciprocal(norm[:, t, 0:1], rstd[:, t:t + 1]))
                V.tensor_scalar(norm[:, t, 1:2], mv[:, t, 0:1], norm[:, t, 0:1], -1.0, ALU.mult,
                                ALU.mult).then_inc(norm_ready, 1)

            def centre(t):
                dve.wait_ge(norm_ready, t + 1)
                V.tensor_scalar(xs[:, t, :], xs[:, t, :], norm[:, t, 0:1], norm[:, t, 1:2], ALU.mult,
                                ALU.add).then_inc(xn_ready, 1)

            def mod2_parts():
                dve.wait_ge(mod2_psum, 1)
                mod_cols(mod2, ps[6])
                bsc = small[:, 32:64].rearrange("p (k c) -> p k c", c=2)
                lb = lncols[:, 1, :].unsqueeze(2).to_broadcast([P, KD, 2])
                lg = lncols[:, 0, :].unsqueeze(2).to_broadcast([P, KD, 2])
                own.link(V.tensor_tensor(bsc, mod2[:, KD:2 * KD, :], lb, ALU.mult))
                own.link(V.tensor_tensor(mod2[:, 0:KD, :], mod2[:, 0:KD, :], bsc, ALU.add))
                V.tensor_tensor(mod2[:, KD:2 * KD, :], mod2[:, KD:2 * KD, :], lg, ALU.mult).then_inc(mod2_ready, 1)

            for b in range(32):
                if b < 7:
                    for k in (range(4) if b == 0 else range(2 * b + 2, 2 * b + 4)):
                        o_part(k)
                if b % 8 == 7:
                    c = b // 8
                    cols = slice(c * 512, (c + 1) * 512)
                    if c == 0:
                        dve.wait_ge(xs_in, 16)
                    if c == 0:
                        dve.wait_ge(g_evac, 2)
                    else:
                        dve.wait_ge(g_evac, 8)
                    for t, bank in enumerate(TOK_BANKS):
                        tile_done(dve, wo_done, c * LT, t, LT, B_WO + 8 * c + 8)
                        V.tensor_tensor(tmp[:, t % 2, 0:512], ps[bank][:, :], gate[:, t // LT, cols],
                                        ALU.mult).then_inc(wo_evac, 1)
                        dve.wait_ge(wo_evac, c * TT + t + 1)
                        own.link(V.scalar_tensor_tensor(out=xs[:, t, cols], in0=xs[:, t, cols], scalar=ALPHA,
                                                        in1=tmp[:, t % 2, 0:512], op0=ALU.mult, op1=ALU.add))
                        own.link(V.bn_stats(stat[:, t, c, :], xs[:, t, cols]))
                        if c == 3:
                            stats(t)
                            if t:
                                scales(t - 1)
                            if t == LT:
                                centre(3)
                                scales(t)
                                centre(4)
                if b < 31:
                    split(None, 0, B_WO + b + 2)
                if b == 24:
                    mod2_parts()

            def h2_part(k):
                r = k % 2
                dve.wait_ge(h2_scaled, k + 1)
                V.tensor_copy(oh[:, k, :], tmp[:, r, :]).then_inc(h2_hi, 1)
                dve.wait_ge(h2_hi, k + 1)
                V.tensor_tensor(ol[:, k, :], tmp[:, r, :], oh[:, k, :].bitcast(f32), ALU.subtract).then_inc(h2_ready, 1)

            for k in range(4):
                h2_part(k)
            split(None, 0, B_FF + 1)

            def ff_group(i, g0, last=False):
                for b in range(16 if last else FF_PER):
                    if b < 16:
                        j, q = divmod(b, 4)
                        if i is None and g0 == 0 and b < 3:
                            for k in range(4 * b + 4, 4 * b + 8):
                                h2_part(k)
                        if q == 3:
                            n = at(i, GT, GT * g0 + j + 1)
                            dve.wait_ge(fexp, n)
                            own.link(V.tensor_scalar(ex[:, :], ex[:, :], 1.0, None, ALU.add))
                            own.link(V.reciprocal(ex[:, :], ex[:, :]))
                            V.tensor_tensor(ex[:, 0:HT], ex[:, 0:HT], ps[UP_BANKS[j % 2][0]][:, 0:HT], ALU.mult)
                            V.tensor_tensor(ex[:, HT:T], ex[:, HT:T], ps[UP_BANKS[j % 2][1]][:, 0:HT],
                                            ALU.mult).then_inc(gate_used, 1)
                            dve.wait_ge(used, at(i, FF_PER, B_FF + FF_PER * g0 + b + 1))
                            dve.wait_ge(gate_used, n)
                            V.tensor_tensor(tmp[:, 0, 0:HT], ex[:, 0:HT], ps[UP_BANKS[j % 2][2]][:, 0:HT], ALU.mult)
                            V.tensor_tensor(tmp[:, 0, HT:T], ex[:, HT:T], ps[UP_BANKS[j % 2][3]][:, 0:HT],
                                            ALU.mult).then_inc(f_ready, 1)
                        split(i, FF_PER, B_FF + FF_PER * g0 + b + 2)
                        if q == 3:
                            dve.wait_ge(f_hi, n)
                            V.tensor_tensor(fl[:, j, :], tmp[:, 0, :], fh[:, j, :].bitcast(f32),
                                            ALU.subtract).then_inc(f_lo, 1)
                    else:
                        c, q = divmod(b - 16, 2)
                        if q == 1:
                            cols = slice(c * 512, (c + 1) * 512)
                            if i is None and g0 == 0:
                                dve.wait_ge(res_ready, (c + 1) * TT)
                            for t, bank in enumerate(DOWN_BANKS):
                                n = at(i, 4 * TT, (4 * g0 + c) * TT + t + 1)
                                if t < LT:
                                    dve.wait_ge(down_done, at(i, 4 * LT, (4 * g0 + c) * LT + t + 1))
                                else:
                                    dve.wait_ge(used, at(i, FF_PER, B_FF + FF_PER * g0 + b + 1))
                                V.tensor_tensor(tmp[:, 1, 0:512], ps[bank][:, :], gate[:, t // LT, cols],
                                                ALU.mult).then_inc(down_evac, 1)
                                dve.wait_ge(down_evac, n)
                                own.link(V.tensor_tensor(xs[:, t, cols], xs[:, t, cols], tmp[:, 1, 0:512], ALU.add))
                        split(i, FF_PER, B_FF + FF_PER * g0 + b + 2)

            ff_group(None, 0)
            with dve.Fori(1, NG - 1) as i:
                own.enter(i, 1, GT * 2 + 4 * TT)
                ff_group(i, 0)
                own.leave(NG - 2)
            ff_group(None, NG - 1, last=True)

            for n in range(B_LAST + 2, N_BLOCKS):
                split(None, 0, n)

            def gain(t):
                dve.wait_ge(xn_ready, TT + t + 1)
                dve.wait_ge(lnb_in, 32)
                V.tensor_tensor(xs[:, t, YG[t]:D], xs[:, t, YG[t]:D], lng[:, YG[t]:D], ALU.mult).then_inc(yg_ready, 1)
                dve.wait_ge(yg_ready, t + 1)
                if YP[t] < D:
                    V.tensor_tensor(xs[:, t, YP[t]:D], xs[:, t, YP[t]:D], lnb[:, YP[t]:D], ALU.add).then_inc(y_ready, 1)

            for t in range(TT):
                for c in range(4):
                    cols = slice(c * 512, (c + 1) * 512)
                    m = 4 * t + c
                    dve.wait_ge(last_done, m + 1)
                    V.tensor_tensor(tmp[:, 1, 0:512], ps[LAST_BANKS[m % 8]][:, :], gate[:, t // LT, cols],
                                    ALU.mult).then_inc(down_evac, 1)
                    dve.wait_ge(down_evac, 4 * TT * (NG - 1) + m + 1)
                    own.link(V.tensor_tensor(xs[:, t, cols], xs[:, t, cols], tmp[:, 1, 0:512], ALU.add))
                    own.link(V.bn_stats(stat[:, t, c, :], xs[:, t, cols]))
                    if c == 1 and t:
                        gain(t - 1)
                stats(t)
                scales(TT + t)
            gain(TT - 1)


        @block.tensor
        def _(pe):
            mm = nc.tensor.matmul

            def mm3(out, ah, al, bh, bl, first, last):
                mm(out, ah, bh, start=first, stop=False)
                mm(out, ah, bl, start=False, stop=False)
                return mm(out, al, bh, start=False, stop=last)

            def arrived(i, per, n):
                pe.wait_ge(lo_ready, at(i, per, n + 1))

            def tok_block(n, ah, al, k0, first, last, banks, before=None, after=None, cols=512, tile=None):
                for t, bank in enumerate(banks):
                    if before:
                        before(t)
                    o = (t if tile is None else tile[t]) * P
                    for kk in range(2):
                        w = slice(kk * cols, (kk + 1) * cols)
                        ins = mm3(ps[bank][:, 0:cols], ah[:, k0 + kk, o:o + P], al[:, k0 + kk, o:o + P],
                                  hi_of(n)[:, w], lo_of(n)[:, w], first and kk == 0, last and kk == 1)
                    if after and t < len(banks) - 1:
                        after(t, ins)
                return ins

            def feat_block(n, bh, bl, k0, first, last, before=None, after=None, widths=(HT, HT), banks=(0, 1, 2, 3), b2=None):
                for o in range(4):
                    if before:
                        before(o)
                    half, w = o % 2, widths[o // 2]
                    xh, xl = (bh, bl) if o < 2 or b2 is None else b2
                    for kk in range(4):
                        c = slice(kk * 256 + o // 2 * P, kk * 256 + o // 2 * P + P)
                        m = slice(half * w, (half + 1) * w)
                        ins = mm3(ps[banks[o]][:, 0:w], hi_of(n)[:, c], lo_of(n)[:, c], xh[:, k0 + kk, m],
                                  xl[:, k0 + kk, m], first and kk == 0, last and kk == 3)
                    if after and o < 3:
                        after(o, ins)
                return ins

            def mod_block(i, per, n, b, chunk_free, bank=7, hi=None, lo=None):
                arrived(i, per, n)
                if b == 0 and chunk_free is not None:
                    pe.wait_ge(modrow_ready, chunk_free)
                hi, lo = (hi_of(n), lo_of(n)) if hi is None else (hi, lo)
                for kk in range(2):
                    w = slice(kk * 512, (kk + 1) * 512)
                    mm(ps[bank][0:4, :], condw[:, 2 * b + kk, :], hi[:, w], start=(b == 0 and kk == 0), stop=False)
                    ins = mm(ps[bank][0:4, :], condw[:, 2 * b + kk, :], lo[:, w], start=False, stop=(b == 7 and kk == 1))
                ins.then_inc(used, 1)

            pe.wait_ge(cond_ready, 1)

            def turn_rows(i, c):
                pe.wait_ge(modrow_ready, at(i, 2, c + 1))
                for j in range(4):
                    o = at(i, 16, 8 * c + 2 * j)
                    ins = mm(ps[6][:, bass.ds(o, 2)], modrow[:, c % 2, j * P:(j + 1) * P], selt[0:4, 0:2],
                             start=True, stop=True)
                ins.then_inc(mod1_psum, 1)

            def mod_pair(i):
                for b in range(16):
                    c = b // 8
                    mod_block(i, 16, b, b % 8, None if i is None else i * 2 + c - 1, MOD_BANKS[c],
                              mhi[:, b % 4, :], mlo[:, b % 4, :])
                    if b % 8 == 2 and (i is not None or c):
                        turn_rows(i, c - 1)

            mod_pair(None)
            with pe.Fori(1, 4) as i:
                mod_pair(i)
            turn_rows(None, 7)

            def mod_columns(shift, scale, done):
                for j in range(2 * KD):
                    rows = shift if j < KD else scale
                    ins = mm(ps[6][:, 2 * j:2 * j + 2], rows[:, j % KD * P:(j % KD + 1) * P], selt[:, 0:2],
                             start=True, stop=True)
                ins.then_inc(done, 1)

            for c in range(2):
                for b in range(8):
                    n = B_V + 8 * c + b
                    arrived(None, 0, n)
                    if c == 0:
                        pe.wait_ge(h_ready, 2 * b + 2)
                        if b == 0:
                            pe.wait_ge(modrow_ready, 8)
                    tok_block(n, hh, hl, 2 * b, b == 0, b == 7, TOK_BANKS,
                              before=(lambda t: pe.wait_ge(v_evac, t + 1)) if c == 1 and b == 0 else None,
                              after=(lambda t, ins: ins.then_inc(v_done, 1)) if b == 7 else None
                              ).then_inc(used, 1)

            def stage(i, a, s, na, kcached=None, h=None, only=None):
                A = lambda c: at(i, 5, 5 * a + c)
                one = (lambda c: a + c if i is None else i + a + c)

                def scores():
                    if s < 5:
                        bk = 4 if na or s % 2 == 0 else 0
                        if s == 0:
                            pe.wait_ge(q_evac, one(1))
                            pe.wait_ge(k_evac, one(1))
                        if not na and s != 1:
                            pe.wait_ge(exp_ready, A(max(s - 1, 0)))
                        if s == 0 and i is None and na:
                            pe.wait_ge(o_evac, a)
                        q = qT[:, s * P:(s + 1) * P]
                        if s < LT:
                            if na:
                                mm(ps[bk][:, :], q, kT[:, 0:LAT], start=True, stop=True)
                                mm(ps[bk + 1][:, 0:CTX], q, kcached, start=True, stop=True).then_inc(scores_ready, 1)
                            else:
                                qq = qrT[:, h, s * P:(s + 1) * P]
                                mm(ps[bk][:, :], q, kT[:, 0:LAT], start=True, stop=False)
                                mm(ps[bk][:, :], qq, krT[:, 0:LAT], start=False, stop=True)
                                mm(ps[bk + 1][:, 0:CTX], q, kT[:, LAT:T], start=True, stop=False)
                                mm(ps[bk + 1][:, 0:CTX], qq, krT[:, LAT:T], start=False, stop=True).then_inc(scores_ready, 1)
                        elif na:
                            mm(ps[4][:, 0:CTX], q, kT[:, LAT:T], start=True, stop=True).then_inc(scores_ready, 1)
                        else:
                            mm(ps[4][:, 0:CTX], q, kT[:, T:KEYS], start=True, stop=False)
                            mm(ps[4][:, 0:CTX], qrT[:, h, LAT:T], krT[:, T:KEYS], start=False,
                               stop=True).then_inc(scores_ready, 1)

                def transposes():
                    if 2 <= s < 7:
                        t = s - 2
                        pe.wait_ge(p_ready, A(t + 1))
                        if t:
                            pe.wait_ge(pt_free, A(t))
                        elif not na:
                            pe.wait_ge(o_evac, a)
                        if t < LT:
                            for k in range(4):
                                nc.tensor.transpose(ps[6][:, k * P:(k + 1) * P], pb[:, t % 3, k * P:(k + 1) * P], idt[:, :])
                            if na and t == 3:
                                nc.tensor.transpose(ps[5][:, 2 * P:3 * P], kT[:, LAT:T], idt[:, :])
                            last = ps[5][:, P:2 * P] if na else ps[7][:, 0:P]
                            nc.tensor.transpose(last, pb[:, t % 3, LAT:T], idt[:, :]).then_inc(pt_ready, 1)
                        else:
                            nc.tensor.transpose(ps[6][:, 0:P], pb[:, t % 3, 0:P], idt[:, :]).then_inc(pt_ready, 1)

                if na:
                    if 1 <= s < 6:
                        pe.wait_ge(max_ready, A(s))
                    transposes()
                    scores()
                elif only == "turn":
                    transposes()
                elif only == "scores":
                    scores()
                if s == 7:
                    pe.wait_ge(pt_free, A(5))
                    pe.wait_ge(vh_ready, one(1))
                    bk = 4 if na else 6
                    for k in range(5):
                        mm(ps[bk][:, :], vh[:, k, :], PT[:, k, :], start=(k == 0), stop=(k == 4))
                    mm(ps[bk + 1][:, 0:CTX], vh[:, 5, :], PTc[:, :], start=True, stop=True).then_inc(pv_ready, 1)

            def na_iter(i, stages):
                for b in range(NA_PER):
                    g, r = divmod(b, 5)
                    n = B_NA + b
                    if r == 0:
                        arrived(i, NA_PER, n)
                        before = None
                        if b == 0:
                            if i is None:
                                before = lambda o: pe.wait_ge(v_evac, TT + 1 + o)
                            else:
                                before = lambda o: pe.wait_ge(q_evac if o < 2 else k_evac, i + 0)
                        feat_block(n, hh, hl, 4 * g, g == 0, g == 3, before=before).then_inc(used, 1)
                    else:
                        m = 4 * g + r - 1
                        if i is None and m == 0:
                            pe.wait_ge(v_evac, 2 * TT)
                        mod_block(i, NA_PER, n, m % 8, (8 + m // 8) if i is None else i * 2 + 8 + m // 8)
                    if stages and r in (1, 4):
                        s = 2 * g + (r == 4)
                        if s == 0:
                            na_first_wait(i)
                        stage(i, -1, s, True, kct[:, i - 1, :])

            def na_first_wait(i):
                pe.wait_ge(na_consts_in, 80)
                pe.wait_ge(lo_ready, at(i, NA_PER, B_NA + 4))

            na_iter(None, False)
            with pe.Fori(1, NH) as i:
                na_iter(i, True)

            for b in range(17):
                n = B_KVL + b
                arrived(None, 0, n)
                if b < 16:
                    c, q = divmod(b, 8)
                    before = None
                    if c == 0 and q == 0:
                        def before(t):
                            if t < 4:
                                pe.wait_ge(q_evac if t < 2 else k_evac, NH)
                            else:
                                pe.wait_ge(modrow_ready, MOD_CHUNKS)
                    elif q == 0:
                        before = lambda t: pe.wait_ge(lat_evac, t + 1)
                    ins = tok_block(n, hh, hl, 2 * q, q == 0, q == 7, TOK_BANKS, before=before,
                                    after=(lambda t, ins: ins.then_inc(lat_done, 1)) if q == 7 else None)
                    ins.then_inc(used, 1)
                else:
                    for half in range(2):
                        pe.wait_ge(lat_evac, TT + half + 1)
                        m = slice(half * HT, (half + 1) * HT)
                        for k in range(KD):
                            w = slice(k * ROPE, (k + 1) * ROPE)
                            ins = mm3(ps[half][0:ROPE, 0:HT], hi_of(n)[:, w], lo_of(n)[:, w], hh[:, k, m], hl[:, k, m],
                                      k == 0, k == KD - 1)
                    ins.then_inc(used, 1)
                    pe.wait_ge(krf_evac, 1)
                    pe.wait_ge(o_evac, NH)
                    for t in range(TT):
                        ins = nc.tensor.transpose(ps[4][:, t * ROPE:(t + 1) * ROPE], krf[:, t * P:(t + 1) * P],
                                                  idt[0:ROPE, 0:ROPE])
                    ins.then_inc(krf_turned, 1)
                if b < 8:
                    stage(None, NH - 1, b, True, kct[:, NH - 1, :])

            pe.wait_ge(lat_evac, 2 * TT)
            for j in range(2 * TT):
                t = j % TT
                src = kvl if j < TT else ql
                pe.wait_ge(kvl_ready if j < TT else ql_ready, t + 1)
                if j >= 4:
                    pe.wait_ge(tr_lo, j - 3)
                for k in range(KL):
                    ins = nc.tensor.transpose(ps[j % 4][:, k * P:(k + 1) * P], src[:, t, k * P:(k + 1) * P], idt[:, :])
                ins.then_inc(tr_done, 1)
            for q in range(2):
                n = B_QR + q
                arrived(None, 0, n)
                if q == 0:
                    pe.wait_ge(tr_lo, 2 * TT)
                tok_block(n, qlh, qll, 2 * q, q == 0, q == 1, TOK_BANKS,
                          after=(lambda t, ins: ins.then_inc(qr_done, 1)) if q else None
                          ).then_inc(used, 1)

            pe.wait_ge(kr_ready, 1)
            for t in range(LT):
                nc.tensor.transpose(ps[4][0:ROPE, t * P:(t + 1) * P], krr[:, t, :], idt[:, :])
            nc.tensor.transpose(ps[5][0:ROPE, 0:P], krr[:, LT, :], idt[:, :]).then_inc(tr_done, 1)

            def turn_q(t):
                pe.wait_ge(qr_roped, t + 1)
                if t:
                    pe.wait_ge(qrt_evac, t)
                for h in range(NH):
                    ins = nc.tensor.transpose(ps[5 + h // 4][0:ROPE, h % 4 * P:(h % 4 + 1) * P],
                                              qr[:, t, h * ROPE:(h + 1) * ROPE], idt[:, :])
                ins.then_inc(qrt_done, 1)

            for c in range(2):
                for q in range(2):
                    n = B_VM + 2 * c + q
                    arrived(None, 0, n)
                    before = None
                    if not c and not q:
                        pe.wait_ge(mla_in, 32)
                        pe.wait_ge(tr_lo, 2 * TT + 1)

                        def before(t):
                            pe.wait_ge(qr_evac, t + 1) if t < TT else pe.wait_ge(krt_evac, 1)
                    elif not q:
                        def before(t):
                            pe.wait_ge(vm_evac, t + 1)
                            if t:
                                turn_q(t - 1)
                    tok_block(n, ckvh, ckvl, 2 * q, q == 0, q == 1, TOK_BANKS + [4], before=before,
                              after=(lambda t, ins: ins.then_inc(vm_done, 1)) if q else None
                              ).then_inc(used, 1)

            for h in range(NH + 1):
                last, cur, more = NH + h - 1, NH + h, h < NH
                if more:
                    n = B_HEAD + h
                    arrived(None, 0, n)
                    before = None
                    if h == 0:
                        pe.wait_ge(vm_evac, 12)
                        pe.wait_ge(qrt_evac, TT)
                    else:
                        def before(o):
                            if o == 1:
                                stage(None, last, 4, False, only="turn")
                            if o >= 2:
                                pe.wait_ge(exp_ready, 5 * last + 4)
                    feat_block(n, qlh, qll, 0, True, True, widths=(HT, KEYS // 2), banks=(2, 3, 0, 1), b2=(ckvh, ckvl),
                               before=before, after=lambda o, ins: ins.then_inc(q_done, 1) if o == 1 else None
                               ).then_inc(used, 1)
                elif h:
                    stage(None, last, 4, False, only="turn")
                if h:
                    stage(None, last, 5, False, only="turn")
                if more:
                    stage(None, cur, 0, False, h=h, only="scores")
                if h:
                    stage(None, last, 6, False, only="turn")
                if more:
                    stage(None, cur, 1, False, h=h, only="scores")
                if h:
                    stage(None, last, 7, False)
                if more:
                    for s in range(2, 5):
                        stage(None, cur, s, False, h=h, only="scores")
                        if s < 4:
                            stage(None, cur, s, False, only="turn")

            def gate_bcast(rows, q):
                for c in range(2):
                    ins = mm(ps[4 + c][:, :], selt[:, 2 + c * P:2 + (c + 1) * P], rows[:, q * 512:(q + 1) * 512],
                             start=True, stop=True)
                ins.then_inc(g_psum, 1)

            for b in range(32):
                n = B_WO + b
                arrived(None, 0, n)
                c, q = divmod(b, 8)
                if c == 0:
                    pe.wait_ge(o_lo, 2 * q + 2)
                if b == 0:
                    before = lambda t: pe.wait_ge(o_evac, 2 * NH) if t == LT else None
                elif q == 0:
                    before = lambda t: pe.wait_ge(wo_evac, (c - 1) * TT + t + 1)
                else:
                    before = None
                ins = tok_block(n, oh, ol, 2 * q, q == 0, q == 7, TOK_BANKS, before=before,
                                after=(lambda t, ins: ins.then_inc(wo_done, 1)) if q == 7 else None)
                ins.then_inc(used, 1)
                if b == 5:
                    pe.wait_ge(rows2_in, 32)
                    pe.wait_ge(o_evac, 2 * NH)
                    gate_bcast(rows2, 0)
                if b in (7, 9, 11):
                    pe.wait_ge(g_evac, b - 5)
                    gate_bcast(rows2, (b - 5) // 2)
                if b == 20:
                    pe.wait_ge(rows3_in, 32)
                    pe.wait_ge(rows2_in, 64)
                    mod_columns(rows3, rows2, mod2_psum)
                if b in (26, 28, 30):
                    pe.wait_ge(rows2_in, 96)
                    pe.wait_ge(g_evac, b - 18)
                    gate_bcast(rows2, (b - 26) // 2)
            pe.wait_ge(g_evac, 14)
            gate_bcast(rows2, 3)
            def turn_x(k):
                r = k % 2
                if k == 0:
                    pe.wait_ge(xn_ready, TT)
                if k == 1:
                    pe.wait_ge(g_evac, 16)
                if k >= 2:
                    pe.wait_ge(h2_scaled, k - 1)
                for t in range(LT):
                    nc.tensor.transpose(ps[6 - 2 * r][:, t * P:(t + 1) * P], xs[:, t, k * P:(k + 1) * P], idt[:, :])
                nc.tensor.transpose(ps[7 - 2 * r][:, 0:P], xs[:, LT, k * P:(k + 1) * P], idt[:, :]).then_inc(xt_ready, 1)

            for k in range(4):
                turn_x(k)

            def ff_group(i, g0):
                for b in range(16 if g0 == NG - 1 else FF_PER):
                    n = B_FF + FF_PER * g0 + b
                    arrived(i, FF_PER, n)
                    if b < 16:
                        j, q = divmod(b, 4)
                        def before(o, j=j, q=q):
                            if i is None and g0 == 0 and j == 0 and q < 3:
                                turn_x(4 * q + 4 + o)
                            if i is None and g0 == 0 and j == 1 and q == 0 and o == 0:
                                pe.wait_ge(h2_scaled, KD)
                            if q:
                                return
                            later = i is not None or g0
                            if j >= 2 or (j == 1 and later):
                                pe.wait_ge(gate_used if o < 2 else f_ready, at(i, GT, GT * g0 + j - 1))
                            if later and (j == 0 or (j == 1 and o == 3)):
                                pe.wait_ge(down_evac, at(i, 4 * TT, (4 * g0 - 1) * TT + DOWN_BANKS.index(UP_BANKS[j][o]) + 1))
                        if i is None and g0 == 0 and b < 4:
                            pe.wait_ge(h2_ready, 4 * b + 4)
                        if i is None and g0 == 0 and b == 0:
                            pe.wait_ge(wo_evac, 4 * TT)
                        ins = feat_block(n, oh, ol, 4 * q, q == 0, q == 3, before=before, banks=UP_BANKS[j % 2],
                                         after=(lambda o, ins: ins.then_inc(gate_done, 1) if o == 1 else None) if q == 3 else None)
                        ins.then_inc(used, 1)
                    else:
                        c, q = divmod(b - 16, 2)

                        def before(t, c=c, q=q):
                            if q:
                                return
                            if c:
                                pe.wait_ge(down_evac, at(i, 4 * TT, (4 * g0 + c - 1) * TT + t + 1))
                            else:
                                pe.wait_ge(gate_used if t < 2 else f_ready, at(i, GT, GT * g0 + (3 if t < 4 else 4)))
                        pe.wait_ge(f_lo, at(i, GT, GT * g0 + 2 * q + 2))
                        ins = tok_block(n, fh, fl, 2 * q, q == 0, q == 1, DOWN_BANKS, before=before,
                                        after=(lambda t, ins: ins.then_inc(down_done, 1)) if q else None)
                        ins.then_inc(used, 1)

            ff_group(None, 0)
            with pe.Fori(1, NG - 1) as i:
                ff_group(i, 0)
            ff_group(None, NG - 1)

            def last_part(t, c, q):
                n = B_LAST + 4 * q + c
                o = slice(t * P, (t + 1) * P)
                for kk in range(2):
                    w = slice(kk * 512, (kk + 1) * 512)
                    ins = mm3(ps[LAST_BANKS[(4 * t + c) % 8]][:, :], fh[:, 2 * q + kk, o], fl[:, 2 * q + kk, o],
                              hi_of(n)[:, w], lo_of(n)[:, w], q == 0 and kk == 0, q == 1 and kk == 1)
                return ins

            for q in range(2):
                pe.wait_ge(f_lo, GT * (NG - 1) + 2 * q + 2)
                for c in range(4):
                    arrived(None, 0, B_LAST + 4 * q + c)
                    if q == 0:
                        pe.wait_ge(f_ready, GT * NG - 1)
                    ins = last_part(0, c, q)
                    if q == 1:
                        ins.then_inc(last_done, 1)
            for m in range(4, 4 * TT):
                if m < 8:
                    pe.wait_ge(f_ready, GT * NG)
                else:
                    pe.wait_ge(down_evac, 4 * TT * (NG - 1) + m - 7)
                last_part(m // 4, m % 4, 0)
                last_part(m // 4, m % 4, 1).then_inc(last_done, 1)


_NAMES = ["wstream", "xT", "xtok", "cond", "bmod", "rpb", "kcT", "vc", "ckvcT", "krcT", "lncol", "lnrow", "latg",
          "bcol", "rope", "cap", "ident", "sel"]
_OUTS = [("y", (TT, P, D)), ("s_k", (CTX, NH * P)), ("s_v", (CTX, NH * P)), ("s_ckv", (CTX, LORA)), ("s_kr", (CTX, ROPE))]


def _tok_blocks(np, w):
    K, N = w.shape
    return w.reshape(K // 256, 2, P, N // 512, 512).transpose(3, 0, 2, 1, 4).reshape(-1, P, 1024)


def _feat_blocks(np, wa, wb):
    K, H, _ = wa.shape
    w = np.stack([wa, wb], axis=2)
    return w.reshape(K // 512, 4, P, H, 256).transpose(3, 0, 2, 1, 4).reshape(-1, P, 1024)


def _layout(np, a):
    f = {k: np.asarray(v) for k, v in a.items()}
    w_in, w_mod, w_qb, w_kvb = f["w_in"][0], f["w_mod"][0], f["w_q_b"][0], f["w_kv_b"][0]
    na = NH * P
    mod = _tok_blocks(np, w_mod)
    v = _tok_blocks(np, w_in[:, 2 * na:3 * na])
    qk = _feat_blocks(np, w_in[:, 0:na].reshape(D, NH, P), w_in[:, na:2 * na].reshape(D, NH, P))
    lat = w_in[:, 3 * na:]
    qb = w_qb.reshape(LORA, NH, P + ROPE)
    kb = w_kvb.reshape(LORA, NH, 2 * P)
    parts = [mod[0:64], v]
    mods = mod[64:].reshape(NH, 4, 4, P, 1024)
    qks = qk.reshape(NH, 4, 1, P, 1024)
    parts.append(np.concatenate([qks, mods], axis=2).reshape(-1, P, 1024))
    parts.append(_tok_blocks(np, lat[:, LORA:2 * LORA]))
    parts.append(_tok_blocks(np, lat[:, 0:LORA]))
    parts.append(lat[:, 2 * LORA:].reshape(KD, P, ROPE).transpose(1, 0, 2).reshape(1, P, 1024))
    parts.append(_tok_blocks(np, qb[:, :, P:].reshape(LORA, NH * ROPE)))
    parts.append(_tok_blocks(np, kb[:, :, P:].reshape(LORA, NH * P)))
    parts.append(_feat_blocks(np, qb[:, :, 0:P], kb[:, :, 0:P]))
    parts.append(_tok_blocks(np, f["w_o"][0]))
    wgu = f["w_gu"][0].reshape(D, 2, FF // P, P)
    up = _feat_blocks(np, wgu[:, 0], wgu[:, 1]).reshape(NG, GT * 4, P, 1024)
    down = _tok_blocks(np, f["w_down"][0]).reshape(4, NG, 2, P, 1024).transpose(1, 0, 2, 3, 4).reshape(NG, 8, P, 1024)
    ff = np.concatenate([up, down], axis=1).reshape(-1, P, 1024)
    parts += [ff[:-8], ff[-8::2], ff[-7::2]]
    x = np.concatenate([f["x_sample"][0], f["x_prompt"][0]], axis=0)
    out = {
        "wstream": np.concatenate(parts, axis=0),
        "xT": x.reshape(T, KD, P).transpose(2, 1, 0),
        "xtok": x.reshape(TT, P, D).transpose(1, 0, 2),
        "cond": np.stack([f["c"][0], f["c_ctx"]], axis=-1).reshape(KD, P, 2).transpose(1, 0, 2),
        "bmod": f["b_mod"][0:1],
        "bcol": f["b_mod"][0, 0:2 * D].reshape(2 * KD, P).transpose(1, 0),
        "rpb": f["na_rpb"][0].reshape(NH * RPB),
        "kcT": f["cache_na_k"][0, 0].transpose(2, 1, 0),
        "vc": f["cache_na_v"][0, 0].reshape(CTX, NH * P),
        "ckvcT": f["cache_mla_ckv"][0, 0].reshape(CTX, KL, P).transpose(2, 1, 0),
        "krcT": f["cache_mla_krope"][0, 0].transpose(1, 0),
        "lncol": np.stack([f["ln1_g"][0].reshape(KD, P).transpose(1, 0), f["ln1_b"][0].reshape(KD, P).transpose(1, 0)], axis=1),
        "lnrow": np.stack([f["ln1_g"][0], f["ln1_b"][0], f["ln2_g"][0], f["ln2_b"][0]], axis=0)[None],
        "latg": np.stack([f["q_a_norm"][0], f["kv_a_norm"][0]], axis=0),
    }
    return out


def _constants(np):
    f32 = np.float32
    half = ROPE // 2
    pos = np.arange(LAT, dtype=np.int32)
    inv = (f32(10000.0) ** (-np.arange(0, half, 2, dtype=f32) / f32(half))).astype(f32)
    cs = []
    for p in (pos // GRID, pos % GRID):
        ang = p.astype(f32)[:, None] * inv
        cs.append((np.cos(ang), np.sin(ang)))
    cos = np.concatenate([cs[0][0], cs[0][0], cs[1][0], cs[1][0]], axis=1)
    sin = np.concatenate([-cs[0][1], cs[0][1], -cs[1][1], cs[1][1]], axis=1)
    rope = np.stack([cos, sin]).reshape(2, LT, P, ROPE).transpose(2, 0, 1, 3).astype(f32)
    col = np.arange(GRID)
    start = np.clip(col - WC // 2, 0, GRID - WC)
    win = (col[None, :] >= start[:, None]) & (col[None, :] < start[:, None] + WC)
    cap = np.where(win, f32(0.0), f32(BIG)).astype(f32)
    sel = np.zeros((5, 2 + 2 * P), f32)
    for r, (a, b) in enumerate([(1, 0), (0, 1), (1, 0), (0, 1), (1, 1)]):
        sel[r, 0], sel[r, 1] = a, b
        sel[r, 2:2 + P], sel[r, 2 + P:] = a, b
    return {"rope": rope, "cap": np.tile(cap, (2, 14)), "ident": np.eye(P, dtype=f32), "sel": sel}


def kernel(**inputs):
    import numpy as np
    import concourse.bacc as bacc
    from concourse.bass_utils import run_bass_kernel_spmd

    arrays = {**_layout(np, inputs), **_constants(np)}
    arrays = {k: np.ascontiguousarray(v) for k, v in arrays.items()}
    nc = bacc.Bacc("TRN2", target_bir_lowering=False, num_devices=1)
    ins = [nc.dram_tensor("in_" + n, arrays[n].shape, mybir.dt.float32, kind="ExternalInput").ap() for n in _NAMES]
    outs = [nc.dram_tensor("out_" + n, s, mybir.dt.float32, kind="ExternalOutput").ap() for n, s in _OUTS]
    build(nc, *ins, *outs)
    res = run_bass_kernel_spmd(nc, [{"in_" + n: arrays[n] for n in _NAMES}], core_ids=[0]).results[0]
    y = res["out_y"].reshape(T, D)
    return (y[LAT:].reshape(1, CTX, D), y[:LAT].reshape(1, LAT, D),
            res["out_s_k"].reshape(1, 1, CTX, NH, P), res["out_s_v"].reshape(1, 1, CTX, NH, P),
            res["out_s_ckv"].reshape(1, 1, CTX, LORA), res["out_s_kr"].reshape(1, 1, CTX, ROPE))
```
